# Optimizing a Trainium2 kernel written in Bass

```python
import jax, jax.numpy as jnp
from jax import lax
import numpy as np

D_MODEL = 1024
BATCH = 1
SEQ = 2048
DEPTH = 2
DEC_BATCH = 8
DEC_SEQ = 16
PAST_LEN = 256

CHUNK = 64
N_A_LAYERS = DEPTH // 2
N_B_LAYERS = DEPTH - N_A_LAYERS
CONV_WIDTH = 3
D_CONV = D_MODEL
N_HEADS = 16
HEAD_DIM = 64
D_ATTN = N_HEADS * HEAD_DIM
Q_BLOCK = 128
EPS = 1e-6

kernel_name = "yoco_shortconv_stickbreaking_step"

def _rmsnorm(x, g):
    xf = x.astype(jnp.float32)
    y = xf * lax.rsqrt(jnp.mean(xf * xf, axis=-1, keepdims=True) + EPS)
    return (y * g.astype(jnp.float32)).astype(x.dtype)

def _short_conv_mixer(xn, prev, w_in, conv_w, w_out):
    proj = xn @ w_in
    b_gate, c_gate, h, z = jnp.split(proj, 4, axis=-1)
    u = c_gate * h
    T = u.shape[1]
    up = jnp.concatenate([prev.astype(u.dtype), u], axis=1)
    conv = conv_w[0] * up[:, 0:T]
    for i in range(1, CONV_WIDTH):
        conv = conv + conv_w[i] * up[:, i:i + T]
    y = jax.nn.silu(z) * b_gate * conv
    return y @ w_out, up[:, T:]

def _sb_block(q, qpos, k, v, kpos):
    scale = HEAD_DIM ** -0.5
    z = jnp.einsum('bqhd,bkhd->bhqk', q, k, preferred_element_type=jnp.float32) * scale
    causal = kpos[None, :] < qpos[:, None]
    log_keep = jnp.where(causal, jax.nn.log_sigmoid(-z), 0.0)
    rev = lax.cumsum(log_keep, axis=log_keep.ndim - 1, reverse=True)
    after = jnp.concatenate([rev[..., 1:], jnp.zeros_like(rev[..., :1])], axis=-1)
    log_a = jnp.where(causal, jax.nn.log_sigmoid(z) + after, -jnp.inf)
    a = jnp.exp(log_a)
    o = jnp.einsum('bhqk,bkhd->bqhd', a, v.astype(jnp.float32))
    return o.astype(q.dtype)

def _sb_prompt(q, k, v):
    b, T, H, d = q.shape
    nb = T // Q_BLOCK
    pos = jnp.arange(T, dtype=jnp.int32)
    qb = q.reshape(b, nb, Q_BLOCK, H, d)
    qpos = pos.reshape(nb, Q_BLOCK)

    def per_seq(args):
        qs, ks, vs = args

        def per_block(a):
            qblk, qp = a
            return _sb_block(qblk[None], qp, ks[None], vs[None], pos)[0]

        return lax.map(per_block, (qs, qpos))

    out = lax.map(per_seq, (qb, k, v))
    return out.reshape(b, T, H, d)

def _sb_sample(q, k_new, v_new, past_k, past_v):
    past = past_k.shape[1]
    tn = q.shape[1]
    k_all = jnp.concatenate([past_k.astype(k_new.dtype), k_new], axis=1)
    v_all = jnp.concatenate([past_v.astype(v_new.dtype), v_new], axis=1)
    kpos = jnp.arange(past + tn, dtype=jnp.int32)
    qpos = past + jnp.arange(tn, dtype=jnp.int32)
    return _sb_block(q, qpos, k_all, v_all, kpos)

def _trunk(x, conv_prev, past_k, past_v,
           a_norm_pre, a_w_in, a_conv_w, a_w_out, a_norm_post,
           kv_norm, w_k, w_v,
           b_norm_pre, b_w_in, b_w_out, b_norm_post):
    b, T, _ = x.shape
    new_conv = []
    k = v = None
    for layer in range(DEPTH):
        if layer < N_A_LAYERS:
            i = layer
            h, st = _short_conv_mixer(_rmsnorm(x, a_norm_pre[i]), conv_prev[i],
                                      a_w_in[i], a_conv_w[i], a_w_out[i])
            new_conv.append(st)
            x = x + _rmsnorm(h, a_norm_post[i])
        else:
            j = layer - N_A_LAYERS
            if j == 0:
                kv_in = _rmsnorm(x, kv_norm)
                k = (kv_in @ w_k).reshape(b, T, N_HEADS, HEAD_DIM)
                v = (kv_in @ w_v).reshape(b, T, N_HEADS, HEAD_DIM)
            proj = _rmsnorm(x, b_norm_pre[j]) @ b_w_in[j]
            q, z = jnp.split(proj, 2, axis=-1)
            q = q.reshape(b, T, N_HEADS, HEAD_DIM)
            if past_k is None:
                o = _sb_prompt(q, k, v)
            else:
                o = _sb_sample(q, k, v, past_k, past_v)
            h = (jax.nn.silu(z) * o.reshape(b, T, D_ATTN)) @ b_w_out[j]
            x = x + _rmsnorm(h, b_norm_post[j])
    return x, jnp.stack(new_conv, axis=0), k, v

def setup_inputs(seed: int = 0) -> dict:
    key = jax.random.key(seed)
    ks = jax.random.split(key, 20)
    f32 = jnp.float32
    nrm = lambda k, shape, s: jax.random.normal(k, shape, f32) * s
    return {
        "x_prompt": nrm(ks[0], (BATCH, SEQ, D_MODEL), 1.0),
        "x_sample": nrm(ks[1], (DEC_BATCH, DEC_SEQ, D_MODEL), 1.0),
        "state_conv": nrm(ks[2], (N_A_LAYERS, DEC_BATCH, CONV_WIDTH - 1, D_CONV), 1.0),
        "cache_k": nrm(ks[3], (DEC_BATCH, PAST_LEN, N_HEADS, HEAD_DIM), 1.0),
        "cache_v": nrm(ks[4], (DEC_BATCH, PAST_LEN, N_HEADS, HEAD_DIM), 1.0),
        "a_norm_pre": 1.0 + nrm(ks[5], (N_A_LAYERS, D_MODEL), 0.02),
        "a_w_in": nrm(ks[6], (N_A_LAYERS, D_MODEL, 4 * D_CONV), D_MODEL ** -0.5),
        "a_conv_w": nrm(ks[7], (N_A_LAYERS, CONV_WIDTH, D_CONV), CONV_WIDTH ** -0.5),
        "a_w_out": nrm(ks[8], (N_A_LAYERS, D_CONV, D_MODEL), D_CONV ** -0.5),
        "a_norm_post": 1.0 + nrm(ks[9], (N_A_LAYERS, D_MODEL), 0.02),
        "kv_norm": 1.0 + nrm(ks[10], (D_MODEL,), 0.02),
        "w_k": nrm(ks[11], (D_MODEL, D_ATTN), D_MODEL ** -0.5),
        "w_v": nrm(ks[12], (D_MODEL, D_ATTN), D_MODEL ** -0.5),
        "b_norm_pre": 1.0 + nrm(ks[13], (N_B_LAYERS, D_MODEL), 0.02),
        "b_w_in": nrm(ks[14], (N_B_LAYERS, D_MODEL, 2 * D_ATTN), D_MODEL ** -0.5),
        "b_w_out": nrm(ks[15], (N_B_LAYERS, D_ATTN, D_MODEL), D_ATTN ** -0.5),
        "b_norm_post": 1.0 + nrm(ks[16], (N_B_LAYERS, D_MODEL), 0.02),
    }

def reference(x_prompt, x_sample, state_conv, cache_k, cache_v,
              a_norm_pre, a_w_in, a_conv_w, a_w_out, a_norm_post,
              kv_norm, w_k, w_v,
              b_norm_pre, b_w_in, b_w_out, b_norm_post):
    weights = (a_norm_pre, a_w_in, a_conv_w, a_w_out, a_norm_post,
               kv_norm, w_k, w_v, b_norm_pre, b_w_in, b_w_out, b_norm_post)
    conv0 = jnp.zeros((N_A_LAYERS, x_prompt.shape[0], CONV_WIDTH - 1, D_CONV), x_prompt.dtype)
    y_prompt, conv_state_prompt, k_prompt, v_prompt = _trunk(x_prompt, conv0, None, None, *weights)
    y_sample, conv_state_sample, k_sample, v_sample = _trunk(x_sample, state_conv, cache_k, cache_v, *weights)
    return (y_prompt, y_sample, conv_state_prompt, conv_state_sample, k_prompt, v_prompt, k_sample, v_sample)


_drawn_inputs = setup_inputs


def setup_inputs(seed=0):
    import zlib

    import numpy as np

    out = dict(_drawn_inputs(seed))
    spreads = {}
    factors = {'a_norm_post': 3.278, 'kv_norm': 2.886, 'b_norm_pre': 4.149, 'b_norm_post': 4.945}
    for name, (base, spread) in spreads.items():
        noise = np.random.default_rng([zlib.crc32(name.encode()), seed]).standard_normal(out[name].shape)
        drawn = base * np.exp(spread * noise) if base else spread * noise
        out[name] = __import__('jax').numpy.asarray(drawn.astype(out[name].dtype))
    for name, factor in factors.items():
        out[name] = (out[name] * factor).astype(out[name].dtype)
    return out
```

```python
import concourse.bass as bass
from concourse import mybir
from contextlib import ExitStack
import numpy as np

F32 = mybir.dt.float32
F32R = mybir.dt.float32r
ALU = mybir.AluOpType
ACT = mybir.ActivationFunctionType

P = 128
D = 1024
KT = D // P
SEQ = 2048
NB, NQ = 8, 16
T = SEQ + NB * NQ
NT = T // P
PAST = 256
H, HD = 16, 64
SCALE = HD ** -0.5
EPS = 1e-6
CW = 3
GROUPS = [(0, 512), (512, 512), (1024, 384), (1408, 384), (1792, 384)]
NG = len(GROUPS)
PAIRS = 7
QT = SEQ // P
QG = 4
NGQ = QT // QG
MASKED = -1e30


def token_tiles(eng, first, second):
    first(0, 0)
    with eng.Fori(0, PAIRS) as j:
        first(j, 1)
        second(j, 0)
        first(j + 1, 0)
        second(j, 1)
    first(PAIRS, 1)
    second(PAIRS, 0)
    first(PAIRS + 1, 0)
    second(PAIRS, 1)
    second(PAIRS + 1, 0)


def is_sample(j, s):
    return isinstance(j, int) and 2 * j + s == NT - 1


def apart(eng, passed):
    eng.sem_inc(passed, 1)


def make_tools(nc, ctx):
    def sb(name, shape, dt=F32):
        return ctx.enter_context(nc.sbuf_tensor(name, shape, dt))

    def pb(name, shape):
        return ctx.enter_context(nc.psum_tensor(name, shape, F32))

    sems = []

    def sem(name):
        sems.append(nc.alloc_semaphore(name))
        return sems[-1]

    def give_back():
        nc.clear_and_free_semaphores(sems)
        nc.all_engine_barrier()

    ctx.callback(give_back)

    def sem2(name, n=2):
        return [sem(f"{name}{i}") for i in range(n)]

    return sb, pb, sem, sem2


def phase_norm_in(nc, x_prompt, x_sample, ident, xh, xl):
    with ExitStack() as ctx:
        sb, pb, sem, sem2 = make_tools(nc, ctx)
        x_in = sb("n_x", [P, 2, D])
        xs = sb("n_xs", [P, 2, D])
        junk = sb("n_junk", [P, D])
        ss = sb("n_ss", [P, 2])
        std = sb("n_std", [P, 2])
        rstd = sb("n_rstd", [P, 2])
        epsb = sb("n_eps", [P, 1])
        ps = pb("n_ps", [P, 2, KT, P])
        x_loaded = sem2("n_x_loaded")
        squared, std_ready, rstd_ready = sem2("n_squared"), sem2("n_std"), sem2("n_rstd")
        xs_ready, turned, hi_done, lo_done = sem2("n_xs_ready"), sem2("n_turned"), sem2("n_hi"), sem2("n_lo")
        eps_set = sem("n_eps_set")
        block = ctx.enter_context(nc.Block())

        @block.sync
        def _(sp):
            def load(j, s):
                sp.wait_ge(xs_ready[s], j)
                if is_sample(j, s):
                    src = x_sample
                else:
                    src = x_prompt[bass.ds((2 * j + s) * P, P), :]
                sp.dma_start(x_in[:, s, :], src).then_inc(x_loaded[s], 16)

            token_tiles(sp, load, lambda j, s: None)

        @block.scalar
        def _(act):
            act.wait_ge(eps_set, 1)

            def sums(j, s):
                act.wait_ge(x_loaded[s], 16 * (j + 1))
                act.wait_ge(rstd_ready[s], j)
                act.activation(junk[:, :], x_in[:, s, :], ACT.Square,
                               accum_out=ss[:, s:s + 1]).then_inc(squared[s], 1)
                act.wait_ge(squared[s], j + 1)
                act.activation(std[:, s:s + 1], ss[:, s:s + 1], ACT.Sqrt, scale=1.0 / D,
                               bias=epsb[:, :]).then_inc(std_ready[s], 1)

            def high(j, s):
                act.wait_ge(turned[s], j + 1)
                act.activation(xh[:, :, bass.ds((2 * j + s) * P, P)], ps[:, s, :, :],
                               ACT.Copy).then_inc(hi_done[s], 1)

            token_tiles(act, sums, high)

        @block.vector
        def _(dve):
            dve.memset(epsb[:, :], EPS).then_inc(eps_set, 1)

            def scale(j, s):
                dve.wait_ge(std_ready[s], j + 1)
                dve.reciprocal(rstd[:, s:s + 1], std[:, s:s + 1]).then_inc(rstd_ready[s], 1)
                dve.wait_ge(rstd_ready[s], j + 1)
                dve.wait_ge(turned[s], j)
                dve.tensor_scalar(xs[:, s, :], x_in[:, s, :], rstd[:, s:s + 1], None,
                                  ALU.mult).then_inc(xs_ready[s], 1)

            def low(j, s):
                at = bass.ds((2 * j + s) * P, P)
                dve.wait_ge(hi_done[s], j + 1)
                dve.tensor_tensor(xl[:, :, at], ps[:, s, :, :], xh[:, :, at].bitcast(F32),
                                  ALU.subtract).then_inc(lo_done[s], 1)

            token_tiles(dve, scale, low)

        @block.tensor
        def _(pe):
            def turn(j, s):
                pe.wait_ge(xs_ready[s], j + 1)
                pe.wait_ge(lo_done[s], j)
                for kt in range(KT):
                    mm = pe.transpose(ps[:, s, kt, :], xs[:, s, kt * P:(kt + 1) * P], ident[:, :])
                mm.then_inc(turned[s], 1)

            token_tiles(pe, turn, lambda j, s: None)


def weight_stream(pool, n_iter, order, gains, raw, wh, wl, raw_loaded, scaled, hi_ready, w_ready, mm_done, passed):
    pool.wait_ge(*gains)
    with pool.Fori(0, n_iter) as c:
        for m, (view, gain) in enumerate(order):
            s, u = m % 2, c * (len(order) // 2) + m // 2
            gain_b = gain.unsqueeze(2).broadcast_to([P, KT, P])
            pool.wait_ge(w_ready[s], u)
            apart(pool, passed)
            pool.dma_start(raw[:, s, :, :], view(c)).then_inc(raw_loaded[s], 16)
            pool.wait_ge(raw_loaded[s], 16 * (u + 1))
            pool.wait_ge(mm_done[(m - 2) % 4], NG * (c + 1 if m >= 2 else c))
            pool.tensor_tensor(wh[s][:, :, :], raw[:, s, :, :], gain_b, ALU.mult).then_inc(hi_ready[s], 1)
            pool.wait_ge(hi_ready[s], u + 1)
            pool.tensor_tensor(raw[:, s, :, :], raw[:, s, :, :], gain_b, ALU.mult).then_inc(scaled[s], 1)
            pool.wait_ge(scaled[s], u + 1)
            pool.tensor_tensor(wl[s][:, :, :], raw[:, s, :, :], wh[s][:, :, :].bitcast(F32),
                               ALU.subtract).then_inc(w_ready[s], 1)


def project(pe, out, w_h, w_l, x_h, x_l, a, n):
    for kt in range(KT):
        r = slice(a, a + n)
        pe.matmul(out, w_h[:, kt, :], x_h[:, kt, r], start=(kt == 0), stop=False)
        pe.matmul(out, w_h[:, kt, :], x_l[:, kt, r], start=False, stop=False)
        mm = pe.matmul(out, w_l[:, kt, :], x_h[:, kt, r], start=False, stop=(kt == KT - 1))
    return mm


def phase_conv(nc, w_in, a_gain, conv_w, state_conv, ident, xh, xl, y_t, conv_p, conv_s):
    with ExitStack() as ctx:
        sb, pb, sem, sem2 = make_tools(nc, ctx)
        raw = sb("c_raw", [P, 2, KT, P])
        wh = [sb(f"c_wh{s}", [P, KT, P], F32R) for s in range(2)]
        wl = [sb(f"c_wl{s}", [P, KT, P], F32R) for s in range(2)]
        gain = sb("c_gain", [P, KT])
        cw_all = sb("c_cw_all", [P, KT, CW])
        cw = sb("c_cw", [P, CW])
        cg = sb("c_cgate", [P, T])
        u = sb("c_u", [P, 2 + SEQ])
        us = sb("c_us", [P, NB, 2 + NQ])
        t = sb("c_t", [P, T])
        sz = sb("c_sz", [P, T])
        st_rows = sb("c_st_rows", [NB * 2, D])
        st_t = sb("c_st_t", [P, KT, NB * 2])
        edge = sb("c_edge", [P, KT, 2 + NB * 2])
        edge_rows = sb("c_edge_rows", [2 + NB * 2, D])
        pg = [pb(f"c_pg{g}", [P, 512]) for g in range(NG)]
        pm = pb("c_pm", [P, 2, 512])
        raw_loaded, scaled, hi_ready, w_ready = (
            sem2("c_raw_loaded"), sem2("c_scaled"), sem2("c_hi_ready"), sem2("c_w_ready"))
        passed = sem("c_passed")
        consts, st_turned, st_ready, zeroed = sem("c_consts"), sem("c_st_turned"), sem("c_st_ready"), sem("c_zeroed")
        mm_done = [sem(f"c_mm_{n}") for n in "chzb"]
        evac = [sem(f"c_evac_{n}") for n in "chzb"]
        taps, cw_ready, gated, edge_done = sem("c_taps"), sem("c_cw_ready"), sem("c_gated"), sem("c_edge_done")
        prefix = sem("c_prefix")
        y_stored, e_turned, e_rows, e_stored = sem("c_y_stored"), sem("c_e_turned"), sem("c_e_rows"), sem("c_e_stored")
        block = ctx.enter_context(nc.Block())
        C, HH, Z, B = range(4)
        blocks = [1, 2, 3, 0]
        w_v = w_in.rearrange("(kt p) (m c f) -> p kt m c f", p=P, m=4, f=P)
        tail = SEQ - GROUPS[-1][0]

        @block.sync
        def _(sp):
            sp.dma_start(gain[:, :], a_gain.rearrange("(kt p) -> p kt", p=P),
                         allow_slow_non_contiguous=True).then_inc(consts, 16)
            sp.dma_start(st_rows[:, :], state_conv).then_inc(consts, 16)
            for w in range(CW):
                sp.dma_start(cw_all[:, :, w], conv_w[w, :].rearrange("(c p) -> p c", p=P),
                             allow_slow_non_contiguous=True).then_inc(consts, 16)
            with sp.Fori(0, KT) as c:
                sp.wait_ge(evac[B], NG * (c + 2))
                sp.dma_start(y_t[bass.ds(c * P, P), :], sz[:, :]).then_inc(y_stored, 16)
            sp.wait_ge(e_rows, 2)
            sp.dma_start(conv_p, edge_rows[0:2, :]).then_inc(e_stored, 16)
            sp.dma_start(conv_s, edge_rows[2:2 + NB * 2, :]).then_inc(e_stored, 16)
            sp.wait_ge(y_stored, 16 * KT)
            sp.wait_ge(e_stored, 32)

        @block.gpsimd
        def _(pool):
            weight_stream(pool, KT, [(lambda c, b=b: w_v[:, :, b, c, :], gain[:, :]) for b in blocks],
                          (consts, 16 * (2 + CW)), raw, wh, wl, raw_loaded, scaled, hi_ready, w_ready, mm_done, passed)

        @block.tensor
        def _(pe):
            pe.wait_ge(consts, 16 * (2 + CW))
            for c in range(KT):
                mm = pe.transpose(pm[:, 0, c * 16:(c + 1) * 16], st_rows[:, c * P:(c + 1) * P],
                                  ident[0:NB * 2, 0:NB * 2])
            mm.then_inc(st_turned, 1)
            with pe.Fori(0, KT) as c:
                for m in range(4):
                    s = m % 2
                    pe.wait_ge(w_ready[s], 2 * c + m // 2 + 1)
                    for g, (a, n) in enumerate(GROUPS):
                        pe.wait_ge(evac[(m - 1) % 4], NG * c + g + 1)
                        mm = project(pe, pg[g][:, 0:n], wh[s], wl[s], xh, xl, a, n)
                        mm.then_inc(mm_done[m], 1)
            pe.wait_ge(edge_done, 2 * KT)
            for c in range(KT):
                mm = pe.transpose(pm[0:18, c // 4, (c % 4) * P:(c % 4 + 1) * P], edge[:, c, :], ident[:, :])
            mm.then_inc(e_turned, 1)

        @block.scalar
        def _(act):
            act.wait_ge(st_turned, 1)
            act.activation(st_t[:, :, :].rearrange("p a b -> p (a b)"), pm[:, 0, 0:KT * 16],
                           ACT.Copy).then_inc(st_ready, 1)
            with act.Fori(0, KT) as c:
                for g, (a, n) in enumerate(GROUPS):
                    act.wait_ge(mm_done[C], NG * c + g + 1)
                    act.wait_ge(evac[HH], NG * c)
                    act.activation(cg[:, a:a + n], pg[g][:, 0:n], ACT.Copy).then_inc(evac[C], 1)
                act.wait_ge(y_stored, 16 * c)
                for g, (a, n) in enumerate(GROUPS):
                    act.wait_ge(mm_done[Z], NG * c + g + 1)
                    act.activation(sz[:, a:a + n], pg[g][:, 0:n], ACT.Silu).then_inc(evac[Z], 1)
            act.wait_ge(e_turned, 1)
            for half in range(2):
                act.activation(edge_rows[:, half * 512:(half + 1) * 512], pm[0:18, half, :],
                               ACT.Copy).then_inc(e_rows, 1)

        @block.vector
        def _(dve):
            dve.wait_ge(consts, 16 * (2 + CW))
            dve.wait_ge(st_ready, 1)
            dve.memset(u[:, 0:2], 0.0).then_inc(evac[B], NG)
            t_s = t[:, SEQ:T].rearrange("p (b q) -> p b q", q=NQ)
            with dve.Fori(0, KT) as c:
                dve.wait_ge(taps, 5 * c)
                dve.tensor_copy(cw[:, :], cw_all[:, c, :]).then_inc(cw_ready, 1)
                dve.tensor_copy(us[:, :, 0:2], st_t[:, c, :].rearrange("p (b w) -> p b w", w=2))\
                   .then_inc(prefix, 1)
                for g, (a, n) in enumerate(GROUPS):
                    dve.wait_ge(mm_done[HH], NG * c + g + 1)
                    dve.wait_ge(evac[C], NG * c + g + 1)
                    np_ = n if g < NG - 1 else tail
                    op = dve.tensor_tensor(u[:, 2 + a:2 + a + np_], pg[g][:, 0:np_], cg[:, a:a + np_], ALU.mult)
                    if g == NG - 1:
                        op = dve.tensor_tensor(
                            us[:, :, 2:2 + NQ], pg[g][:, np_:n].rearrange("p (b q) -> p b q", q=NQ),
                            cg[:, SEQ:T].rearrange("p (b q) -> p b q", q=NQ), ALU.mult)
                    op.then_inc(evac[HH], 1)
                dve.wait_ge(evac[HH], NG * (c + 1))
                dve.wait_ge(cw_ready, c + 1)
                dve.wait_ge(prefix, c + 1)
                dve.wait_ge(evac[B], NG * (c + 1))
                dve.tensor_copy(edge[:, c, 0:2], u[:, SEQ:SEQ + 2]).then_inc(edge_done, 1)
                dve.tensor_copy(edge[:, c, 2:18].rearrange("p (b w) -> p b w", w=2),
                                us[:, :, NQ:NQ + 2]).then_inc(edge_done, 1)
                dve.tensor_scalar(t[:, 0:SEQ], u[:, 0:SEQ], cw[:, 0:1], None, ALU.mult).then_inc(taps, 1)
                dve.tensor_scalar(t_s, us[:, :, 0:NQ], cw[:, 0:1], None, ALU.mult).then_inc(taps, 1)
                dve.wait_ge(taps, 5 * c + 2)
                dve.scalar_tensor_tensor(t[:, 0:SEQ], u[:, 1:1 + SEQ], cw[:, 1:2], t[:, 0:SEQ],
                                         ALU.mult, ALU.add).then_inc(taps, 1)
                dve.scalar_tensor_tensor(t_s, us[:, :, 1:1 + NQ], cw[:, 1:2], t_s, ALU.mult, ALU.add)\
                   .then_inc(taps, 1)
                dve.wait_ge(taps, 5 * c + 4)
                dve.scalar_tensor_tensor(t[:, 0:SEQ], u[:, 2:2 + SEQ], cw[:, 2:3], t[:, 0:SEQ],
                                         ALU.mult, ALU.add)
                dve.scalar_tensor_tensor(t_s, us[:, :, 2:2 + NQ], cw[:, 2:3], t_s, ALU.mult, ALU.add)\
                   .then_inc(taps, 1)
                dve.wait_ge(taps, 5 * c + 5)
                for g, (a, n) in enumerate(GROUPS):
                    dve.wait_ge(evac[Z], NG * c + g + 1)
                    dve.tensor_tensor(t[:, a:a + n], t[:, a:a + n], sz[:, a:a + n], ALU.mult)\
                       .then_inc(gated, 1)
                for g, (a, n) in enumerate(GROUPS):
                    dve.wait_ge(mm_done[B], NG * c + g + 1)
                    dve.wait_ge(gated, NG * c + g + 1)
                    dve.tensor_tensor(sz[:, a:a + n], pg[g][:, 0:n], t[:, a:a + n], ALU.mult)\
                       .then_inc(evac[B], 1)


def phase_out(nc, tag, parts, w_out, post_gain, x_prompt, x_sample, ident, out_prompt, out_sample, x32):
    with ExitStack() as ctx:
        sb, pb, sem, sem2 = make_tools(nc, ctx)
        n_in = len(parts)
        raw = sb(tag + "raw", [P, 2, D])
        wh = sb(tag + "wh", [P, KT, D], F32R)
        wl = sb(tag + "wl", [P, KT, D], F32R)
        gain = sb(tag + "gain", [P, D])
        y_in = sb(tag + "y_in", [P, 2, n_in, KT, P])
        yh = [sb(f"{tag}yh{s}", [P, KT, P], F32R) for s in range(2)]
        yl = [sb(f"{tag}yl{s}", [P, KT, P], F32R) for s in range(2)]
        x_in = sb(tag + "x", [P, 2, D])
        xn = sb(tag + "xn", [P, 2, D])
        xs = sb(tag + "xs", [P, D])
        junk = sb(tag + "junk", [P, D])
        ss = sb(tag + "ss", [P, 2, 2])
        std = sb(tag + "std", [P, 2, 2])
        rstd = sb(tag + "rstd", [P, 2, 2])
        epsb = sb(tag + "eps", [P, 1])
        ph = pb(tag + "ph", [P, 2, D])
        pt = pb(tag + "pt", [P, 2, KT, P])
        w_loaded, w_hi, w_lo = sem2(tag + "w_loaded"), sem(tag + "w_hi"), sem(tag + "w_lo")
        consts = sem(tag + "consts")
        y_loaded, y_sum, y_whole, y_hi, y_lo = (sem2(tag + "y_loaded"), sem2(tag + "y_sum"), sem2(tag + "y_whole"),
                                                sem2(tag + "y_hi"), sem2(tag + "y_lo"))
        x_loaded, mm_done = sem2(tag + "x_loaded"), sem2(tag + "mm_done")
        squared, std_ready, rstd_ready = sem2(tag + "squared"), sem2(tag + "std_ready"), sem2(tag + "rstd_ready")
        normed, summed, stored = sem2(tag + "normed"), sem2(tag + "summed"), sem2(tag + "stored")
        scaled, turned, kept = sem(tag + "scaled"), sem2(tag + "turned"), sem2(tag + "kept")
        block = ctx.enter_context(nc.Block())
        w_v = w_out.rearrange("(kt p) n -> p kt n", p=P)
        views = [a.rearrange("(kt p) t -> p kt t", p=P) for a in parts]
        norms = 2 if x32 is not None else 1

        @block.sync
        def _(sp):
            sp.dma_start(gain[:, :], post_gain.partition_broadcast(P)).then_inc(consts, 16)
            for kt in range(KT):
                if kt >= 2:
                    sp.wait_ge(w_lo, kt - 1)
                sp.dma_start(raw[:, kt % 2, :], w_v[:, kt, :]).then_inc(w_loaded[kt % 2], 16)

            def load(j, s):
                at = bass.ds((2 * j + s) * P, P)
                sp.wait_ge(y_lo[s], j)
                for i, v in enumerate(views):
                    sp.dma_start(y_in[:, s, i, :, :], v[:, :, at]).then_inc(y_loaded[s], 16)
                sp.wait_ge(summed[s], j)
                src = x_sample if is_sample(j, s) else x_prompt[bass.ds((2 * j + s) * P, P), :]
                sp.dma_start(x_in[:, s, :], src).then_inc(x_loaded[s], 16)

            def store(j, s):
                sp.wait_ge(summed[s], j + 1)
                dst = out_sample if is_sample(j, s) else out_prompt[bass.ds((2 * j + s) * P, P), :]
                sp.dma_start(dst, xn[:, s, :]).then_inc(stored[s], 16)

            token_tiles(sp, load, store)
            sp.wait_ge(stored[0], 16 * (NT // 2 + 1))
            sp.wait_ge(stored[1], 16 * (NT // 2))

        @block.scalar
        def _(act):
            for kt in range(KT):
                act.wait_ge(w_loaded[kt % 2], 16 * (kt // 2 + 1))
                act.activation(wh[:, kt, :], raw[:, kt % 2, :], ACT.Copy).then_inc(w_hi, 1)

            def split(j, s):
                if n_in == 1:
                    act.wait_ge(y_loaded[s], 16 * (j + 1))
                else:
                    act.wait_ge(y_whole[s], j + 1)
                act.wait_ge(mm_done[s], j)
                act.activation(yh[s][:, :, :], y_in[:, s, 0, :, :], ACT.Copy).then_inc(y_hi[s], 1)

            def rms(src, j, s, k):
                act.wait_ge(rstd_ready[s], norms * j + k)
                act.activation(junk[:, :], src, ACT.Square, accum_out=ss[:, s, k:k + 1]).then_inc(squared[s], 1)
                act.wait_ge(squared[s], norms * j + k + 1)
                act.activation(std[:, s, k:k + 1], ss[:, s, k:k + 1], ACT.Sqrt, scale=1.0 / D,
                               bias=epsb[:, :]).then_inc(std_ready[s], 1)

            def tail(j, s):
                act.wait_ge(mm_done[s], j + 1)
                rms(ph[:, s, :], j, s, 0)
                if x32 is not None:
                    act.wait_ge(summed[s], j + 1)
                    rms(xn[:, s, :], j, s, 1)
                    act.wait_ge(turned[s], j + 1)
                    act.activation(x32[:, :, bass.ds((2 * j + s) * P, P)], pt[:, s, :, :],
                                   ACT.Copy).then_inc(kept[s], 1)

            act.wait_ge(consts, 17)
            token_tiles(act, split, tail)

        @block.vector
        def _(dve):
            dve.memset(epsb[:, :], EPS).then_inc(consts, 1)
            for kt in range(KT):
                dve.wait_ge(w_hi, kt + 1)
                dve.tensor_tensor(wl[:, kt, :], raw[:, kt % 2, :], wh[:, kt, :].bitcast(F32),
                                  ALU.subtract).then_inc(w_lo, 1)

            def split(j, s):
                y = y_in[:, s, 0, :, :]
                if n_in == 3:
                    dve.wait_ge(y_loaded[s], 16 * n_in * (j + 1))
                    dve.tensor_tensor(y, y, y_in[:, s, 1, :, :], ALU.add).then_inc(y_sum[s], 1)
                    dve.wait_ge(y_sum[s], j + 1)
                    dve.tensor_tensor(y, y, y_in[:, s, 2, :, :], ALU.mult).then_inc(y_whole[s], 1)
                dve.wait_ge(y_hi[s], j + 1)
                dve.tensor_tensor(yl[s][:, :, :], y, yh[s][:, :, :].bitcast(F32),
                                  ALU.subtract).then_inc(y_lo[s], 1)

            def inverse(j, s, k):
                dve.wait_ge(std_ready[s], norms * j + k + 1)
                dve.reciprocal(rstd[:, s, k:k + 1], std[:, s, k:k + 1]).then_inc(rstd_ready[s], 1)
                dve.wait_ge(rstd_ready[s], norms * j + k + 1)

            def tail(j, s):
                inverse(j, s, 0)
                dve.wait_ge(stored[s], 16 * j)
                dve.scalar_tensor_tensor(xn[:, s, :], ph[:, s, :], rstd[:, s, 0:1], gain[:, :],
                                         ALU.mult, ALU.mult).then_inc(normed[s], 1)
                dve.wait_ge(normed[s], j + 1)
                dve.wait_ge(x_loaded[s], 16 * (j + 1))
                dve.tensor_tensor(xn[:, s, :], xn[:, s, :], x_in[:, s, :], ALU.add).then_inc(summed[s], 1)
                if x32 is not None:
                    inverse(j, s, 1)
                    dve.wait_ge(turned[1 - s], j + s)
                    dve.tensor_scalar(xs[:, :], xn[:, s, :], rstd[:, s, 1:2], None, ALU.mult).then_inc(scaled, 1)

            dve.wait_ge(consts, 17)
            token_tiles(dve, split, tail)

        @block.tensor
        def _(pe):
            pe.wait_ge(w_lo, KT)

            def multiply(j, s):
                pe.wait_ge(y_lo[s], j + 1)
                pe.wait_ge(normed[s], j)
                for n in range(2):
                    r = slice(n * 512, (n + 1) * 512)
                    for kt in range(KT):
                        o = ph[:, s, r]
                        pe.matmul(o, yh[s][:, kt, :], wh[:, kt, r], start=(kt == 0), stop=False)
                        pe.matmul(o, yh[s][:, kt, :], wl[:, kt, r], start=False, stop=False)
                        mm = pe.matmul(o, yl[s][:, kt, :], wh[:, kt, r], start=False, stop=(kt == KT - 1))
                mm.then_inc(mm_done[s], 1)

            def turn(j, s):
                if x32 is not None:
                    pe.wait_ge(scaled, 2 * j + s + 1)
                    pe.wait_ge(kept[s], j)
                    for kt in range(KT):
                        mm = pe.transpose(pt[:, s, kt, :], xs[:, kt * P:(kt + 1) * P], ident[:, :])
                    mm.then_inc(turned[s], 1)

            token_tiles(pe, multiply, turn)


def phase_qkvz(nc, w_k, w_v, w_qz, kv_gain, b_gain, ident, x32, xl, qh_t, ql_t, kh_t, kl_t, sz_t,
               k_prompt, v_prompt, k_sample, v_sample):
    with ExitStack() as ctx:
        sb, pb, sem, sem2 = make_tools(nc, ctx)
        xh = sb("q_xh", [P, KT, T], F32R)
        raw = sb("q_raw", [P, 2, KT, P])
        wh = [sb(f"q_wh{s}", [P, KT, P], F32R) for s in range(2)]
        wl = [sb(f"q_wl{s}", [P, KT, P], F32R) for s in range(2)]
        g_kv = sb("q_g_kv", [P, KT])
        g_b = sb("q_g_b", [P, KT])
        hi = sb("q_hi", [P, 2, 512], F32R)
        lo = sb("q_lo", [P, 2, 512], F32R)
        full = sb("q_full", [P, 2, 512])
        gate = sb("q_gate", [P, 2, 512])
        rows = sb("q_rows", [P, 2, 4, P])
        pg = [pb(f"q_pg{g}", [P, 512]) for g in range(NG)]
        pt = pb("q_pt", [P, 2, 4, P])
        raw_loaded, scaled, hi_ready, w_ready = (
            sem2("q_raw_loaded"), sem2("q_scaled"), sem2("q_hi_ready"), sem2("q_w_ready"))
        passed, passed_sp = sem("q_passed"), sem("q_passed_sp")
        consts, x_hi, x_lo = sem("q_consts"), sem("q_x_hi"), sem("q_x_lo")
        mm_done = [sem(f"q_mm_{n}") for n in "kvqz"]
        high, low, hl_stored = sem2("q_high"), sem2("q_low"), sem2("q_hl_stored")
        whole, turned, rowed, rows_stored = sem2("q_whole"), sem2("q_turned"), sem2("q_rowed"), sem2("q_rows_stored")
        gated, gate_stored = sem("q_gated"), sem2("q_gate_stored")
        block = ctx.enter_context(nc.Block())
        K, V, Q, Z = range(4)
        k_v = w_k.rearrange("(kt p) (c f) -> p kt c f", p=P, f=P)
        v_v = w_v.rearrange("(kt p) (c f) -> p kt c f", p=P, f=P)
        qz_v = w_qz.rearrange("(kt p) (m c f) -> p kt m c f", p=P, m=2, f=P)
        def uses(kinds, m, g):
            n = [(mm, gg) for mm in kinds for gg in range(NG)]
            s = (NG * m + g) % 2
            same = [x for x in n if (NG * x[0] + x[1]) % 2 == s]
            return s, len(same), same.index((m, g))

        @block.sync
        def _(sp):
            for tile, src in ((g_kv, kv_gain), (g_b, b_gain)):
                sp.dma_start(tile[:, :], src.rearrange("(kt p) -> p kt", p=P),
                             allow_slow_non_contiguous=True).then_inc(consts, 16)

            def rows_out(c, m, g):
                a, n = GROUPS[g]
                s, per, k = uses((K, V), m, g)
                sp.wait_ge(rowed[s], per * c + k + 1)
                apart(sp, passed_sp)
                out_p, out_s = ((k_prompt, k_sample), (v_prompt, v_sample))[m]
                nt, np_ = n // P, (min(a + n, SEQ) - a) // P
                cols = bass.ds(c * P, P)
                sp.dma_start(out_p[a:a + np_ * P, cols].rearrange("(i p) f -> p i f", p=P),
                             rows[:, s, 0:np_, :]).then_inc(rows_stored[s], 16)
                if np_ < nt:
                    sp.dma_start(out_s[:, cols], rows[:, s, np_, :]).then_inc(rows_stored[s], 16)
                else:
                    sp.sem_inc(rows_stored[s], 16)

            with sp.Fori(0, KT) as c:
                at = bass.ds(c * P, P)
                for m in (K, V, Q, Z):
                    for g, (a, n) in enumerate(GROUPS):
                        if m in (K, Q):
                            s, per, k = uses((K, Q), m, g)
                            for part, done, dst in ((hi, high, (kh_t, qh_t)), (lo, low, (kl_t, ql_t))):
                                sp.wait_ge(done[s], per * c + k + 1)
                                sp.dma_start(dst[m == Q][at, a:a + n], part[:, s, 0:n].bitcast(F32))\
                                  .then_inc(hl_stored[s], 16)
                        if m == Z:
                            s, per, k = uses((Z,), m, g)
                            sp.wait_ge(gated, NG * (c + 1) + g + 1)
                            sp.dma_start(sz_t[at, a:a + n], gate[:, s, 0:n]).then_inc(gate_stored[s], 16)
                        if m in (K, V) and g >= 1:
                            rows_out(c, m, g - 1)
                        if m in (V, Q) and g == 0:
                            rows_out(c, m - 1, NG - 1)
            for s in range(2):
                sp.wait_ge(hl_stored[s], 32 * uses((K, Q), 0, s)[1] * KT)
                sp.wait_ge(gate_stored[s], 16 * uses((Z,), Z, 1 - s)[1] * KT)
                sp.wait_ge(rows_stored[s], 32 * uses((K, V), 0, s)[1] * KT)

        @block.gpsimd
        def _(pool):
            order = [(lambda c: k_v[:, :, c, :], g_kv[:, :]), (lambda c: v_v[:, :, c, :], g_kv[:, :]),
                     (lambda c: qz_v[:, :, 0, c, :], g_b[:, :]), (lambda c: qz_v[:, :, 1, c, :], g_b[:, :])]
            weight_stream(pool, KT, order, (consts, 32), raw, wh, wl, raw_loaded, scaled, hi_ready, w_ready, mm_done, passed)

        @block.tensor
        def _(pe):
            pe.wait_ge(x_lo, NG)

            def turn(c, m, g):
                s, per, k = uses((K, V), m, g)
                pe.wait_ge(whole[s], per * c + k + 1)
                pe.wait_ge(rowed[s], per * c + k)
                for i in range(GROUPS[g][1] // P):
                    mm = pe.transpose(pt[:, s, i, :], full[:, s, i * P:(i + 1) * P], ident[:, :])
                mm.then_inc(turned[s], 1)

            def bank_read(c, m, g):
                if m == K:
                    pe.wait_ge(gated, NG * c + g + 1)
                else:
                    kinds, done = ((K, Q), low) if m - 1 in (K, Q) else ((K, V), whole)
                    s, per, k = uses(kinds, m - 1, g)
                    pe.wait_ge(done[s], per * c + k + 1)

            with pe.Fori(0, KT) as c:
                for m in range(4):
                    s = m % 2
                    pe.wait_ge(w_ready[s], 2 * c + m // 2 + 1)
                    for g, (a, n) in enumerate(GROUPS):
                        bank_read(c, m, g)
                        mm = project(pe, pg[g][:, 0:n], wh[s], wl[s], xh, xl, a, n)
                        mm.then_inc(mm_done[m], 1)
                        if m in (K, V) and g >= 1:
                            turn(c, m, g - 1)
                        if m in (V, Q) and g == 0:
                            turn(c, m - 1, NG - 1)

        def rows_copy(act, c, m, g):
            s, per, k = uses((K, V), m, g)
            nt = GROUPS[g][1] // P
            act.wait_ge(turned[s], per * c + k + 1)
            act.wait_ge(rows_stored[s], 32 * (per * c + k))
            act.activation(rows[:, s, 0:nt, :], pt[:, s, 0:nt, :], ACT.Copy).then_inc(rowed[s], 1)

        @block.scalar
        def _(act):
            for g, (a, n) in enumerate(GROUPS):
                act.activation(xh[:, :, a:a + n], x32[:, :, a:a + n], ACT.Copy).then_inc(x_hi, 1)
            with act.Fori(0, KT) as c:
                for m in range(4):
                    for g, (a, n) in enumerate(GROUPS):
                        act.wait_ge(mm_done[m], NG * c + g + 1)
                        if m in (K, V):
                            s, per, k = uses((K, V), m, g)
                            act.wait_ge(turned[s], per * c + k)
                            act.activation(full[:, s, 0:n], pg[g][:, 0:n], ACT.Copy).then_inc(whole[s], 1)
                        if m == Q:
                            s, per, k = uses((K, Q), m, g)
                            act.wait_ge(hl_stored[s], 32 * (per * c + k))
                            act.activation(hi[:, s, 0:n], pg[g][:, 0:n], ACT.Copy).then_inc(high[s], 1)
                        if m == Z:
                            s, per, k = uses((Z,), m, g)
                            act.wait_ge(gate_stored[s], 16 * (per * c + k))
                            act.activation(gate[:, s, 0:n], pg[g][:, 0:n], ACT.Silu).then_inc(gated, 1)
                        if m in (K, V) and g >= 1:
                            rows_copy(act, c, m, g - 1)
                        if m in (V, Q) and g == 0:
                            rows_copy(act, c, m - 1, NG - 1)

        @block.vector
        def _(dve):
            for g, (a, n) in enumerate(GROUPS):
                dve.wait_ge(x_hi, g + 1)
                dve.tensor_tensor(xl[:, :, a:a + n], x32[:, :, a:a + n], xh[:, :, a:a + n].bitcast(F32),
                                  ALU.subtract).then_inc(x_lo, 1)
            dve.sem_inc(gated, NG)
            with dve.Fori(0, KT) as c:
                for m in (K, Q):
                    for g, (a, n) in enumerate(GROUPS):
                        s, per, k = uses((K, Q), m, g)
                        if m == K:
                            ws, wper, wk = uses((K, V), m, g)
                            dve.wait_ge(whole[ws], wper * c + wk + 1)
                            dve.wait_ge(hl_stored[s], 32 * (per * c + k))
                            dve.tensor_copy(hi[:, s, 0:n], pg[g][:, 0:n]).then_inc(high[s], 1)
                        dve.wait_ge(high[s], per * c + k + 1)
                        dve.wait_ge(hl_stored[s], 32 * (per * c + k))
                        dve.tensor_tensor(lo[:, s, 0:n], pg[g][:, 0:n], hi[:, s, 0:n].bitcast(F32),
                                          ALU.subtract).then_inc(low[s], 1)


Z_W = 1024
PIECES = [(i, p, min(p + Z_W, (i + 1) * P)) for i in range(QT) for p in range(0, (i + 1) * P, Z_W)]
BLOCKS = [(g, kb) for g in range(NGQ) for kb in range(QG * (g + 1))]
N_PIECE, N_BLOCK = len(PIECES), len(BLOCKS)


def phase_attend(nc, qh_t, ql_t, kh_t, kl_t, v_prompt, ident, identr, maskr, oa_t, ob_t):
    with ExitStack() as ctx:
        sb, pb, sem, sem2 = make_tools(nc, ctx)
        q2 = [sb(f"a_q{s}", [P, SEQ], F32R) for s in range(2)]
        kh2 = [sb(f"a_kh{s}", [P, SEQ], F32R) for s in range(2)]
        kl2 = [sb(f"a_kl{s}", [P, SEQ], F32R) for s in range(2)]
        v_in = sb("a_v_in", [P, 2, QT, HD])
        v2 = [sb(f"a_v{s}", [P, QT, 2, HD], F32R) for s in range(2)]
        a = sb("a_a", [P, 2, QG, SEQ])
        keep = sb("a_keep", [P, 2, SEQ])
        prod = sb("a_prod", [P, 2, SEQ + 1])
        ath = [sb(f"a_ath{s}", [P, QG * P], F32R) for s in range(4)]
        atl = [sb(f"a_atl{s}", [P, QG * P], F32R) for s in range(4)]
        o_sb = sb("a_o", [P, 2, QG * P])
        pz = pb("a_pz", [P, 2, Z_W])
        pt = pb("a_pt", [P, 2, QG * P])
        po = pb("a_po", [P, 2, QG * P])
        passed, passed_sp = sem("a_passed"), sem("a_passed_sp")
        qk_loaded, v_loaded = sem2("a_qk_loaded"), sem2("a_v_loaded")
        v_hi, v_ready = sem2("a_v_hi"), sem2("a_v_ready")
        z_ready, z_used = sem2("a_z_ready"), sem2("a_z_used")
        scanned, weighted, one_set = sem2("a_scanned"), sem2("a_weighted"), sem("a_one_set")
        t_ready, at_hi, at_ready, av_done = (sem2("a_t_ready"), sem2("a_at_hi", 4), sem2("a_at_ready", 4),
                                             sem2("a_av_done", 4))
        o_read, o_stored = sem2("a_o_read"), sem2("a_o_stored")
        block = ctx.enter_context(nc.Block())
        NPAIR = H // 2
        group_end = [BLOCKS.index((g, QG * (g + 1) - 1)) // 4 + 1 for g in range(NGQ)]
        per_z, per_i, per_at = N_PIECE // 2, QT // 2, N_BLOCK // 4

        def heads(step, last):
            for hh in range(2):
                for g in range(NGQ):
                    nxt = (0, hh, g + 1) if g < NGQ - 1 else (0, 1, 0) if hh == 0 else (1, 0, 0)
                    step(hh, g, None if last and nxt[0] else nxt)

        def all_heads(eng, prologue, step, epilogue=None):
            prologue()
            with eng.Fori(0, NPAIR - 1) as pr:
                heads(lambda hh, g, nxt: step(pr, hh, g, nxt), False)
            heads(lambda hh, g, nxt: step(NPAIR - 1, hh, g, nxt), True)

        def interleaved(score, value, tail):
            def step(pr, hh, g, nxt):
                first = BLOCKS.index((g, 0))
                for q in range(QG):
                    for b in range(first + q * (g + 1), first + (q + 1) * (g + 1)):
                        value(pr, hh, b)
                    if nxt:
                        score(pr + nxt[0], nxt[1], QG * nxt[2] + q)
                tail(pr, hh, g, nxt)
            return step

        @block.sync
        def _(sp):
            def load(pr, hh):
                rows = bass.ds((2 * pr + hh) * HD, HD)
                for dst, top, bottom in ((q2, qh_t, ql_t), (kh2, kh_t, kh_t), (kl2, kl_t, kl_t)):
                    sp.dma_start(dst[hh][0:HD, :].bitcast(F32), top[rows, 0:SEQ]).then_inc(qk_loaded[hh], 16)
                    sp.dma_start(dst[hh][HD:P, :].bitcast(F32), bottom[rows, 0:SEQ]).then_inc(qk_loaded[hh], 16)

            def load_v(pr, hh):
                cols = bass.ds((2 * pr + hh) * HD, HD)
                sp.dma_start(v_in[:, hh, :, :], v_prompt[:, cols].rearrange("(b p) d -> p b d", p=P))\
                  .then_inc(v_loaded[hh], 16)

            def prologue():
                for hh in range(2):
                    load(0, hh)
                    load_v(0, hh)

            def step(pr, hh, g, nxt):
                more = nxt is not None and not (isinstance(pr, int) and pr == NPAIR - 1)
                if g == NGQ - 1 and not (isinstance(pr, int) and pr == NPAIR - 1):
                    sp.wait_ge(z_ready[1], per_z * (2 * pr + hh + 1))
                    load(pr + 1, hh)
                    sp.wait_ge(v_ready[hh], pr + 1)
                    apart(sp, passed_sp)
                    load_v(pr + 1, hh)
                sp.wait_ge(o_read[g % 2], (2 * pr + hh) * 2 + g // 2 + 1)
                rows, at = bass.ds((2 * pr + hh) * HD, HD), slice(g * QG * P, (g + 1) * QG * P)
                sp.dma_start(oa_t[rows, at], o_sb[0:HD, g % 2, :]).then_inc(o_stored[g % 2], 16)
                sp.dma_start(ob_t[rows, at], o_sb[HD:P, g % 2, :]).then_inc(o_stored[g % 2], 16)

            all_heads(sp, prologue, step)
            for s in range(2):
                sp.wait_ge(o_stored[s], 32 * H * NGQ // 2)

        @block.tensor
        def _(pe):
            def score(pr, hh, i):
                if i == 0:
                    pe.wait_ge(qk_loaded[hh], 96 * (pr + 1))
                for n, (ii, p0, p1) in enumerate(PIECES):
                    if ii != i:
                        continue
                    s = n % 2
                    pe.wait_ge(z_used[s], (2 * pr + hh) * per_z + n // 2)
                    for r0 in range(p0, p1, 512):
                        r1 = min(r0 + 512, p1)
                        o = pz[:, s, r0 - p0:r1 - p0]
                        lhs = q2[hh][:, i * P:(i + 1) * P]
                        pe.matmul(o, lhs, kh2[hh][:, r0:r1], start=True, stop=False)
                        if r1 == (i + 1) * P:
                            pe.matmul(pz[:, s, r1 - P - p0:r1 - p0], identr[:, :], maskr[:, :],
                                      start=False, stop=False)
                        mm = pe.matmul(o, lhs, kl2[hh][:, r0:r1], start=False, stop=True)
                    mm.then_inc(z_ready[s], 1)

            def multiply(pr, hh, b):
                g, kb = BLOCKS[b]
                c0, s = max(0, kb - QG * g) * P, b % 4
                if kb == 0:
                    pe.wait_ge(o_read[g % 2], (2 * pr + hh) * 2 + g // 2)
                pe.wait_ge(at_ready[s], (2 * pr + hh) * per_at + b // 4 + 1)
                o = po[:, g % 2, c0:QG * P]
                last = kb == QG * (g + 1) - 1
                pe.matmul(o, v2[hh][:, kb, :, :], ath[s][:, c0:], start=(kb == 0), stop=False,
                          skip_group_check=True)
                pe.matmul(o, v2[hh][:, kb, :, :], atl[s][:, c0:], start=False, stop=last,
                          skip_group_check=True).then_inc(av_done[s], 1)

            def value(pr, hh, b):
                g, kb = BLOCKS[b]
                if b == 0:
                    pe.wait_ge(v_ready[hh], pr + 1)
                if kb == 0:
                    for i in (QG * g + 2, QG * g + 3):
                        pe.wait_ge(weighted[i % 2], (2 * pr + hh) * per_i + i // 2 + 1)
                pe.wait_ge(at_ready[(b - 2) % 4], (2 * pr + hh) * per_at + (b - 2) // 4 + 1)
                for i in range(max(kb, QG * g), QG * (g + 1)):
                    q = i - QG * g
                    mm = pe.transpose(pt[:, b % 2, q * P:(q + 1) * P], a[:, g % 2, q, kb * P:(kb + 1) * P],
                                      ident[:, :])
                mm.then_inc(t_ready[b % 2], 1)
                if kb >= 2:
                    multiply(pr, hh, b - 2)

            def tail(pr, hh, g, nxt):
                end = BLOCKS.index((g, QG * (g + 1) - 1))
                multiply(pr, hh, end - 1)
                multiply(pr, hh, end)

            def prologue():
                for i in range(QG):
                    score(0, 0, i)

            all_heads(pe, prologue, interleaved(score, value, tail))

        @block.scalar
        def _(act):
            def score(pr, hh, i):
                for n, (ii, p0, p1) in enumerate(PIECES):
                    if ii != i:
                        continue
                    s, g = n % 2, i // QG
                    if p0 == 0:
                        if g >= 2:
                            act.wait_ge(av_done[3], (2 * pr + hh) * per_at + group_end[g - 2])
                        elif not (isinstance(pr, int) and pr == 0 and hh == 0):
                            act.wait_ge(av_done[3], (2 * pr + hh - 1) * per_at + group_end[g + 2])
                        act.wait_ge(scanned[i % 2], (2 * pr + hh) * per_i + i // 2)
                    act.wait_ge(z_ready[s], (2 * pr + hh) * per_z + n // 2 + 1)
                    act.activation(a[:, g % 2, i % QG, p0:p1], pz[:, s, 0:p1 - p0], ACT.Sigmoid, scale=SCALE)
                    act.activation(keep[:, i % 2, p0:p1], pz[:, s, 0:p1 - p0], ACT.Sigmoid,
                                   scale=-SCALE).then_inc(z_used[s], 1)

            def value(pr, hh, b):
                g, kb = BLOCKS[b]
                c0, s = max(0, kb - QG * g) * P, b % 4
                act.wait_ge(t_ready[b % 2], (2 * pr + hh) * (N_BLOCK // 2) + b // 2 + 1)
                act.wait_ge(av_done[s], (2 * pr + hh) * per_at + b // 4)
                act.activation(ath[s][:, c0:], pt[:, b % 2, c0:], ACT.Copy).then_inc(at_hi[s], 1)

            def tail(pr, hh, g, nxt):
                act.wait_ge(av_done[3], (2 * pr + hh) * per_at + group_end[g])
                act.wait_ge(o_stored[g % 2], 32 * ((2 * pr + hh) * 2 + g // 2))
                act.activation(o_sb[:, g % 2, :], po[:, g % 2, :], ACT.Copy).then_inc(o_read[g % 2], 1)

            def prologue():
                for i in range(QG):
                    score(0, 0, i)

            all_heads(act, prologue, interleaved(score, value, tail))

        def weight(eng, pr, hh, i):
            s, w = i % 2, (i + 1) * P
            tile = a[:, (i // QG) % 2, i % QG, 0:w]
            eng.wait_ge(scanned[s], (2 * pr + hh) * per_i + i // 2 + 1)
            eng.tensor_tensor(tile, tile, prod[:, s, SEQ - w + 1:SEQ + 1], ALU.mult).then_inc(weighted[s], 1)

        @block.vector
        def _(dve):
            def score(pr, hh, i):
                s, w = i % 2, (i + 1) * P
                n = max(n for n, (ii, _, _) in enumerate(PIECES) if ii == i)
                dve.wait_ge(z_used[n % 2], (2 * pr + hh) * per_z + n // 2 + 1)
                dve.wait_ge(weighted[s], (2 * pr + hh) * per_i + i // 2)
                dve.tensor_tensor_scan(prod[:, s, SEQ - w:SEQ][:, ::-1], keep[:, s, 0:w][:, ::-1],
                                       keep[:, s, 0:w][:, ::-1], 1.0, ALU.mult, ALU.bypass)\
                   .then_inc(scanned[s], 1)
                if s == 0:
                    weight(dve, pr, hh, i)

            def value(pr, hh, b):
                g, kb = BLOCKS[b]
                c0, s = max(0, kb - QG * g) * P, b % 4
                dve.wait_ge(at_hi[s], (2 * pr + hh) * per_at + b // 4 + 1)
                dve.tensor_tensor(atl[s][:, c0:], pt[:, b % 2, c0:], ath[s][:, c0:].bitcast(F32),
                                  ALU.subtract).then_inc(at_ready[s], 1)

            def prologue():
                dve.memset(prod[:, :, SEQ:SEQ + 1], 1.0).then_inc(one_set, 1)
                dve.wait_ge(one_set, 1)
                for i in range(QG):
                    score(0, 0, i)

            all_heads(dve, prologue, interleaved(score, value, lambda *x: None))

        @block.gpsimd
        def _(pool):
            def score(pr, hh, i):
                if i % 2:
                    weight(pool, pr, hh, i)

            def split_v(pr, hh):
                pool.wait_ge(v_loaded[hh], 16 * (pr + 1))
                apart(pool, passed)
                pool.tensor_copy(v2[hh][:, :, 0, :], v_in[:, hh, :, :]).then_inc(v_hi[hh], 1)
                pool.wait_ge(v_hi[hh], pr + 1)
                pool.tensor_tensor(v2[hh][:, :, 1, :], v_in[:, hh, :, :], v2[hh][:, :, 0, :].bitcast(F32),
                                   ALU.subtract).then_inc(v_ready[hh], 1)

            def tail(pr, hh, g, nxt):
                if g == 1:
                    if hh == 0:
                        pool.wait_ge(av_done[3], (2 * pr) * per_at)
                        split_v(pr, 1)
                    elif not (isinstance(pr, int) and pr == NPAIR - 1):
                        pool.wait_ge(av_done[3], (2 * pr + 1) * per_at)
                        split_v(pr + 1, 0)

            def prologue():
                split_v(0, 0)
                pool.wait_ge(one_set, 1)
                for i in range(QG):
                    score(0, 0, i)

            all_heads(pool, prologue, interleaved(score, lambda *x: None, tail))


def phase_attend_sample(nc, qh_t, ql_t, kh_t, kl_t, cache_k, cache_v, v_sample, ident, identr, mask_r,
                        oa_t, ob_t):
    with ExitStack() as ctx:
        sb, pb, sem, sem2 = make_tools(nc, ctx)
        NK, HH, KB = PAST + NQ, H // 2, PAST // P
        q_all = sb("s_q", [P, H, P])
        knh = sb("s_knh", [P, H, P], F32R)
        knl = sb("s_knl", [P, H, P], F32R)
        q_pad = [sb(f"s_q_pad{s}", [P, HH * (P + NQ)], F32R) for s in range(2)]
        k_in = sb("s_k_in", [P, KB, H, 2, HD])
        v_in = sb("s_v_in", [P, KB, D])
        vn_in = sb("s_vn_in", [NQ, D])
        kth = sb("s_kth", [P, H, PAST], F32R)
        ktl = sb("s_ktl", [P, H, PAST], F32R)
        v2 = sb("s_v2", [P, KB, H, 2, HD], F32R)
        vn2 = sb("s_vn2", [NQ, H, 2, HD], F32R)
        a = sb("s_a", [P, 2, NK])
        keep = sb("s_keep", [P, 2, NK])
        prod = sb("s_prod", [P, 2, NK + 1])
        ath = [sb(f"s_ath{s}", [P, KB + 1, P], F32R) for s in range(2)]
        atl = [sb(f"s_atl{s}", [P, KB + 1, P], F32R) for s in range(2)]
        o_sb = sb("s_o", [P, H, P])
        pz = pb("s_pz", [P, 2, 512])
        pt = pb("s_pt", [P, 2, 4, P])
        po = pb("s_po", [P, H, P])
        loaded, k_loaded, v_loaded = sem("s_loaded"), sem("s_k_loaded"), sem("s_v_loaded")
        zeroed, q_set = sem("s_zeroed"), sem2("s_q_set")
        k_turned, k_hi, k_lo = sem2("s_k_turned"), sem2("s_k_hi"), sem2("s_k_lo")
        v_hi, v_lo = sem("s_v_hi"), sem("s_v_lo")
        z_ready, z_used, scanned, weighted = sem2("s_z_ready"), sem2("s_z_used"), sem2("s_scanned"), sem2("s_weighted")
        a_turned, at_hi, at_lo, av_done = sem2("s_a_turned"), sem2("s_at_hi"), sem2("s_at_lo"), sem2("s_av_done")
        o_read, o_stored = sem("s_o_read"), sem("s_o_stored")
        block = ctx.enter_context(nc.Block())
        NROUND = KB * H // 4
        new = slice(SEQ, T)
        head_major = lambda ap: ap[:, new].rearrange("(h d) t -> d h t", d=HD)

        @block.sync
        def _(sp):
            for dst, top, bottom in ((q_all, qh_t, ql_t), (knh, kh_t, kh_t), (knl, kl_t, kl_t)):
                for part, src in ((slice(0, HD), top), (slice(HD, P), bottom)):
                    d = dst[part, :, :] if dst is q_all else dst[part, :, :].bitcast(F32)
                    sp.dma_start(d, head_major(src)).then_inc(loaded, 16)
            with sp.Fori(0, NB) as b:
                sp.wait_ge(k_turned[1], NROUND // 2 * b)
                for twin in range(2):
                    for kb in range(KB):
                        sp.dma_start(k_in[:, kb, :, twin, :],
                                     cache_k[b, kb * P:(kb + 1) * P, :].rearrange("p (h d) -> p h d", d=HD))\
                          .then_inc(k_loaded, 16)
                sp.wait_ge(v_lo, 2 * b)
                sp.dma_start(v_in[:, :, :], cache_v[b, :, :].rearrange("(kb p) n -> p kb n", p=P))\
                  .then_inc(v_loaded, 16)
                sp.dma_start(vn_in[:, :], v_sample[bass.ds(b * NQ, NQ), :]).then_inc(v_loaded, 16)
            sp.wait_ge(o_read, 4)
            for part, dst in ((slice(0, HD), oa_t), (slice(HD, P), ob_t)):
                sp.dma_start(head_major(dst), o_sb[part, :, :]).then_inc(o_stored, 16)
            sp.wait_ge(o_stored, 32)

        @block.tensor
        def _(pe):
            pe.wait_ge(loaded, 96)
            with pe.Fori(0, NB) as b:
                pe.wait_ge(k_loaded, 32 * KB * (b + 1))
                for r in range(NROUND):
                    s, kb = r % 2, r // (H // 4)
                    pe.wait_ge(k_lo[s], NROUND // 2 * b + r // 2)
                    if r < 2:
                        pe.wait_ge(at_lo[s], 2 * b)
                    for i in range(4):
                        h = (4 * r + i) % H
                        mm = pe.transpose(pt[:, s, i, :], k_in[:, kb, h, :, :], ident[:, :])
                    mm.then_inc(k_turned[s], 1)
                for f in range(2):
                    pe.wait_ge(q_set[f], b + 1)
                    pe.wait_ge(z_used[f], b)
                    for s in range(2):
                        pe.wait_ge(k_lo[s], NROUND // 2 * (b + 1))
                    lhs = [q_pad[f][:, j * P:(j + 1) * P] for j in range(HH)]
                    for j in range(HH):
                        o = pz[:, f, 0:PAST]
                        pe.matmul(o, lhs[j], kth[:, HH * f + j, :], start=(j == 0), stop=False)
                        pe.matmul(o, lhs[j], ktl[:, HH * f + j, :], start=False, stop=(j == HH - 1))
                    for j in range(HH):
                        o = pz[:, f, PAST:NK]
                        at = bass.ds(b * NQ, NQ)
                        pe.matmul(o, lhs[j], knh[:, HH * f + j, at], start=(j == 0), stop=False)
                        pe.matmul(o, lhs[j], knl[:, HH * f + j, at], start=False, stop=False)
                    pe.matmul(o, identr[:, :], mask_r[:, :], start=False, stop=True).then_inc(z_ready[f], 1)
                for f in range(2):
                    pe.wait_ge(weighted[f], b + 1)
                    for kb in range(KB):
                        pe.transpose(pt[:, f, kb, :], a[:, f, kb * P:(kb + 1) * P], ident[:, :])
                    pe.transpose(pt[0:NQ, f, KB, :], a[:, f, PAST:NK], ident[:, :]).then_inc(a_turned[f], 1)
                pe.wait_ge(v_lo, 2 * (b + 1))
                for f in range(2):
                    pe.wait_ge(at_lo[f], 2 * (b + 1))
                    for j in range(HH):
                        h = HH * f + j
                        o = po[:, h, bass.ds(b * NQ, NQ)]
                        c = slice(j * NQ, (j + 1) * NQ)
                        for kb in range(KB):
                            pe.matmul(o, v2[:, kb, h, :, :], ath[f][:, kb, c], start=(kb == 0), stop=False)
                            pe.matmul(o, v2[:, kb, h, :, :], atl[f][:, kb, c], start=False, stop=False)
                        pe.matmul(o, vn2[:, h, :, :], ath[f][0:NQ, KB, c], start=False, stop=False)
                        mm = pe.matmul(o, vn2[:, h, :, :], atl[f][0:NQ, KB, c], start=False, stop=True)
                    mm.then_inc(av_done[f], 1)

        @block.scalar
        def _(act):
            with act.Fori(0, NB) as b:
                for r in range(NROUND):
                    s, kb, h0 = r % 2, r // (H // 4), (4 * r) % H
                    act.wait_ge(k_turned[s], NROUND // 2 * b + r // 2 + 1)
                    if r == 0:
                        act.wait_ge(z_ready[1], b)
                    act.activation(kth[:, h0:h0 + 4, kb * P:(kb + 1) * P], pt[:, s, :, :],
                                   ACT.Copy).then_inc(k_hi[s], 1)
                act.wait_ge(v_loaded, 32 * (b + 1))
                act.wait_ge(av_done[1], b)
                split = lambda ap: ap.rearrange("p kb (h d) -> p (kb h) d", d=HD)
                act.activation(v2[:, :, :, 0, :].rearrange("p kb h d -> p (kb h) d"), split(v_in[:, :, :]),
                               ACT.Copy).then_inc(v_hi, 1)
                act.activation(vn2[:, :, 0, :], vn_in[:, :].rearrange("p (h d) -> p h d", d=HD),
                               ACT.Copy).then_inc(v_hi, 1)
                for f in range(2):
                    act.wait_ge(z_ready[f], b + 1)
                    act.wait_ge(a_turned[f], b)
                    act.activation(a[:, f, :], pz[:, f, 0:NK], ACT.Sigmoid, scale=SCALE)
                    act.wait_ge(scanned[f], b)
                    act.activation(keep[:, f, :], pz[:, f, 0:NK], ACT.Sigmoid, scale=-SCALE)\
                       .then_inc(z_used[f], 1)
                for f in range(2):
                    act.wait_ge(a_turned[f], b + 1)
                    act.wait_ge(av_done[f], b)
                    act.activation(ath[f][:, 0:KB, :], pt[:, f, 0:KB, :], ACT.Copy).then_inc(at_hi[f], 1)
                    act.activation(ath[f][0:NQ, KB, :], pt[0:NQ, f, KB, :], ACT.Copy).then_inc(at_hi[f], 1)
            act.wait_ge(av_done[1], NB)
            for n in range(4):
                act.activation(o_sb[:, 4 * n:4 * n + 4, :], po[:, 4 * n:4 * n + 4, :], ACT.Copy)\
                   .then_inc(o_read, 1)

        @block.vector
        def _(dve):
            for f in range(2):
                dve.memset(q_pad[f][:, :].bitcast(F32), 0.0).then_inc(zeroed, 1)
                dve.memset(prod[:, f, NK:NK + 1], 1.0).then_inc(zeroed, 1)
            dve.wait_ge(zeroed, 4)
            dve.wait_ge(loaded, 96)
            with dve.Fori(0, NB) as b:
                for f in range(2):
                    dve.wait_ge(z_ready[f], b)
                    dve.tensor_copy(q_pad[f][:, :].rearrange("p (j r) -> p j r", r=P + NQ)[:, :, 0:NQ],
                                    q_all[:, HH * f:HH * (f + 1), bass.ds(b * NQ, NQ)]).then_inc(q_set[f], 1)
                for r in range(NROUND):
                    s, kb, h0 = r % 2, r // (H // 4), (4 * r) % H
                    at = slice(kb * P, (kb + 1) * P)
                    dve.wait_ge(k_hi[s], NROUND // 2 * b + r // 2 + 1)
                    dve.tensor_tensor(ktl[:, h0:h0 + 4, at], pt[:, s, :, :],
                                      kth[:, h0:h0 + 4, at].bitcast(F32), ALU.subtract).then_inc(k_lo[s], 1)
                dve.wait_ge(v_hi, 2 * (b + 1))
                split = lambda ap: ap.rearrange("p kb (h d) -> p (kb h) d", d=HD)
                part = lambda i: v2[:, :, :, i, :].rearrange("p kb h d -> p (kb h) d")
                dve.tensor_tensor(part(1), split(v_in[:, :, :]), part(0).bitcast(F32), ALU.subtract)\
                   .then_inc(v_lo, 1)
                dve.tensor_tensor(vn2[:, :, 1, :], vn_in[:, :].rearrange("p (h d) -> p h d", d=HD),
                                  vn2[:, :, 0, :].bitcast(F32), ALU.subtract).then_inc(v_lo, 1)
                for f in range(2):
                    dve.wait_ge(z_used[f], b + 1)
                    dve.wait_ge(weighted[f], b)
                    dve.tensor_tensor_scan(prod[:, f, 0:NK][:, ::-1], keep[:, f, :][:, ::-1],
                                           keep[:, f, :][:, ::-1], 1.0, ALU.mult, ALU.bypass)\
                       .then_inc(scanned[f], 1)
                    dve.wait_ge(scanned[f], b + 1)
                    dve.tensor_tensor(a[:, f, :], a[:, f, :], prod[:, f, 1:NK + 1], ALU.mult)\
                       .then_inc(weighted[f], 1)
                for f in range(2):
                    dve.wait_ge(at_hi[f], 2 * (b + 1))
                    dve.tensor_tensor(atl[f][:, 0:KB, :], pt[:, f, 0:KB, :], ath[f][:, 0:KB, :].bitcast(F32),
                                      ALU.subtract).then_inc(at_lo[f], 1)
                    dve.tensor_tensor(atl[f][0:NQ, KB, :], pt[0:NQ, f, KB, :],
                                      ath[f][0:NQ, KB, :].bitcast(F32), ALU.subtract).then_inc(at_lo[f], 1)


def build(nc, x_prompt, x_sample, state_conv, cache_k, cache_v, a_norm_pre, a_w_in, a_conv_w, a_w_out,
          a_norm_post, kv_norm, w_k, w_v, b_norm_pre, b_w_in, b_w_out, b_norm_post, ident_in, mask_in,
          mask_s_in, y_prompt, y_sample, conv_p, conv_s, k_prompt, v_prompt, k_sample, v_sample):
    flat = lambda ap: ap.rearrange("b t d -> (b t) d")
    heads = lambda ap: ap.rearrange("b t h d -> (b t) (h d)")
    xp, xsm, yp, ysm = flat(x_prompt), flat(x_sample), flat(y_prompt), flat(y_sample)
    kp, vp, ks, vs = heads(k_prompt), heads(v_prompt), heads(k_sample), heads(v_sample)

    def scratch(name, shape):
        return nc.dram_tensor(name, shape, F32, kind="Internal").ap()

    y_t, qh_t, ql_t, kh_t, kl_t, sz_t, oa_t, ob_t = (
        scratch(n, [D, T]) for n in ("y_t", "qh_t", "ql_t", "kh_t", "kl_t", "sz_t", "oa_t", "ob_t"))
    x1 = scratch("x1", [T, D])

    with ExitStack() as ctx:
        sb, pb, sem, sem2 = make_tools(nc, ctx)
        ident = sb("ident", [P, P])
        mask = sb("mask", [P, P])
        mask_s = sb("mask_s", [P, NQ])
        identr = sb("identr", [P, P], F32R)
        maskr = sb("maskr", [P, P], F32R)
        mask_sr = sb("mask_sr", [P, NQ], F32R)
        loaded, rounded = sem("k_loaded"), sem("k_rounded")
        with nc.Block() as block:
            @block.sync
            def _(sp):
                for dst, src in ((ident, ident_in), (mask, mask_in), (mask_s, mask_s_in)):
                    sp.dma_start(dst[:, :], src).then_inc(loaded, 16)

            @block.vector
            def _(dve):
                dve.wait_ge(loaded, 48)
                for dst, src in ((identr, ident), (maskr, mask), (mask_sr, mask_s)):
                    dve.tensor_copy(dst[:, :], src[:, :]).then_inc(rounded, 1)
                dve.wait_ge(rounded, 3)

        with ExitStack() as act_ctx:
            slab_at = (nc.sbuf_base + 31) // 32 * 32
            act_ctx.enter_context(nc.sbuf_tensor("slab", [P, KT * T], F32))
            at_slab = lambda name, dt: nc.alloc_sbuf_tensor_at(name, [P, KT, T], dt, offset=slab_at)
            with nc.sbuf_tensor("a_xh", [P, KT, T], F32R) as xh:
                xl = at_slab("a_xl", F32R)
                phase_norm_in(nc, xp, xsm, ident, xh, xl)
                phase_conv(nc, a_w_in[0], a_norm_pre[0], a_conv_w[0], state_conv[0].rearrange("b w d -> (b w) d"),
                           ident, xh, xl, y_t, conv_p[0, 0], conv_s[0].rearrange("b w d -> (b w) d"))
            x32 = at_slab("b_x32", F32)
            phase_out(nc, "f_", [y_t], a_w_out[0], a_norm_post[0], xp, xsm, ident,
                      x1[0:SEQ, :], x1[SEQ:T, :], x32)
            phase_qkvz(nc, w_k, w_v, b_w_in[0], kv_norm, b_norm_pre[0], ident, x32, at_slab("b_xl", F32R),
                       qh_t, ql_t, kh_t, kl_t, sz_t, kp, vp, ks, vs)
        phase_attend(nc, qh_t, ql_t, kh_t, kl_t, vp, ident, identr, maskr, oa_t, ob_t)
        phase_attend_sample(nc, qh_t, ql_t, kh_t, kl_t, cache_k.rearrange("b t h d -> b t (h d)"),
                            cache_v.rearrange("b t h d -> b t (h d)"), vs, ident, identr, mask_sr, oa_t, ob_t)
        phase_out(nc, "g_", [oa_t, ob_t, sz_t], b_w_out[0], b_norm_post[0], x1[0:SEQ, :], x1[SEQ:T, :], ident,
                  yp, ysm, None)


_INS = ["x_prompt", "x_sample", "state_conv", "cache_k", "cache_v", "a_norm_pre", "a_w_in", "a_conv_w",
        "a_w_out", "a_norm_post", "kv_norm", "w_k", "w_v", "b_norm_pre", "b_w_in", "b_w_out", "b_norm_post"]
_OUTS = [(1, SEQ, D), (NB, NQ, D), (1, 1, 2, D), (1, NB, 2, D), (1, SEQ, H, HD), (1, SEQ, H, HD),
         (NB, NQ, H, HD), (NB, NQ, H, HD)]


def kernel(**inputs):
    import concourse.bacc as bacc
    from concourse.bass_utils import run_bass_kernel_spmd

    nc = bacc.Bacc("TRN2", target_bir_lowering=False, num_devices=1)
    arrays = {name: np.ascontiguousarray(inputs[name]) for name in _INS}
    arrays["ident"] = np.eye(P, dtype=np.float32)
    arrays["mask"] = np.where(np.arange(P)[None, :] >= np.arange(P)[:, None], MASKED, 0.0).astype(np.float32)
    arrays["mask_s"] = np.where(np.arange(NQ)[None, :] >= np.arange(P)[:, None] % NQ, MASKED, 0.0)\
        .astype(np.float32)
    args = [nc.dram_tensor("in_" + n, a.shape, F32, kind="ExternalInput").ap() for n, a in arrays.items()]
    args += [nc.dram_tensor(f"out_{i}", s, F32, kind="ExternalOutput").ap() for i, s in enumerate(_OUTS)]
    build(nc, *args)
    r = run_bass_kernel_spmd(nc, [{"in_" + n: a for n, a in arrays.items()}], core_ids=[0])
    return tuple(r.results[0][f"out_{i}"] for i in range(len(_OUTS)))
```

```python
import concourse.bass as bass
from concourse import mybir
from contextlib import ExitStack
import numpy as np

F32 = mybir.dt.float32
F32R = mybir.dt.float32r
ALU = mybir.AluOpType
ACT = mybir.ActivationFunctionType

P = 128
D = 1024
KT = D // P
SEQ = 2048
NB, NQ = 8, 16
T = SEQ + NB * NQ
NT = T // P
PAST = 256
H, HD = 16, 64
SCALE = HD ** -0.5
EPS = 1e-6
CW = 3
GROUPS = [(0, 512), (512, 512), (1024, 384), (1408, 384), (1792, 384)]
NG = len(GROUPS)
PAIRS = 7
QT = SEQ // P
QG = 4
NGQ = QT // QG
MASKED = -1e30


def nothing(*_):
    pass


def token_tiles(eng, first, second, third=nothing):
    first(0, 0)
    first(0, 1)
    second(0, 0)
    with eng.Fori(0, PAIRS) as j:
        first(j + 1, 0)
        third(j, 0)
        second(j, 1)
        first(j + 1, 1)
        third(j, 1)
        second(j + 1, 0)
    first(PAIRS + 1, 0)
    third(PAIRS, 0)
    second(PAIRS, 1)
    third(PAIRS, 1)
    second(PAIRS + 1, 0)
    third(PAIRS + 1, 0)


def is_sample(j, s):
    return isinstance(j, int) and 2 * j + s == NT - 1


def apart(eng, passed):
    eng.sem_inc(passed, 1)


def make_tools(nc, ctx):
    def sb(name, shape, dt=F32):
        return ctx.enter_context(nc.sbuf_tensor(name, shape, dt))

    def pb(name, shape):
        return ctx.enter_context(nc.psum_tensor(name, shape, F32))

    sems = []

    def sem(name):
        sems.append(nc.alloc_semaphore(name))
        return sems[-1]

    def give_back():
        nc.clear_and_free_semaphores(sems)
        nc.all_engine_barrier()

    ctx.callback(give_back)

    def sem2(name, n=2):
        return [sem(f"{name}{i}") for i in range(n)]

    return sb, pb, sem, sem2


def phase_norm_in(nc, x_prompt, x_sample, ident, xh, xl):
    with ExitStack() as ctx:
        sb, pb, sem, sem2 = make_tools(nc, ctx)
        x_in = sb("n_x", [P, 2, D])
        xs = sb("n_xs", [P, 2, D])
        junk = sb("n_junk", [P, D])
        ss = sb("n_ss", [P, 2])
        std = sb("n_std", [P, 2])
        rstd = sb("n_rstd", [P, 2])
        epsb = sb("n_eps", [P, 1])
        ps = pb("n_ps", [P, 2, KT, P])
        x_loaded = sem2("n_x_loaded")
        squared, std_ready, rstd_ready = sem2("n_squared"), sem2("n_std"), sem2("n_rstd")
        xs_ready, turned, hi_done, lo_done = sem2("n_xs_ready"), sem2("n_turned"), sem2("n_hi"), sem2("n_lo")
        eps_set = sem("n_eps_set")
        block = ctx.enter_context(nc.Block())

        @block.sync
        def _(sp):
            def load(j, s):
                sp.wait_ge(xs_ready[s], j)
                if is_sample(j, s):
                    src = x_sample
                else:
                    src = x_prompt[bass.ds((2 * j + s) * P, P), :]
                sp.dma_start(x_in[:, s, :], src).then_inc(x_loaded[s], 16)

            token_tiles(sp, load, nothing)

        @block.scalar
        def _(act):
            act.wait_ge(eps_set, 1)

            def sums(j, s):
                act.wait_ge(x_loaded[s], 16 * (j + 1))
                act.wait_ge(rstd_ready[s], j)
                act.activation(junk[:, :], x_in[:, s, :], ACT.Square,
                               accum_out=ss[:, s:s + 1]).then_inc(squared[s], 1)
                act.wait_ge(squared[s], j + 1)
                act.activation(std[:, s:s + 1], ss[:, s:s + 1], ACT.Sqrt, scale=1.0 / D,
                               bias=epsb[:, :]).then_inc(std_ready[s], 1)

            def high(j, s):
                act.wait_ge(turned[s], j + 1)
                act.activation(xh[:, :, bass.ds((2 * j + s) * P, P)], ps[:, s, :, :],
                               ACT.Copy).then_inc(hi_done[s], 1)

            token_tiles(act, sums, high)

        @block.vector
        def _(dve):
            dve.memset(epsb[:, :], EPS).then_inc(eps_set, 1)

            def scale(j, s):
                dve.wait_ge(std_ready[s], j + 1)
                dve.reciprocal(rstd[:, s:s + 1], std[:, s:s + 1]).then_inc(rstd_ready[s], 1)
                dve.wait_ge(rstd_ready[s], j + 1)
                dve.wait_ge(turned[s], j)
                dve.tensor_scalar(xs[:, s, :], x_in[:, s, :], rstd[:, s:s + 1], None,
                                  ALU.mult).then_inc(xs_ready[s], 1)

            def low(j, s):
                at = bass.ds((2 * j + s) * P, P)
                dve.wait_ge(hi_done[s], j + 1)
                dve.tensor_tensor(xl[:, :, at], ps[:, s, :, :], xh[:, :, at].bitcast(F32),
                                  ALU.subtract).then_inc(lo_done[s], 1)

            token_tiles(dve, scale, low)

        @block.tensor
        def _(pe):
            def turn(j, s):
                pe.wait_ge(xs_ready[s], j + 1)
                pe.wait_ge(lo_done[s], j)
                for kt in range(KT):
                    mm = pe.transpose(ps[:, s, kt, :], xs[:, s, kt * P:(kt + 1) * P], ident[:, :])
                mm.then_inc(turned[s], 1)

            token_tiles(pe, turn, nothing)


def weight_stream(pool, n_iter, order, gains, raw, wh, wl, raw_loaded, scaled, hi_ready, w_ready, mm_done, passed):
    pool.wait_ge(*gains)
    with pool.Fori(0, n_iter) as c:
        for m, (view, gain) in enumerate(order):
            s, u = m % 2, c * (len(order) // 2) + m // 2
            gain_b = gain.unsqueeze(2).broadcast_to([P, KT, P])
            pool.wait_ge(w_ready[s], u)
            apart(pool, passed)
            pool.dma_start(raw[:, s, :, :], view(c)).then_inc(raw_loaded[s], 16)
            pool.wait_ge(raw_loaded[s], 16 * (u + 1))
            pool.wait_ge(mm_done[(m - 2) % 4], NG * (c + 1 if m >= 2 else c))
            pool.tensor_tensor(wh[s][:, :, :], raw[:, s, :, :], gain_b, ALU.mult).then_inc(hi_ready[s], 1)
            pool.wait_ge(hi_ready[s], u + 1)
            pool.tensor_tensor(raw[:, s, :, :], raw[:, s, :, :], gain_b, ALU.mult).then_inc(scaled[s], 1)
            pool.wait_ge(scaled[s], u + 1)
            pool.tensor_tensor(wl[s][:, :, :], raw[:, s, :, :], wh[s][:, :, :].bitcast(F32),
                               ALU.subtract).then_inc(w_ready[s], 1)


def project(pe, out, w_h, w_l, x_h, x_l, a, n):
    for kt in range(KT):
        r = slice(a, a + n)
        pe.matmul(out, w_h[:, kt, :], x_h[:, kt, r], start=(kt == 0), stop=False)
        pe.matmul(out, w_h[:, kt, :], x_l[:, kt, r], start=False, stop=False)
        mm = pe.matmul(out, w_l[:, kt, :], x_h[:, kt, r], start=False, stop=(kt == KT - 1))
    return mm


def phase_conv(nc, w_in, a_gain, conv_w, state_conv, ident, xh, xl, y_t, conv_p, conv_s):
    with ExitStack() as ctx:
        sb, pb, sem, sem2 = make_tools(nc, ctx)
        raw = sb("c_raw", [P, 2, KT, P])
        wh = [sb(f"c_wh{s}", [P, KT, P], F32R) for s in range(2)]
        wl = [sb(f"c_wl{s}", [P, KT, P], F32R) for s in range(2)]
        gain = sb("c_gain", [P, KT])
        cw_all = sb("c_cw_all", [P, KT, CW])
        cw = sb("c_cw", [P, CW])
        cg = sb("c_cgate", [P, T])
        u = sb("c_u", [P, 2 + SEQ])
        us = sb("c_us", [P, NB, 2 + NQ])
        t = sb("c_t", [P, T])
        sz = sb("c_sz", [P, T])
        st_rows = sb("c_st_rows", [NB * 2, D])
        st_t = sb("c_st_t", [P, KT, NB * 2])
        edge = sb("c_edge", [P, KT, 2 + NB * 2])
        edge_rows = sb("c_edge_rows", [2 + NB * 2, D])
        pg = [pb(f"c_pg{g}", [P, 512]) for g in range(NG)]
        pm = pb("c_pm", [P, 2, 512])
        raw_loaded, scaled, hi_ready, w_ready = (
            sem2("c_raw_loaded"), sem2("c_scaled"), sem2("c_hi_ready"), sem2("c_w_ready"))
        passed = sem("c_passed")
        consts, st_turned, st_ready, zeroed = sem("c_consts"), sem("c_st_turned"), sem("c_st_ready"), sem("c_zeroed")
        mm_done = [sem(f"c_mm_{n}") for n in "chzb"]
        evac = [sem(f"c_evac_{n}") for n in "chzb"]
        taps, cw_ready, gated, edge_done = sem("c_taps"), sem("c_cw_ready"), sem("c_gated"), sem("c_edge_done")
        prefix = sem("c_prefix")
        y_stored, e_turned, e_rows, e_stored = sem("c_y_stored"), sem("c_e_turned"), sem("c_e_rows"), sem("c_e_stored")
        block = ctx.enter_context(nc.Block())
        C, HH, Z, B = range(4)
        blocks = [1, 2, 3, 0]
        w_v = w_in.rearrange("(kt p) (m c f) -> p kt m c f", p=P, m=4, f=P)
        tail = SEQ - GROUPS[-1][0]

        @block.sync
        def _(sp):
            sp.dma_start(gain[:, :], a_gain.rearrange("(kt p) -> p kt", p=P),
                         allow_slow_non_contiguous=True).then_inc(consts, 16)
            sp.dma_start(st_rows[:, :], state_conv).then_inc(consts, 16)
            for w in range(CW):
                sp.dma_start(cw_all[:, :, w], conv_w[w, :].rearrange("(c p) -> p c", p=P),
                             allow_slow_non_contiguous=True).then_inc(consts, 16)
            with sp.Fori(0, KT) as c:
                sp.wait_ge(evac[B], NG * (c + 2))
                sp.dma_start(y_t[bass.ds(c * P, P), :], sz[:, :]).then_inc(y_stored, 16)
            sp.wait_ge(e_rows, 2)
            sp.dma_start(conv_p, edge_rows[0:2, :]).then_inc(e_stored, 16)
            sp.dma_start(conv_s, edge_rows[2:2 + NB * 2, :]).then_inc(e_stored, 16)
            sp.wait_ge(y_stored, 16 * KT)
            sp.wait_ge(e_stored, 32)

        @block.gpsimd
        def _(pool):
            weight_stream(pool, KT, [(lambda c, b=b: w_v[:, :, b, c, :], gain[:, :]) for b in blocks],
                          (consts, 16 * (2 + CW)), raw, wh, wl, raw_loaded, scaled, hi_ready, w_ready, mm_done, passed)

        @block.tensor
        def _(pe):
            pe.wait_ge(consts, 16 * (2 + CW))
            for c in range(KT):
                mm = pe.transpose(pm[:, 0, c * 16:(c + 1) * 16], st_rows[:, c * P:(c + 1) * P],
                                  ident[0:NB * 2, 0:NB * 2])
            mm.then_inc(st_turned, 1)
            with pe.Fori(0, KT) as c:
                for m in range(4):
                    s = m % 2
                    pe.wait_ge(w_ready[s], 2 * c + m // 2 + 1)
                    for g, (a, n) in enumerate(GROUPS):
                        pe.wait_ge(evac[(m - 1) % 4], NG * c + g + 1)
                        mm = project(pe, pg[g][:, 0:n], wh[s], wl[s], xh, xl, a, n)
                        mm.then_inc(mm_done[m], 1)
            pe.wait_ge(edge_done, 2 * KT)
            for c in range(KT):
                mm = pe.transpose(pm[0:18, c // 4, (c % 4) * P:(c % 4 + 1) * P], edge[:, c, :], ident[:, :])
            mm.then_inc(e_turned, 1)

        @block.scalar
        def _(act):
            act.wait_ge(st_turned, 1)
            act.activation(st_t[:, :, :].rearrange("p a b -> p (a b)"), pm[:, 0, 0:KT * 16],
                           ACT.Copy).then_inc(st_ready, 1)
            with act.Fori(0, KT) as c:
                for g, (a, n) in enumerate(GROUPS):
                    act.wait_ge(mm_done[C], NG * c + g + 1)
                    act.wait_ge(evac[HH], NG * c)
                    act.activation(cg[:, a:a + n], pg[g][:, 0:n], ACT.Copy).then_inc(evac[C], 1)
                act.wait_ge(y_stored, 16 * c)
                for g, (a, n) in enumerate(GROUPS):
                    act.wait_ge(mm_done[Z], NG * c + g + 1)
                    act.activation(sz[:, a:a + n], pg[g][:, 0:n], ACT.Silu).then_inc(evac[Z], 1)
            act.wait_ge(e_turned, 1)
            for half in range(2):
                act.activation(edge_rows[:, half * 512:(half + 1) * 512], pm[0:18, half, :],
                               ACT.Copy).then_inc(e_rows, 1)

        @block.vector
        def _(dve):
            dve.wait_ge(consts, 16 * (2 + CW))
            dve.wait_ge(st_ready, 1)
            dve.memset(u[:, 0:2], 0.0).then_inc(evac[B], NG)
            t_s = t[:, SEQ:T].rearrange("p (b q) -> p b q", q=NQ)
            with dve.Fori(0, KT) as c:
                dve.wait_ge(taps, 5 * c)
                dve.tensor_copy(cw[:, :], cw_all[:, c, :]).then_inc(cw_ready, 1)
                dve.tensor_copy(us[:, :, 0:2], st_t[:, c, :].rearrange("p (b w) -> p b w", w=2))\
                   .then_inc(prefix, 1)
                for g, (a, n) in enumerate(GROUPS):
                    dve.wait_ge(mm_done[HH], NG * c + g + 1)
                    dve.wait_ge(evac[C], NG * c + g + 1)
                    np_ = n if g < NG - 1 else tail
                    op = dve.tensor_tensor(u[:, 2 + a:2 + a + np_], pg[g][:, 0:np_], cg[:, a:a + np_], ALU.mult)
                    if g == NG - 1:
                        op = dve.tensor_tensor(
                            us[:, :, 2:2 + NQ], pg[g][:, np_:n].rearrange("p (b q) -> p b q", q=NQ),
                            cg[:, SEQ:T].rearrange("p (b q) -> p b q", q=NQ), ALU.mult)
                    op.then_inc(evac[HH], 1)
                dve.wait_ge(evac[HH], NG * (c + 1))
                dve.wait_ge(cw_ready, c + 1)
                dve.wait_ge(prefix, c + 1)
                dve.wait_ge(evac[B], NG * (c + 1))
                dve.tensor_copy(edge[:, c, 0:2], u[:, SEQ:SEQ + 2]).then_inc(edge_done, 1)
                dve.tensor_copy(edge[:, c, 2:18].rearrange("p (b w) -> p b w", w=2),
                                us[:, :, NQ:NQ + 2]).then_inc(edge_done, 1)
                dve.tensor_scalar(t[:, 0:SEQ], u[:, 0:SEQ], cw[:, 0:1], None, ALU.mult).then_inc(taps, 1)
                dve.tensor_scalar(t_s, us[:, :, 0:NQ], cw[:, 0:1], None, ALU.mult).then_inc(taps, 1)
                dve.wait_ge(taps, 5 * c + 2)
                dve.scalar_tensor_tensor(t[:, 0:SEQ], u[:, 1:1 + SEQ], cw[:, 1:2], t[:, 0:SEQ],
                                         ALU.mult, ALU.add).then_inc(taps, 1)
                dve.scalar_tensor_tensor(t_s, us[:, :, 1:1 + NQ], cw[:, 1:2], t_s, ALU.mult, ALU.add)\
                   .then_inc(taps, 1)
                dve.wait_ge(taps, 5 * c + 4)
                dve.scalar_tensor_tensor(t[:, 0:SEQ], u[:, 2:2 + SEQ], cw[:, 2:3], t[:, 0:SEQ],
                                         ALU.mult, ALU.add)
                dve.scalar_tensor_tensor(t_s, us[:, :, 2:2 + NQ], cw[:, 2:3], t_s, ALU.mult, ALU.add)\
                   .then_inc(taps, 1)
                dve.wait_ge(taps, 5 * c + 5)
                for g, (a, n) in enumerate(GROUPS):
                    dve.wait_ge(evac[Z], NG * c + g + 1)
                    dve.tensor_tensor(t[:, a:a + n], t[:, a:a + n], sz[:, a:a + n], ALU.mult)\
                       .then_inc(gated, 1)
                for g, (a, n) in enumerate(GROUPS):
                    dve.wait_ge(mm_done[B], NG * c + g + 1)
                    dve.wait_ge(gated, NG * c + g + 1)
                    dve.tensor_tensor(sz[:, a:a + n], pg[g][:, 0:n], t[:, a:a + n], ALU.mult)\
                       .then_inc(evac[B], 1)


def phase_out(nc, tag, parts, w_out, post_gain, x_prompt, x_sample, ident, out_prompt, out_sample, x32):
    with ExitStack() as ctx:
        sb, pb, sem, sem2 = make_tools(nc, ctx)
        n_in = len(parts)
        raw = sb(tag + "raw", [P, 2, D])
        wh = sb(tag + "wh", [P, KT, D], F32R)
        wl = sb(tag + "wl", [P, KT, D], F32R)
        gain = sb(tag + "gain", [P, D])
        y_in = sb(tag + "y_in", [P, 2, n_in, KT, P])
        yh = [sb(f"{tag}yh{s}", [P, KT, P], F32R) for s in range(2)]
        yl = [sb(f"{tag}yl{s}", [P, KT, P], F32R) for s in range(2)]
        x_in = sb(tag + "x", [P, 2, D])
        xn = sb(tag + "xn", [P, 2, D])
        xs = sb(tag + "xs", [P, D])
        junk = sb(tag + "junk", [P, D])
        ss = sb(tag + "ss", [P, 2, 2])
        std = sb(tag + "std", [P, 2, 2])
        rstd = sb(tag + "rstd", [P, 2, 2])
        epsb = sb(tag + "eps", [P, 1])
        ph = pb(tag + "ph", [P, 2, D])
        pt = pb(tag + "pt", [P, 2, KT, P])
        w_loaded, w_hi, w_lo = sem2(tag + "w_loaded"), sem(tag + "w_hi"), sem(tag + "w_lo")
        consts, passed = sem(tag + "consts"), sem(tag + "passed")
        y_loaded, y_sum, y_whole, y_hi, y_lo = (sem2(tag + "y_loaded"), sem2(tag + "y_sum"), sem2(tag + "y_whole"),
                                                sem2(tag + "y_hi"), sem2(tag + "y_lo"))
        x_loaded, mm_done = sem2(tag + "x_loaded"), sem2(tag + "mm_done")
        squared, std_ready, rstd_ready = sem2(tag + "squared"), sem2(tag + "std_ready"), sem2(tag + "rstd_ready")
        normed, summed, stored = sem2(tag + "normed"), sem2(tag + "summed"), sem2(tag + "stored")
        scaled, turned, kept = sem(tag + "scaled"), sem2(tag + "turned"), sem2(tag + "kept")
        block = ctx.enter_context(nc.Block())
        w_v = w_out.rearrange("(kt p) n -> p kt n", p=P)
        views = [a.rearrange("(kt p) t -> p kt t", p=P) for a in parts]
        norms = 2 if x32 is not None else 1

        @block.sync
        def _(sp):
            sp.dma_start(gain[:, :], post_gain.partition_broadcast(P)).then_inc(consts, 16)
            for kt in range(KT):
                if kt >= 2:
                    sp.wait_ge(w_lo, kt - 1)
                sp.dma_start(raw[:, kt % 2, :], w_v[:, kt, :]).then_inc(w_loaded[kt % 2], 16)

            def load(j, s):
                at = bass.ds((2 * j + s) * P, P)
                sp.wait_ge(y_lo[s], j)
                for i, v in enumerate(views):
                    sp.dma_start(y_in[:, s, i, :, :], v[:, :, at]).then_inc(y_loaded[s], 16)
                sp.wait_ge(summed[s], j)
                src = x_sample if is_sample(j, s) else x_prompt[bass.ds((2 * j + s) * P, P), :]
                sp.dma_start(x_in[:, s, :], src).then_inc(x_loaded[s], 16)

            token_tiles(sp, load, nothing)

        @block.gpsimd
        def _(pool):
            def store(j, s):
                pool.wait_ge(summed[s], j + 1)
                apart(pool, passed)
                dst = out_sample if is_sample(j, s) else out_prompt[bass.ds((2 * j + s) * P, P), :]
                pool.dma_start(dst, xn[:, s, :]).then_inc(stored[s], 16)

            token_tiles(pool, nothing, store)
            pool.wait_ge(stored[0], 16 * (NT // 2 + 1))
            pool.wait_ge(stored[1], 16 * (NT // 2))

        @block.scalar
        def _(act):
            for kt in range(KT):
                act.wait_ge(w_loaded[kt % 2], 16 * (kt // 2 + 1))
                act.activation(wh[:, kt, :], raw[:, kt % 2, :], ACT.Copy).then_inc(w_hi, 1)

            def split(j, s):
                if n_in == 1:
                    act.wait_ge(y_loaded[s], 16 * (j + 1))
                else:
                    act.wait_ge(y_whole[s], j + 1)
                act.wait_ge(mm_done[s], j)
                act.activation(yh[s][:, :, :], y_in[:, s, 0, :, :], ACT.Copy).then_inc(y_hi[s], 1)

            def rms(src, j, s, k):
                act.wait_ge(rstd_ready[s], norms * j + k)
                act.activation(junk[:, :], src, ACT.Square, accum_out=ss[:, s, k:k + 1]).then_inc(squared[s], 1)
                act.wait_ge(squared[s], norms * j + k + 1)
                act.activation(std[:, s, k:k + 1], ss[:, s, k:k + 1], ACT.Sqrt, scale=1.0 / D,
                               bias=epsb[:, :]).then_inc(std_ready[s], 1)

            def tail(j, s):
                act.wait_ge(mm_done[s], j + 1)
                rms(ph[:, s, :], j, s, 0)
                if x32 is not None:
                    act.wait_ge(summed[s], j + 1)
                    rms(xn[:, s, :], j, s, 1)

            def keep(j, s):
                if x32 is not None:
                    act.wait_ge(turned[s], j + 1)
                    act.activation(x32[:, :, bass.ds((2 * j + s) * P, P)], pt[:, s, :, :],
                                   ACT.Copy).then_inc(kept[s], 1)

            act.wait_ge(consts, 17)
            token_tiles(act, split, tail, keep)

        @block.vector
        def _(dve):
            dve.memset(epsb[:, :], EPS).then_inc(consts, 1)
            for kt in range(KT):
                dve.wait_ge(w_hi, kt + 1)
                dve.tensor_tensor(wl[:, kt, :], raw[:, kt % 2, :], wh[:, kt, :].bitcast(F32),
                                  ALU.subtract).then_inc(w_lo, 1)

            def split(j, s):
                y = y_in[:, s, 0, :, :]
                if n_in == 3:
                    dve.wait_ge(y_loaded[s], 16 * n_in * (j + 1))
                    dve.tensor_tensor(y, y, y_in[:, s, 1, :, :], ALU.add).then_inc(y_sum[s], 1)
                    dve.wait_ge(y_sum[s], j + 1)
                    dve.tensor_tensor(y, y, y_in[:, s, 2, :, :], ALU.mult).then_inc(y_whole[s], 1)
                dve.wait_ge(y_hi[s], j + 1)
                dve.tensor_tensor(yl[s][:, :, :], y, yh[s][:, :, :].bitcast(F32),
                                  ALU.subtract).then_inc(y_lo[s], 1)

            def inverse(j, s, k):
                dve.wait_ge(std_ready[s], norms * j + k + 1)
                dve.reciprocal(rstd[:, s, k:k + 1], std[:, s, k:k + 1]).then_inc(rstd_ready[s], 1)
                dve.wait_ge(rstd_ready[s], norms * j + k + 1)

            def tail(j, s):
                inverse(j, s, 0)
                dve.wait_ge(stored[s], 16 * j)
                dve.scalar_tensor_tensor(xn[:, s, :], ph[:, s, :], rstd[:, s, 0:1], gain[:, :],
                                         ALU.mult, ALU.mult).then_inc(normed[s], 1)
                dve.wait_ge(normed[s], j + 1)
                dve.wait_ge(x_loaded[s], 16 * (j + 1))
                dve.tensor_tensor(xn[:, s, :], xn[:, s, :], x_in[:, s, :], ALU.add).then_inc(summed[s], 1)
                if x32 is not None:
                    inverse(j, s, 1)
                    dve.wait_ge(turned[1 - s], j + s)
                    dve.tensor_scalar(xs[:, :], xn[:, s, :], rstd[:, s, 1:2], None, ALU.mult).then_inc(scaled, 1)

            dve.wait_ge(consts, 17)
            token_tiles(dve, split, tail)

        @block.tensor
        def _(pe):
            pe.wait_ge(w_lo, KT)

            def multiply(j, s):
                pe.wait_ge(y_lo[s], j + 1)
                pe.wait_ge(normed[s], j)
                for n in range(2):
                    r = slice(n * 512, (n + 1) * 512)
                    for kt in range(KT):
                        o = ph[:, s, r]
                        pe.matmul(o, yh[s][:, kt, :], wh[:, kt, r], start=(kt == 0), stop=False)
                        pe.matmul(o, yh[s][:, kt, :], wl[:, kt, r], start=False, stop=False)
                        mm = pe.matmul(o, yl[s][:, kt, :], wh[:, kt, r], start=False, stop=(kt == KT - 1))
                mm.then_inc(mm_done[s], 1)

            def turn(j, s):
                if x32 is not None:
                    pe.wait_ge(scaled, 2 * j + s + 1)
                    pe.wait_ge(kept[s], j)
                    for kt in range(KT):
                        mm = pe.transpose(pt[:, s, kt, :], xs[:, kt * P:(kt + 1) * P], ident[:, :])
                    mm.then_inc(turned[s], 1)

            token_tiles(pe, multiply, turn)


def phase_qkvz(nc, w_k, w_v, w_qz, kv_gain, b_gain, ident, x32, xl, qh_t, ql_t, kh_t, kl_t, sz_t,
               k_prompt, v_prompt, k_sample, v_sample):
    with ExitStack() as ctx:
        sb, pb, sem, sem2 = make_tools(nc, ctx)
        xh = sb("q_xh", [P, KT, T], F32R)
        raw = sb("q_raw", [P, 2, KT, P])
        wh = [sb(f"q_wh{s}", [P, KT, P], F32R) for s in range(2)]
        wl = [sb(f"q_wl{s}", [P, KT, P], F32R) for s in range(2)]
        g_kv = sb("q_g_kv", [P, KT])
        g_b = sb("q_g_b", [P, KT])
        hi = sb("q_hi", [P, 2, 512], F32R)
        lo = sb("q_lo", [P, 2, 512], F32R)
        full = sb("q_full", [P, 2, 512])
        gate = sb("q_gate", [P, 2, 512])
        rows = sb("q_rows", [P, 2, 4, P])
        pg = [pb(f"q_pg{g}", [P, 512]) for g in range(NG)]
        pt = pb("q_pt", [P, 2, 4, P])
        raw_loaded, scaled, hi_ready, w_ready = (
            sem2("q_raw_loaded"), sem2("q_scaled"), sem2("q_hi_ready"), sem2("q_w_ready"))
        passed, passed_sp = sem("q_passed"), sem("q_passed_sp")
        consts, x_hi, x_lo = sem("q_consts"), sem("q_x_hi"), sem("q_x_lo")
        mm_done = [sem(f"q_mm_{n}") for n in "kvqz"]
        high, low, hl_stored = sem2("q_high"), sem2("q_low"), sem2("q_hl_stored")
        whole, turned, rowed, rows_stored = sem2("q_whole"), sem2("q_turned"), sem2("q_rowed"), sem2("q_rows_stored")
        gated, gate_stored = sem("q_gated"), sem2("q_gate_stored")
        block = ctx.enter_context(nc.Block())
        K, V, Q, Z = range(4)
        k_v = w_k.rearrange("(kt p) (c f) -> p kt c f", p=P, f=P)
        v_v = w_v.rearrange("(kt p) (c f) -> p kt c f", p=P, f=P)
        qz_v = w_qz.rearrange("(kt p) (m c f) -> p kt m c f", p=P, m=2, f=P)
        def uses(kinds, m, g):
            n = [(mm, gg) for mm in kinds for gg in range(NG)]
            s = (NG * m + g) % 2
            same = [x for x in n if (NG * x[0] + x[1]) % 2 == s]
            return s, len(same), same.index((m, g))

        @block.sync
        def _(sp):
            for tile, src in ((g_kv, kv_gain), (g_b, b_gain)):
                sp.dma_start(tile[:, :], src.rearrange("(kt p) -> p kt", p=P),
                             allow_slow_non_contiguous=True).then_inc(consts, 16)

            def rows_out(c, m, g):
                a, n = GROUPS[g]
                s, per, k = uses((K, V), m, g)
                sp.wait_ge(rowed[s], per * c + k + 1)
                apart(sp, passed_sp)
                out_p, out_s = ((k_prompt, k_sample), (v_prompt, v_sample))[m]
                nt, np_ = n // P, (min(a + n, SEQ) - a) // P
                cols = bass.ds(c * P, P)
                sp.dma_start(out_p[a:a + np_ * P, cols].rearrange("(i p) f -> p i f", p=P),
                             rows[:, s, 0:np_, :]).then_inc(rows_stored[s], 16)
                if np_ < nt:
                    sp.dma_start(out_s[:, cols], rows[:, s, np_, :]).then_inc(rows_stored[s], 16)
                else:
                    sp.sem_inc(rows_stored[s], 16)

            with sp.Fori(0, KT) as c:
                at = bass.ds(c * P, P)
                for m in (K, V, Q, Z):
                    for g, (a, n) in enumerate(GROUPS):
                        if m in (K, Q):
                            s, per, k = uses((K, Q), m, g)
                            for part, done, dst in ((hi, high, (kh_t, qh_t)), (lo, low, (kl_t, ql_t))):
                                sp.wait_ge(done[s], per * c + k + 1)
                                sp.dma_start(dst[m == Q][at, a:a + n], part[:, s, 0:n].bitcast(F32))\
                                  .then_inc(hl_stored[s], 16)
                        if m == Z:
                            s, per, k = uses((Z,), m, g)
                            sp.wait_ge(gated, NG * (c + 1) + g + 1)
                            sp.dma_start(sz_t[at, a:a + n], gate[:, s, 0:n]).then_inc(gate_stored[s], 16)
                        if m in (K, V) and g >= 1:
                            rows_out(c, m, g - 1)
                        if m in (V, Q) and g == 0:
                            rows_out(c, m - 1, NG - 1)
            for s in range(2):
                sp.wait_ge(hl_stored[s], 32 * uses((K, Q), 0, s)[1] * KT)
                sp.wait_ge(gate_stored[s], 16 * uses((Z,), Z, 1 - s)[1] * KT)
                sp.wait_ge(rows_stored[s], 32 * uses((K, V), 0, s)[1] * KT)

        @block.gpsimd
        def _(pool):
            order = [(lambda c: k_v[:, :, c, :], g_kv[:, :]), (lambda c: v_v[:, :, c, :], g_kv[:, :]),
                     (lambda c: qz_v[:, :, 0, c, :], g_b[:, :]), (lambda c: qz_v[:, :, 1, c, :], g_b[:, :])]
            weight_stream(pool, KT, order, (consts, 32), raw, wh, wl, raw_loaded, scaled, hi_ready, w_ready, mm_done, passed)

        @block.tensor
        def _(pe):
            pe.wait_ge(x_lo, NG)

            def turn(c, m, g):
                s, per, k = uses((K, V), m, g)
                pe.wait_ge(whole[s], per * c + k + 1)
                pe.wait_ge(rowed[s], per * c + k)
                for i in range(GROUPS[g][1] // P):
                    mm = pe.transpose(pt[:, s, i, :], full[:, s, i * P:(i + 1) * P], ident[:, :])
                mm.then_inc(turned[s], 1)

            def bank_read(c, m, g):
                if m == K:
                    pe.wait_ge(gated, NG * c + g + 1)
                else:
                    kinds, done = ((K, Q), low) if m - 1 in (K, Q) else ((K, V), whole)
                    s, per, k = uses(kinds, m - 1, g)
                    pe.wait_ge(done[s], per * c + k + 1)

            with pe.Fori(0, KT) as c:
                for m in range(4):
                    s = m % 2
                    pe.wait_ge(w_ready[s], 2 * c + m // 2 + 1)
                    for g, (a, n) in enumerate(GROUPS):
                        bank_read(c, m, g)
                        mm = project(pe, pg[g][:, 0:n], wh[s], wl[s], xh, xl, a, n)
                        mm.then_inc(mm_done[m], 1)
                        if m in (K, V) and g >= 1:
                            turn(c, m, g - 1)
                        if m in (V, Q) and g == 0:
                            turn(c, m - 1, NG - 1)

        def rows_copy(act, c, m, g):
            s, per, k = uses((K, V), m, g)
            nt = GROUPS[g][1] // P
            act.wait_ge(turned[s], per * c + k + 1)
            act.wait_ge(rows_stored[s], 32 * (per * c + k))
            act.activation(rows[:, s, 0:nt, :], pt[:, s, 0:nt, :], ACT.Copy).then_inc(rowed[s], 1)

        @block.scalar
        def _(act):
            for g, (a, n) in enumerate(GROUPS):
                act.activation(xh[:, :, a:a + n], x32[:, :, a:a + n], ACT.Copy).then_inc(x_hi, 1)
            with act.Fori(0, KT) as c:
                for m in range(4):
                    for g, (a, n) in enumerate(GROUPS):
                        act.wait_ge(mm_done[m], NG * c + g + 1)
                        if m in (K, V):
                            s, per, k = uses((K, V), m, g)
                            act.wait_ge(turned[s], per * c + k)
                            act.activation(full[:, s, 0:n], pg[g][:, 0:n], ACT.Copy).then_inc(whole[s], 1)
                        if m == Q:
                            s, per, k = uses((K, Q), m, g)
                            act.wait_ge(hl_stored[s], 32 * (per * c + k))
                            act.activation(hi[:, s, 0:n], pg[g][:, 0:n], ACT.Copy).then_inc(high[s], 1)
                        if m == Z:
                            s, per, k = uses((Z,), m, g)
                            act.wait_ge(gate_stored[s], 16 * (per * c + k))
                            act.activation(gate[:, s, 0:n], pg[g][:, 0:n], ACT.Silu).then_inc(gated, 1)
                        if m in (K, V) and g >= 1:
                            rows_copy(act, c, m, g - 1)
                        if m in (V, Q) and g == 0:
                            rows_copy(act, c, m - 1, NG - 1)

        @block.vector
        def _(dve):
            for g, (a, n) in enumerate(GROUPS):
                dve.wait_ge(x_hi, g + 1)
                dve.tensor_tensor(xl[:, :, a:a + n], x32[:, :, a:a + n], xh[:, :, a:a + n].bitcast(F32),
                                  ALU.subtract).then_inc(x_lo, 1)
            dve.sem_inc(gated, NG)
            with dve.Fori(0, KT) as c:
                for m in (K, Q):
                    for g, (a, n) in enumerate(GROUPS):
                        s, per, k = uses((K, Q), m, g)
                        if m == K:
                            ws, wper, wk = uses((K, V), m, g)
                            dve.wait_ge(whole[ws], wper * c + wk + 1)
                            dve.wait_ge(hl_stored[s], 32 * (per * c + k))
                            dve.tensor_copy(hi[:, s, 0:n], pg[g][:, 0:n]).then_inc(high[s], 1)
                        dve.wait_ge(high[s], per * c + k + 1)
                        dve.wait_ge(hl_stored[s], 32 * (per * c + k))
                        dve.tensor_tensor(lo[:, s, 0:n], pg[g][:, 0:n], hi[:, s, 0:n].bitcast(F32),
                                          ALU.subtract).then_inc(low[s], 1)


Z_W = 1024
ORDER = list(reversed(range(NGQ)))
PIECES = [(i, p, min(p + Z_W, (i + 1) * P)) for g in ORDER for i in range(QG * g, QG * (g + 1))
          for p in reversed(range(0, (i + 1) * P, Z_W))]
BLOCKS = [(g, kb) for g in ORDER for kb in range(QG * (g + 1))]
N_PIECE, N_BLOCK = len(PIECES), len(BLOCKS)
POOL_TILES = (0, 1, 2)


def piece_uses(n):
    return sum(PIECES[m][0] % 2 == PIECES[n][0] % 2 for m in range(n))


def tile_uses(i):
    last = max(n for n, x in enumerate(PIECES) if x[0] == i)
    return piece_uses(last) + 1


LEAD = 10000
ON_PE, ON_ACT, ON_DVE = -1, 0, 1


def cycle(behind):
    starts = [sum(p1 - p0 for _, p0, p1 in PIECES[:n]) for n in range(N_PIECE + 1)]
    total = starts[-1]
    items = [(b * total / N_BLOCK, "value", b, 0) for b in range(N_BLOCK)]
    for n in range(N_PIECE):
        turn, k = divmod(n + behind, N_PIECE)
        at = starts[k] + total * turn - LEAD
        items.append((at + total * (at < 0), "score", n, int(at < 0)))
    return [x[1:] for x in sorted(items)]


def phase_attend(nc, qh_t, ql_t, kh_t, kl_t, v_prompt, ident, identr, maskr, oa_t, ob_t):
    with ExitStack() as ctx:
        sb, pb, sem, sem2 = make_tools(nc, ctx)
        q2 = [sb(f"a_q{s}", [P, SEQ], F32R) for s in range(2)]
        kh2 = [sb(f"a_kh{s}", [P, SEQ], F32R) for s in range(2)]
        kl2 = [sb(f"a_kl{s}", [P, SEQ], F32R) for s in range(2)]
        v_in = sb("a_v_in", [P, 2, QT, HD])
        v2 = [sb(f"a_v{s}", [P, QT, 2, HD], F32R) for s in range(2)]
        a = [sb(f"a_a{g}", [P, QG, QG * P * (g + 1)]) for g in range(NGQ)]
        keep = sb("a_keep", [P, 2, SEQ])
        prod = sb("a_prod", [P, 2, SEQ + 1])
        ath = [sb(f"a_ath{s}", [P, QG * P], F32R) for s in range(4)]
        atl = [sb(f"a_atl{s}", [P, QG * P], F32R) for s in range(4)]
        o_sb = sb("a_o", [P, 2, QG * P])
        pz = pb("a_pz", [P, 2, Z_W])
        pt = pb("a_pt", [P, 2, QG * P])
        po = pb("a_po", [P, 2, QG * P])
        passed, passed_sp = sem("a_passed"), sem("a_passed_sp")
        qk_loaded, v_loaded = sem2("a_qk_loaded"), sem2("a_v_loaded")
        v_hi, v_ready = sem2("a_v_hi"), sem2("a_v_ready")
        z_ready, z_used = sem2("a_z_ready"), sem2("a_z_used")
        scanned, weighted, one_set = sem2("a_scanned"), sem2("a_weighted"), sem("a_one_set")
        t_ready, at_hi, at_ready, av_done = (sem2("a_t_ready"), sem2("a_at_hi", 4), sem2("a_at_ready", 4),
                                             sem2("a_av_done", 4))
        o_read, o_stored = sem2("a_o_read"), sem2("a_o_stored")
        block = ctx.enter_context(nc.Block())
        NPAIR = H // 2
        group_end = [BLOCKS.index((g, QG * (g + 1) - 1)) // 4 + 1 for g in range(NGQ)]
        per_z, per_i, per_at = N_PIECE // 2, N_PIECE // 2, N_BLOCK // 4

        ENDS = {BLOCKS.index((g, QG * (g + 1) - 1)): g for g in range(1, NGQ)}

        def group_uses(pr, hh, g):
            return (2 * pr + hh) * (NGQ // 2) + ORDER.index(g) // 2

        def all_heads(eng, behind, score, value=nothing, tail=nothing):
            def pair(pr, last):
                for hh in range(2):
                    for what, n, ahead in cycle(behind):
                        if what == "value":
                            value(pr, hh, n)
                            if n - 3 in ENDS:
                                tail(pr, hh, ENDS[n - 3])
                            if n == 2 and hh == 1:
                                tail(pr, 0, 0)
                        elif not ahead:
                            score(pr, hh, n)
                        elif hh == 0:
                            score(pr, 1, n)
                        elif not last:
                            score(pr + 1, 0, n)
                tail(pr, 1, 0)

            for what, n, ahead in cycle(behind):
                if ahead:
                    score(0, 0, n)
            with eng.Fori(0, NPAIR - 1) as pr:
                pair(pr, False)
            pair(NPAIR - 1, True)

        @block.sync
        def _(sp):
            def load(pr, hh):
                rows = bass.ds((2 * pr + hh) * HD, HD)
                for dst, top, bottom in ((q2, qh_t, ql_t), (kh2, kh_t, kh_t), (kl2, kl_t, kl_t)):
                    sp.dma_start(dst[hh][0:HD, :].bitcast(F32), top[rows, 0:SEQ]).then_inc(qk_loaded[hh], 16)
                    sp.dma_start(dst[hh][HD:P, :].bitcast(F32), bottom[rows, 0:SEQ]).then_inc(qk_loaded[hh], 16)

            def load_v(pr, hh):
                cols = bass.ds((2 * pr + hh) * HD, HD)
                sp.dma_start(v_in[:, hh, :, :], v_prompt[:, cols].rearrange("(b p) d -> p b d", p=P))\
                  .then_inc(v_loaded[hh], 16)

            def pair(pr, last):
                for hh in range(2):
                    for g in ORDER:
                        sp.wait_ge(o_read[g % 2], group_uses(pr, hh, g) + 1)
                        apart(sp, passed_sp)
                        rows, at = bass.ds((2 * pr + hh) * HD, HD), slice(g * QG * P, (g + 1) * QG * P)
                        sp.dma_start(oa_t[rows, at], o_sb[0:HD, g % 2, :]).then_inc(o_stored[g % 2], 16)
                        sp.dma_start(ob_t[rows, at], o_sb[HD:P, g % 2, :]).then_inc(o_stored[g % 2], 16)
                        if g == NGQ - 1 and not last:
                            sp.wait_ge(z_ready[1], per_z * (2 * pr + hh + 1))
                            load(pr + 1, hh)
                            sp.wait_ge(v_ready[hh], pr + 1)
                            apart(sp, passed_sp)
                            load_v(pr + 1, hh)

            for hh in range(2):
                load(0, hh)
                load_v(0, hh)
            with sp.Fori(0, NPAIR - 1) as pr:
                pair(pr, False)
            pair(NPAIR - 1, True)
            for s in range(2):
                sp.wait_ge(o_stored[s], 32 * H * NGQ // 2)

        @block.tensor
        def _(pe):
            def score(pr, hh, n):
                i, p0, p1 = PIECES[n]
                if n == 0:
                    pe.wait_ge(qk_loaded[hh], 96 * (pr + 1))
                s = n % 2
                pe.wait_ge(z_used[s], (2 * pr + hh) * per_z + n // 2)
                for r0 in range(p0, p1, 512):
                    r1 = min(r0 + 512, p1)
                    o = pz[:, s, r0 - p0:r1 - p0]
                    lhs = q2[hh][:, i * P:(i + 1) * P]
                    pe.matmul(o, lhs, kh2[hh][:, r0:r1], start=True, stop=False)
                    if r1 == (i + 1) * P:
                        pe.matmul(pz[:, s, r1 - P - p0:r1 - p0], identr[:, :], maskr[:, :],
                                  start=False, stop=False)
                    mm = pe.matmul(o, lhs, kl2[hh][:, r0:r1], start=False, stop=True)
                mm.then_inc(z_ready[s], 1)

            def multiply(pr, hh, b):
                g, kb = BLOCKS[b]
                c0, s = max(0, kb - QG * g) * P, b % 4
                if kb == 0:
                    pe.wait_ge(o_read[g % 2], group_uses(pr, hh, g))
                pe.wait_ge(at_ready[s], (2 * pr + hh) * per_at + b // 4 + 1)
                o = po[:, g % 2, c0:QG * P]
                last = kb == QG * (g + 1) - 1
                pe.matmul(o, v2[hh][:, kb, :, :], ath[s][:, c0:], start=(kb == 0), stop=False,
                          skip_group_check=True)
                pe.matmul(o, v2[hh][:, kb, :, :], atl[s][:, c0:], start=False, stop=last,
                          skip_group_check=True).then_inc(av_done[s], 1)

            def value(pr, hh, b):
                g, kb = BLOCKS[b]
                if b == 0:
                    pe.wait_ge(v_ready[hh], pr + 1)
                if kb == 0:
                    for i in (QG * g + 2, QG * g + 3):
                        pe.wait_ge(weighted[i % 2], (2 * pr + hh) * per_i + tile_uses(i))
                pe.wait_ge(at_ready[(b - 2) % 4], (2 * pr + hh) * per_at + (b - 2) // 4 + 1)
                for i in range(max(kb, QG * g), QG * (g + 1)):
                    q = i - QG * g
                    mm = pe.transpose(pt[:, b % 2, q * P:(q + 1) * P], a[g][:, q, kb * P:(kb + 1) * P],
                                      ident[:, :])
                mm.then_inc(t_ready[b % 2], 1)
                if b >= 2:
                    multiply(pr, hh, b - 2)
                elif hh == 1:
                    multiply(pr, 0, N_BLOCK + b - 2)

            def tail(pr, hh, g):
                if (hh, g) == (1, 0):
                    multiply(pr, hh, N_BLOCK - 2)
                    multiply(pr, hh, N_BLOCK - 1)

            all_heads(pe, ON_PE, score, value, tail)

        @block.scalar
        def _(act):
            def score(pr, hh, n):
                i, p0, p1 = PIECES[n]
                s, g = n % 2, i // QG
                if p1 == (i + 1) * P:
                    if ("score", n, 1) in cycle(ON_ACT) and not (isinstance(pr, int) and pr == 0 and hh == 0):
                        act.wait_ge(av_done[3], (2 * pr + hh - 1) * per_at + group_end[g])
                    act.wait_ge(scanned[i % 2], (2 * pr + hh) * per_i + piece_uses(n))
                act.wait_ge(z_ready[s], (2 * pr + hh) * per_z + n // 2 + 1)
                act.activation(a[g][:, i % QG, p0:p1], pz[:, s, 0:p1 - p0], ACT.Sigmoid, scale=SCALE)
                act.activation(keep[:, i % 2, p0:p1], pz[:, s, 0:p1 - p0], ACT.Sigmoid,
                               scale=-SCALE).then_inc(z_used[s], 1)

            def value(pr, hh, b):
                g, kb = BLOCKS[b]
                c0, s = max(0, kb - QG * g) * P, b % 4
                act.wait_ge(t_ready[b % 2], (2 * pr + hh) * (N_BLOCK // 2) + b // 2 + 1)
                act.wait_ge(av_done[s], (2 * pr + hh) * per_at + b // 4)
                act.activation(ath[s][:, c0:], pt[:, b % 2, c0:], ACT.Copy).then_inc(at_hi[s], 1)

            def tail(pr, hh, g):
                act.wait_ge(av_done[3], (2 * pr + hh) * per_at + group_end[g])
                act.wait_ge(o_stored[g % 2], 32 * (group_uses(pr, hh, g)))
                act.activation(o_sb[:, g % 2, :], po[:, g % 2, :], ACT.Copy).then_inc(o_read[g % 2], 1)

            all_heads(act, ON_ACT, score, value, tail)

        def weight(eng, pr, hh, n):
            i, p0, p1 = PIECES[n]
            s, at = i % 2, SEQ - (i + 1) * P
            piece = a[i // QG][:, i % QG, p0:p1]
            eng.wait_ge(scanned[s], (2 * pr + hh) * per_i + piece_uses(n) + 1)
            eng.tensor_tensor(piece, piece, prod[:, s, at + p0 + 1:at + p1 + 1], ALU.mult).then_inc(weighted[s], 1)

        @block.vector
        def _(dve):
            def score(pr, hh, n):
                i, p0, p1 = PIECES[n]
                s, at = i % 2, SEQ - (i + 1) * P
                dve.wait_ge(z_used[n % 2], (2 * pr + hh) * per_z + n // 2 + 1)
                if p1 == (i + 1) * P:
                    dve.wait_ge(weighted[s], (2 * pr + hh) * per_i + piece_uses(n))
                    start = 1.0
                else:
                    dve.wait_ge(scanned[s], (2 * pr + hh) * per_i + piece_uses(n))
                    start = prod[:, s, at + p1:at + p1 + 1]
                back = keep[:, s, p0:p1][:, ::-1]
                dve.tensor_tensor_scan(prod[:, s, at + p0:at + p1][:, ::-1], back, back, start,
                                       ALU.mult, ALU.bypass).then_inc(scanned[s], 1)
                if i % QG not in POOL_TILES:
                    weight(dve, pr, hh, n)

            def value(pr, hh, b):
                g, kb = BLOCKS[b]
                c0, s = max(0, kb - QG * g) * P, b % 4
                dve.wait_ge(at_hi[s], (2 * pr + hh) * per_at + b // 4 + 1)
                dve.tensor_tensor(atl[s][:, c0:], pt[:, b % 2, c0:], ath[s][:, c0:].bitcast(F32),
                                  ALU.subtract).then_inc(at_ready[s], 1)

            dve.memset(prod[:, :, SEQ:SEQ + 1], 1.0).then_inc(one_set, 1)
            dve.wait_ge(one_set, 1)
            all_heads(dve, ON_DVE, score, value)

        @block.gpsimd
        def _(pool):
            def score(pr, hh, n):
                if PIECES[n][0] % QG in POOL_TILES:
                    weight(pool, pr, hh, n)

            def split_v(pr, hh):
                pool.wait_ge(v_loaded[hh], 16 * (pr + 1))
                apart(pool, passed)
                pool.tensor_copy(v2[hh][:, :, 0, :], v_in[:, hh, :, :]).then_inc(v_hi[hh], 1)
                pool.wait_ge(v_hi[hh], pr + 1)
                pool.tensor_tensor(v2[hh][:, :, 1, :], v_in[:, hh, :, :], v2[hh][:, :, 0, :].bitcast(F32),
                                   ALU.subtract).then_inc(v_ready[hh], 1)

            def value(pr, hh, b):
                if b == N_BLOCK // 2:
                    if hh == 0:
                        pool.wait_ge(av_done[3], (2 * pr) * per_at)
                        split_v(pr, 1)
                    elif not (isinstance(pr, int) and pr == NPAIR - 1):
                        pool.wait_ge(av_done[3], (2 * pr + 1) * per_at)
                        split_v(pr + 1, 0)

            split_v(0, 0)
            pool.wait_ge(one_set, 1)
            all_heads(pool, ON_DVE, score, value)


def phase_attend_sample(nc, qh_t, ql_t, kh_t, kl_t, cache_k, cache_v, v_sample, ident, identr, mask_r,
                        oa_t, ob_t):
    with ExitStack() as ctx:
        sb, pb, sem, sem2 = make_tools(nc, ctx)
        NK, HH, KB = PAST + NQ, H // 2, PAST // P
        q_all = sb("s_q", [P, H, P])
        knh = sb("s_knh", [P, H, P], F32R)
        knl = sb("s_knl", [P, H, P], F32R)
        q_pad = [sb(f"s_q_pad{s}", [P, HH * (P + NQ)], F32R) for s in range(2)]
        k_in = sb("s_k_in", [P, KB, H, 2, HD])
        v_in = sb("s_v_in", [P, KB, D])
        vn_in = sb("s_vn_in", [NQ, D])
        kth = sb("s_kth", [P, H, PAST], F32R)
        ktl = sb("s_ktl", [P, H, PAST], F32R)
        v2 = sb("s_v2", [P, KB, H, 2, HD], F32R)
        vn2 = sb("s_vn2", [NQ, H, 2, HD], F32R)
        a = sb("s_a", [P, 2, NK])
        keep = sb("s_keep", [P, 2, NK])
        prod = sb("s_prod", [P, 2, NK + 1])
        ath = [sb(f"s_ath{s}", [P, KB + 1, P], F32R) for s in range(2)]
        atl = [sb(f"s_atl{s}", [P, KB + 1, P], F32R) for s in range(2)]
        o_sb = sb("s_o", [P, H, P])
        pz = pb("s_pz", [P, 2, 512])
        pt = pb("s_pt", [P, 2, 4, P])
        po = pb("s_po", [P, H, P])
        loaded, k_loaded, v_loaded = sem("s_loaded"), sem("s_k_loaded"), sem("s_v_loaded")
        zeroed, q_set = sem("s_zeroed"), sem2("s_q_set")
        k_turned, k_hi, k_lo = sem2("s_k_turned"), sem2("s_k_hi"), sem2("s_k_lo")
        v_hi, v_lo = sem("s_v_hi"), sem("s_v_lo")
        z_ready, z_used, scanned, weighted = sem2("s_z_ready"), sem2("s_z_used"), sem2("s_scanned"), sem2("s_weighted")
        a_turned, at_hi, at_lo, av_done = sem2("s_a_turned"), sem2("s_at_hi"), sem2("s_at_lo"), sem2("s_av_done")
        o_read, o_stored = sem("s_o_read"), sem("s_o_stored")
        block = ctx.enter_context(nc.Block())
        NROUND = KB * H // 4
        new = slice(SEQ, T)
        head_major = lambda ap: ap[:, new].rearrange("(h d) t -> d h t", d=HD)

        @block.sync
        def _(sp):
            for dst, top, bottom in ((q_all, qh_t, ql_t), (knh, kh_t, kh_t), (knl, kl_t, kl_t)):
                for part, src in ((slice(0, HD), top), (slice(HD, P), bottom)):
                    d = dst[part, :, :] if dst is q_all else dst[part, :, :].bitcast(F32)
                    sp.dma_start(d, head_major(src)).then_inc(loaded, 16)
            with sp.Fori(0, NB) as b:
                sp.wait_ge(k_turned[1], NROUND // 2 * b)
                for twin in range(2):
                    for kb in range(KB):
                        sp.dma_start(k_in[:, kb, :, twin, :],
                                     cache_k[b, kb * P:(kb + 1) * P, :].rearrange("p (h d) -> p h d", d=HD))\
                          .then_inc(k_loaded, 16)
                sp.wait_ge(v_lo, 2 * b)
                sp.dma_start(v_in[:, :, :], cache_v[b, :, :].rearrange("(kb p) n -> p kb n", p=P))\
                  .then_inc(v_loaded, 16)
                sp.dma_start(vn_in[:, :], v_sample[bass.ds(b * NQ, NQ), :]).then_inc(v_loaded, 16)
            sp.wait_ge(o_read, 4)
            for part, dst in ((slice(0, HD), oa_t), (slice(HD, P), ob_t)):
                sp.dma_start(head_major(dst), o_sb[part, :, :]).then_inc(o_stored, 16)
            sp.wait_ge(o_stored, 32)

        @block.tensor
        def _(pe):
            pe.wait_ge(loaded, 96)
            with pe.Fori(0, NB) as b:
                pe.wait_ge(k_loaded, 32 * KB * (b + 1))
                for r in range(NROUND):
                    s, kb = r % 2, r // (H // 4)
                    pe.wait_ge(k_lo[s], NROUND // 2 * b + r // 2)
                    if r < 2:
                        pe.wait_ge(at_lo[s], 2 * b)
                    for i in range(4):
                        h = (4 * r + i) % H
                        mm = pe.transpose(pt[:, s, i, :], k_in[:, kb, h, :, :], ident[:, :])
                    mm.then_inc(k_turned[s], 1)
                for f in range(2):
                    pe.wait_ge(q_set[f], b + 1)
                    pe.wait_ge(z_used[f], b)
                    for s in range(2):
                        pe.wait_ge(k_lo[s], NROUND // 2 * (b + 1))
                    lhs = [q_pad[f][:, j * P:(j + 1) * P] for j in range(HH)]
                    for j in range(HH):
                        o = pz[:, f, 0:PAST]
                        pe.matmul(o, lhs[j], kth[:, HH * f + j, :], start=(j == 0), stop=False)
                        pe.matmul(o, lhs[j], ktl[:, HH * f + j, :], start=False, stop=(j == HH - 1))
                    for j in range(HH):
                        o = pz[:, f, PAST:NK]
                        at = bass.ds(b * NQ, NQ)
                        pe.matmul(o, lhs[j], knh[:, HH * f + j, at], start=(j == 0), stop=False)
                        pe.matmul(o, lhs[j], knl[:, HH * f + j, at], start=False, stop=False)
                    pe.matmul(o, identr[:, :], mask_r[:, :], start=False, stop=True).then_inc(z_ready[f], 1)
                for f in range(2):
                    pe.wait_ge(weighted[f], b + 1)
                    for kb in range(KB):
                        pe.transpose(pt[:, f, kb, :], a[:, f, kb * P:(kb + 1) * P], ident[:, :])
                    pe.transpose(pt[0:NQ, f, KB, :], a[:, f, PAST:NK], ident[:, :]).then_inc(a_turned[f], 1)
                pe.wait_ge(v_lo, 2 * (b + 1))
                for f in range(2):
                    pe.wait_ge(at_lo[f], 2 * (b + 1))
                    for j in range(HH):
                        h = HH * f + j
                        o = po[:, h, bass.ds(b * NQ, NQ)]
                        c = slice(j * NQ, (j + 1) * NQ)
                        for kb in range(KB):
                            pe.matmul(o, v2[:, kb, h, :, :], ath[f][:, kb, c], start=(kb == 0), stop=False)
                            pe.matmul(o, v2[:, kb, h, :, :], atl[f][:, kb, c], start=False, stop=False)
                        pe.matmul(o, vn2[:, h, :, :], ath[f][0:NQ, KB, c], start=False, stop=False)
                        mm = pe.matmul(o, vn2[:, h, :, :], atl[f][0:NQ, KB, c], start=False, stop=True)
                    mm.then_inc(av_done[f], 1)

        @block.scalar
        def _(act):
            with act.Fori(0, NB) as b:
                for r in range(NROUND):
                    s, kb, h0 = r % 2, r // (H // 4), (4 * r) % H
                    act.wait_ge(k_turned[s], NROUND // 2 * b + r // 2 + 1)
                    if r == 0:
                        act.wait_ge(z_ready[1], b)
                    act.activation(kth[:, h0:h0 + 4, kb * P:(kb + 1) * P], pt[:, s, :, :],
                                   ACT.Copy).then_inc(k_hi[s], 1)
                act.wait_ge(v_loaded, 32 * (b + 1))
                act.wait_ge(av_done[1], b)
                split = lambda ap: ap.rearrange("p kb (h d) -> p (kb h) d", d=HD)
                act.activation(v2[:, :, :, 0, :].rearrange("p kb h d -> p (kb h) d"), split(v_in[:, :, :]),
                               ACT.Copy).then_inc(v_hi, 1)
                act.activation(vn2[:, :, 0, :], vn_in[:, :].rearrange("p (h d) -> p h d", d=HD),
                               ACT.Copy).then_inc(v_hi, 1)
                for f in range(2):
                    act.wait_ge(z_ready[f], b + 1)
                    act.wait_ge(a_turned[f], b)
                    act.activation(a[:, f, :], pz[:, f, 0:NK], ACT.Sigmoid, scale=SCALE)
                    act.wait_ge(scanned[f], b)
                    act.activation(keep[:, f, :], pz[:, f, 0:NK], ACT.Sigmoid, scale=-SCALE)\
                       .then_inc(z_used[f], 1)
                for f in range(2):
                    act.wait_ge(a_turned[f], b + 1)
                    act.wait_ge(av_done[f], b)
                    act.activation(ath[f][:, 0:KB, :], pt[:, f, 0:KB, :], ACT.Copy).then_inc(at_hi[f], 1)
                    act.activation(ath[f][0:NQ, KB, :], pt[0:NQ, f, KB, :], ACT.Copy).then_inc(at_hi[f], 1)
            act.wait_ge(av_done[1], NB)
            for n in range(4):
                act.activation(o_sb[:, 4 * n:4 * n + 4, :], po[:, 4 * n:4 * n + 4, :], ACT.Copy)\
                   .then_inc(o_read, 1)

        @block.vector
        def _(dve):
            for f in range(2):
                dve.memset(q_pad[f][:, :].bitcast(F32), 0.0).then_inc(zeroed, 1)
                dve.memset(prod[:, f, NK:NK + 1], 1.0).then_inc(zeroed, 1)
            dve.wait_ge(zeroed, 4)
            dve.wait_ge(loaded, 96)
            with dve.Fori(0, NB) as b:
                for f in range(2):
                    dve.wait_ge(z_ready[f], b)
                    dve.tensor_copy(q_pad[f][:, :].rearrange("p (j r) -> p j r", r=P + NQ)[:, :, 0:NQ],
                                    q_all[:, HH * f:HH * (f + 1), bass.ds(b * NQ, NQ)]).then_inc(q_set[f], 1)
                for r in range(NROUND):
                    s, kb, h0 = r % 2, r // (H // 4), (4 * r) % H
                    at = slice(kb * P, (kb + 1) * P)
                    dve.wait_ge(k_hi[s], NROUND // 2 * b + r // 2 + 1)
                    dve.tensor_tensor(ktl[:, h0:h0 + 4, at], pt[:, s, :, :],
                                      kth[:, h0:h0 + 4, at].bitcast(F32), ALU.subtract).then_inc(k_lo[s], 1)
                dve.wait_ge(v_hi, 2 * (b + 1))
                split = lambda ap: ap.rearrange("p kb (h d) -> p (kb h) d", d=HD)
                part = lambda i: v2[:, :, :, i, :].rearrange("p kb h d -> p (kb h) d")
                dve.tensor_tensor(part(1), split(v_in[:, :, :]), part(0).bitcast(F32), ALU.subtract)\
                   .then_inc(v_lo, 1)
                dve.tensor_tensor(vn2[:, :, 1, :], vn_in[:, :].rearrange("p (h d) -> p h d", d=HD),
                                  vn2[:, :, 0, :].bitcast(F32), ALU.subtract).then_inc(v_lo, 1)
                for f in range(2):
                    dve.wait_ge(z_used[f], b + 1)
                    dve.wait_ge(weighted[f], b)
                    dve.tensor_tensor_scan(prod[:, f, 0:NK][:, ::-1], keep[:, f, :][:, ::-1],
                                           keep[:, f, :][:, ::-1], 1.0, ALU.mult, ALU.bypass)\
                       .then_inc(scanned[f], 1)
                    dve.wait_ge(scanned[f], b + 1)
                    dve.tensor_tensor(a[:, f, :], a[:, f, :], prod[:, f, 1:NK + 1], ALU.mult)\
                       .then_inc(weighted[f], 1)
                for f in range(2):
                    dve.wait_ge(at_hi[f], 2 * (b + 1))
                    dve.tensor_tensor(atl[f][:, 0:KB, :], pt[:, f, 0:KB, :], ath[f][:, 0:KB, :].bitcast(F32),
                                      ALU.subtract).then_inc(at_lo[f], 1)
                    dve.tensor_tensor(atl[f][0:NQ, KB, :], pt[0:NQ, f, KB, :],
                                      ath[f][0:NQ, KB, :].bitcast(F32), ALU.subtract).then_inc(at_lo[f], 1)


def build(nc, x_prompt, x_sample, state_conv, cache_k, cache_v, a_norm_pre, a_w_in, a_conv_w, a_w_out,
          a_norm_post, kv_norm, w_k, w_v, b_norm_pre, b_w_in, b_w_out, b_norm_post, ident_in, mask_in,
          mask_s_in, y_prompt, y_sample, conv_p, conv_s, k_prompt, v_prompt, k_sample, v_sample):
    flat = lambda ap: ap.rearrange("b t d -> (b t) d")
    heads = lambda ap: ap.rearrange("b t h d -> (b t) (h d)")
    xp, xsm, yp, ysm = flat(x_prompt), flat(x_sample), flat(y_prompt), flat(y_sample)
    kp, vp, ks, vs = heads(k_prompt), heads(v_prompt), heads(k_sample), heads(v_sample)

    def scratch(name, shape):
        return nc.dram_tensor(name, shape, F32, kind="Internal").ap()

    y_t, qh_t, ql_t, kh_t, kl_t, sz_t, oa_t, ob_t = (
        scratch(n, [D, T]) for n in ("y_t", "qh_t", "ql_t", "kh_t", "kl_t", "sz_t", "oa_t", "ob_t"))
    x1 = scratch("x1", [T, D])

    with ExitStack() as ctx:
        sb, pb, sem, sem2 = make_tools(nc, ctx)
        ident = sb("ident", [P, P])
        mask = sb("mask", [P, P])
        mask_s = sb("mask_s", [P, NQ])
        identr = sb("identr", [P, P], F32R)
        maskr = sb("maskr", [P, P], F32R)
        mask_sr = sb("mask_sr", [P, NQ], F32R)
        loaded, rounded = sem("k_loaded"), sem("k_rounded")
        with nc.Block() as block:
            @block.sync
            def _(sp):
                for dst, src in ((ident, ident_in), (mask, mask_in), (mask_s, mask_s_in)):
                    sp.dma_start(dst[:, :], src).then_inc(loaded, 16)

            @block.vector
            def _(dve):
                dve.wait_ge(loaded, 48)
                for dst, src in ((identr, ident), (maskr, mask), (mask_sr, mask_s)):
                    dve.tensor_copy(dst[:, :], src[:, :]).then_inc(rounded, 1)
                dve.wait_ge(rounded, 3)

        with ExitStack() as act_ctx:
            slab_at = (nc.sbuf_base + 31) // 32 * 32
            act_ctx.enter_context(nc.sbuf_tensor("slab", [P, KT * T], F32))
            at_slab = lambda name, dt: nc.alloc_sbuf_tensor_at(name, [P, KT, T], dt, offset=slab_at)
            with nc.sbuf_tensor("a_xh", [P, KT, T], F32R) as xh:
                xl = at_slab("a_xl", F32R)
                phase_norm_in(nc, xp, xsm, ident, xh, xl)
                phase_conv(nc, a_w_in[0], a_norm_pre[0], a_conv_w[0], state_conv[0].rearrange("b w d -> (b w) d"),
                           ident, xh, xl, y_t, conv_p[0, 0], conv_s[0].rearrange("b w d -> (b w) d"))
            x32 = at_slab("b_x32", F32)
            phase_out(nc, "f_", [y_t], a_w_out[0], a_norm_post[0], xp, xsm, ident,
                      x1[0:SEQ, :], x1[SEQ:T, :], x32)
            phase_qkvz(nc, w_k, w_v, b_w_in[0], kv_norm, b_norm_pre[0], ident, x32, at_slab("b_xl", F32R),
                       qh_t, ql_t, kh_t, kl_t, sz_t, kp, vp, ks, vs)
        phase_attend(nc, qh_t, ql_t, kh_t, kl_t, vp, ident, identr, maskr, oa_t, ob_t)
        phase_attend_sample(nc, qh_t, ql_t, kh_t, kl_t, cache_k.rearrange("b t h d -> b t (h d)"),
                            cache_v.rearrange("b t h d -> b t (h d)"), vs, ident, identr, mask_sr, oa_t, ob_t)
        phase_out(nc, "g_", [oa_t, ob_t, sz_t], b_w_out[0], b_norm_post[0], x1[0:SEQ, :], x1[SEQ:T, :], ident,
                  yp, ysm, None)


_INS = ["x_prompt", "x_sample", "state_conv", "cache_k", "cache_v", "a_norm_pre", "a_w_in", "a_conv_w",
        "a_w_out", "a_norm_post", "kv_norm", "w_k", "w_v", "b_norm_pre", "b_w_in", "b_w_out", "b_norm_post"]
_OUTS = [(1, SEQ, D), (NB, NQ, D), (1, 1, 2, D), (1, NB, 2, D), (1, SEQ, H, HD), (1, SEQ, H, HD),
         (NB, NQ, H, HD), (NB, NQ, H, HD)]


def kernel(**inputs):
    import concourse.bacc as bacc
    from concourse.bass_utils import run_bass_kernel_spmd

    nc = bacc.Bacc("TRN2", target_bir_lowering=False, num_devices=1)
    arrays = {name: np.ascontiguousarray(inputs[name]) for name in _INS}
    arrays["ident"] = np.eye(P, dtype=np.float32)
    arrays["mask"] = np.where(np.arange(P)[None, :] >= np.arange(P)[:, None], MASKED, 0.0).astype(np.float32)
    arrays["mask_s"] = np.where(np.arange(NQ)[None, :] >= np.arange(P)[:, None] % NQ, MASKED, 0.0)\
        .astype(np.float32)
    args = [nc.dram_tensor("in_" + n, a.shape, F32, kind="ExternalInput").ap() for n, a in arrays.items()]
    args += [nc.dram_tensor(f"out_{i}", s, F32, kind="ExternalOutput").ap() for i, s in enumerate(_OUTS)]
    build(nc, *args)
    r = run_bass_kernel_spmd(nc, [{"in_" + n: a for n, a in arrays.items()}], core_ids=[0])
    return tuple(r.results[0][f"out_{i}"] for i in range(len(_OUTS)))
```

```python
import concourse.bass as bass
from concourse import mybir
from contextlib import ExitStack
import numpy as np

F32 = mybir.dt.float32
F32R = mybir.dt.float32r
ALU = mybir.AluOpType
ACT = mybir.ActivationFunctionType

P = 128
D = 1024
KT = D // P
SEQ = 2048
NB, NQ = 8, 16
T = SEQ + NB * NQ
NT = T // P
PAST = 256
H, HD = 16, 64
SCALE = HD ** -0.5
EPS = 1e-6
CW = 3
GROUPS = [(0, 512), (512, 512), (1024, 384), (1408, 384), (1792, 384)]
NG = len(GROUPS)
QT = SEQ // P
QG = 4
NGQ = QT // QG
MASKED = -1e30


def nothing(*_):
    pass


def token_tiles(eng, first, second, third=nothing, slots=2):
    def step(j, k):
        at = lambda k: (j + k // slots, k % slots)
        first(*at(k + 1))
        third(*at(k - 1))
        second(*at(k))

    n = (NT - 2) // slots
    first(0, 0)
    first(0, 1)
    second(0, 0)
    with eng.Fori(0, n) as j:
        for k in range(1, slots + 1):
            step(j, k)
    for k in range(n * slots + 1, NT - 1):
        step(0, k)
    last = NT - 1
    third((last - 1) // slots, (last - 1) % slots)
    second(last // slots, last % slots)
    third(last // slots, last % slots)


def is_sample(j, s, slots=2):
    return isinstance(j, int) and slots * j + s == NT - 1


def apart(eng, passed):
    eng.sem_inc(passed, 1)


def wait_past(eng, sem, count):
    if not (isinstance(count, int) and count <= 0):
        eng.wait_ge(sem, count)


def make_tools(nc, ctx):
    def sb(name, shape, dt=F32):
        return ctx.enter_context(nc.sbuf_tensor(name, shape, dt))

    def pb(name, shape):
        return ctx.enter_context(nc.psum_tensor(name, shape, F32))

    sems = []

    def sem(name):
        sems.append(nc.alloc_semaphore(name))
        return sems[-1]

    def give_back():
        nc.clear_and_free_semaphores(sems)
        nc.all_engine_barrier()

    ctx.callback(give_back)

    def sem2(name, n=2):
        return [sem(f"{name}{i}") for i in range(n)]

    return sb, pb, sem, sem2


def phase_norm_in(nc, x_prompt, x_sample, ident, xh, xl, consts, begin_next, room, pg):
    with ExitStack() as ctx:
        sb, pb, sem, sem2 = make_tools(nc, ctx)
        S = 4
        x_in = sb("n_x", [P, S, D])
        xs = sb("n_xs", [P, S, D])
        junk = sb("n_junk", [P, D])
        ss = sb("n_ss", [P, S])
        std = sb("n_std", [P, S])
        rstd = sb("n_rstd", [P, S])
        epsb = sb("n_eps", [P, 1])
        ps = pb("n_ps", [P, 2, KT // 2, P])
        x_loaded = sem2("n_x_loaded", S)
        squared, std_ready, rstd_ready = sem2("n_squared", S), sem2("n_std", S), sem2("n_rstd", S)
        xs_ready, turned, hi_done, lo_done = sem2("n_xs_ready", S), sem2("n_turned"), sem2("n_hi"), sem2("n_lo")
        eps_set, consts_loaded = sem("n_eps_set"), sem("n_consts_loaded")
        first_split, projected = sem("n_first_split"), sem("n_projected")
        HK = KT // 2
        block = ctx.enter_context(nc.Block())

        @block.sync
        def _(sp):
            def load(j, s):
                sp.wait_ge(xs_ready[s], j)
                if is_sample(j, s, S):
                    src = x_sample
                else:
                    src = x_prompt[bass.ds((S * j + s) * P, P), :]
                sp.dma_start(x_in[:, s, :], src).then_inc(x_loaded[s], 16)

            token_tiles(sp, load, nothing, slots=S)
            for dst, src in consts:
                sp.dma_start(dst, src, allow_slow_non_contiguous=True).then_inc(consts_loaded, 16)
            sp.wait_ge(consts_loaded, 16 * len(consts))

        @block.gpsimd
        def _(pool):
            begin_next(pool, sem, first_split)

        @block.scalar
        def _(act):
            act.wait_ge(eps_set, 1)

            def sums(j, s):
                act.wait_ge(x_loaded[s], 16 * (j + 1))
                act.wait_ge(rstd_ready[s], j)
                act.activation(junk[:, :], x_in[:, s, :], ACT.Square,
                               accum_out=ss[:, s:s + 1]).then_inc(squared[s], 1)
                act.wait_ge(squared[s], j + 1)
                act.activation(std[:, s:s + 1], ss[:, s:s + 1], ACT.Sqrt, scale=1.0 / D,
                               bias=epsb[:, :]).then_inc(std_ready[s], 1)

            def high(j, s):
                t = S * j + s
                for h in range(2):
                    act.wait_ge(turned[h], t + 1 + S * h)
                    act.activation(xh[:, h * HK:(h + 1) * HK, bass.ds(t * P, P)], ps[:, h, :, :],
                                   ACT.Copy).then_inc(hi_done[h], 1)

            token_tiles(act, sums, high, slots=S)

        @block.vector
        def _(dve):
            dve.memset(epsb[:, :], EPS).then_inc(eps_set, 1)

            def scale(j, s):
                dve.wait_ge(std_ready[s], j + 1)
                dve.reciprocal(rstd[:, s:s + 1], std[:, s:s + 1]).then_inc(rstd_ready[s], 1)
                dve.wait_ge(rstd_ready[s], j + 1)
                dve.wait_ge(turned[1], S * j + s + 1)
                dve.tensor_scalar(xs[:, s, :], x_in[:, s, :], rstd[:, s:s + 1], None,
                                  ALU.mult).then_inc(xs_ready[s], 1)

            def low(j, s):
                t = S * j + s
                at = bass.ds(t * P, P)
                for h in range(2):
                    half = slice(h * HK, (h + 1) * HK)
                    dve.wait_ge(hi_done[h], t + 1)
                    dve.tensor_tensor(xl[:, half, at], ps[:, h, :, :], xh[:, half, at].bitcast(F32),
                                      ALU.subtract).then_inc(lo_done[h], 1)

            token_tiles(dve, scale, low, slots=S)

        @block.tensor
        def _(pe):
            pe.sem_inc(turned[1], S)

            def project_group(g, kt0, kt1):
                a, n = GROUPS[g]
                if kt0 == 0:
                    pe.wait_ge(first_split, 1)
                    for h in range(2):
                        pe.wait_ge(lo_done[h], (a + n) // P)
                mm = project(pe, pg[g][:, 0:n], room[1][0], room[2][0], xh, xl, a, n, kt0, kt1)
                if kt1 == KT:
                    mm.then_inc(projected, 1)

            for t in range(NT):
                j, s = divmod(t, S)
                pe.wait_ge(xs_ready[s], j + 1)
                for h in range(2):
                    wait_past(pe, lo_done[h], t)
                    for i in range(HK):
                        kt = h * HK + i
                        mm = pe.transpose(ps[:, h, i, :], xs[:, s, kt * P:(kt + 1) * P], ident[:, :])
                    mm.then_inc(turned[h], 1)
                for g in range(NG - 1):
                    t0, n = GROUPS[g + 1][0] // P, GROUPS[g + 1][1] // P
                    if t0 <= t < t0 + n:
                        project_group(g, (t - t0) * KT // n, (t - t0 + 1) * KT // n)
            project_group(NG - 1, 0, KT)
            pe.wait_ge(projected, NG)


def stream_room(nc, ctx, tag, n_gains):
    new = lambda name, shape, dt=F32: ctx.enter_context(nc.sbuf_tensor(tag + name, shape, dt))
    raw = new("raw", [P, 2, KT, P])
    wh, wl = [new("wh0", [P, KT, P], F32R)], [new("wl0", [P, KT, P], F32R)]
    gains = [new(f"gain{i}", [P, KT]) for i in range(n_gains)]
    return raw, wh, wl, gains


def whole_room(sb, tag, room):
    raw, wh, wl, gains = room
    return raw, wh + [sb(tag + "wh1", [P, KT, P], F32R)], wl + [sb(tag + "wl1", [P, KT, P], F32R)], gains


def load_gains(eng, gains, sources, loaded):
    for tile, src in zip(gains, sources):
        eng.dma_start(tile[:, :], src.rearrange("(kt p) -> p kt", p=P),
                      allow_slow_non_contiguous=True).then_inc(loaded, 16)


def split_weights(pool, room, s, gain, hi_ready, scaled, w_ready, u):
    raw, wh, wl, _ = room
    gain_b = gain.unsqueeze(2).broadcast_to([P, KT, P])
    pool.tensor_tensor(wh[s][:, :, :], raw[:, s, :, :], gain_b, ALU.mult).then_inc(hi_ready, 1)
    pool.wait_ge(hi_ready, u + 1)
    pool.tensor_tensor(raw[:, s, :, :], raw[:, s, :, :], gain_b, ALU.mult).then_inc(scaled, 1)
    pool.wait_ge(scaled, u + 1)
    pool.tensor_tensor(wl[s][:, :, :], raw[:, s, :, :], wh[s][:, :, :].bitcast(F32), ALU.subtract)\
        .then_inc(w_ready, 1)


def begin_stream(pool, room, order, gain_sources, sem, tag, split):
    raw, _, _, gains = room
    loaded, hi_ready, scaled = (sem(tag + n) for n in ("loaded", "hi_ready", "scaled"))
    load_gains(pool, gains, gain_sources, loaded)
    for m in range(2):
        pool.dma_start(raw[:, m, :, :], order[m][0](0)).then_inc(loaded, 16)
    pool.wait_ge(loaded, 16 * (len(gains) + 2))
    split_weights(pool, room, 0, order[0][1], hi_ready, scaled, split, 0)
    pool.wait_ge(split, 1)
    pool.dma_start(raw[:, 0, :, :], order[2][0](0)).then_inc(loaded, 16)
    pool.wait_ge(loaded, 16 * (len(gains) + 3))


def weight_stream(pool, n_iter, order, room, raw_loaded, scaled, hi_ready, w_ready, mm_done, passed):
    raw, n = room[0], len(order)

    def turn(c, first, last):
        for m, (_, gain) in enumerate(order):
            s, u = m % 2, c * (n // 2) + m // 2
            if not (first and m == 0):
                wait_past(pool, raw_loaded[s], 16 * (u + 1 - (2 - s)))
                if not (first and m < 2):
                    pool.wait_ge(mm_done[(m - 2) % n], NG * (c + 1 if m >= 2 else c))
                split_weights(pool, room, s, gain, hi_ready[s], scaled[s], w_ready[s], u)
                if not (last and m + 2 >= n):
                    nxt, cc = (m + 2, c) if m + 2 < n else (m + 2 - n, c + 1)
                    pool.wait_ge(w_ready[s], u + 1)
                    apart(pool, passed)
                    pool.dma_start(raw[:, s, :, :], order[nxt][0](cc)).then_inc(raw_loaded[s], 16)

    for done in (hi_ready[0], scaled[0], w_ready[0]):
        pool.sem_inc(done, 1)
    turn(0, True, False)
    with pool.Fori(1, n_iter - 1) as c:
        turn(c, False, False)
    turn(n_iter - 1, False, True)


def conv_order(w_in, room):
    w_v = w_in.rearrange("(kt p) (m c f) -> p kt m c f", p=P, m=4, f=P)
    return [(lambda c, b=b: w_v[:, :, b, c, :], room[3][0][:, :]) for b in (1, 2, 3, 0)]


def qkvz_order(w_k, w_v, w_qz, room):
    k_v = w_k.rearrange("(kt p) (c f) -> p kt c f", p=P, f=P)
    v_v = w_v.rearrange("(kt p) (c f) -> p kt c f", p=P, f=P)
    qz_v = w_qz.rearrange("(kt p) (m c f) -> p kt m c f", p=P, m=2, f=P)
    g_kv, g_b = (g[:, :] for g in room[3])
    return [(lambda c: k_v[:, :, c, :], g_kv), (lambda c: v_v[:, :, c, :], g_kv),
            (lambda c: qz_v[:, :, 0, c, :], g_b), (lambda c: qz_v[:, :, 1, c, :], g_b)]


def project(pe, out, w_h, w_l, x_h, x_l, a, n, kt0=0, kt1=KT):
    for kt in range(kt0, kt1):
        r = slice(a, a + n)
        pe.matmul(out, w_h[:, kt, :], x_h[:, kt, r], start=(kt == 0), stop=False)
        pe.matmul(out, w_h[:, kt, :], x_l[:, kt, r], start=False, stop=False)
        mm = pe.matmul(out, w_l[:, kt, :], x_h[:, kt, r], start=False, stop=(kt == KT - 1))
    return mm


def phase_conv(nc, order, room, pg, st_rows, cw_all, ident, xh, xl, y_t, conv_p, conv_s):
    with ExitStack() as ctx:
        sb, pb, sem, sem2 = make_tools(nc, ctx)
        room = whole_room(sb, "c_", room)
        _, wh, wl, _ = room
        cw = sb("c_cw", [P, CW])
        cg = sb("c_cgate", [P, T])
        u = sb("c_u", [P, 2 + SEQ])
        us = sb("c_us", [P, NB, 2 + NQ])
        t = sb("c_t", [P, T])
        sz = sb("c_sz", [P, T])
        st_t = sb("c_st_t", [P, KT, NB * 2])
        edge = sb("c_edge", [P, KT, 2 + NB * 2])
        edge_rows = sb("c_edge_rows", [2 + NB * 2, D])
        pm = pb("c_pm", [P, 2, 512])
        raw_loaded, scaled, hi_ready, w_ready = (
            sem2("c_raw_loaded"), sem2("c_scaled"), sem2("c_hi_ready"), sem2("c_w_ready"))
        passed = sem("c_passed")
        st_turned, st_ready = sem("c_st_turned"), sem("c_st_ready")
        mm_done = [sem(f"c_mm_{n}") for n in "chzb"]
        evac = [sem(f"c_evac_{n}") for n in "chzb"]
        taps, cw_ready, gated, edge_done = sem("c_taps"), sem("c_cw_ready"), sem("c_gated"), sem("c_edge_done")
        prefix = sem("c_prefix")
        y_stored, e_turned = sem("c_y_stored"), sem("c_e_turned")
        e_rows, e_stored = sem("c_e_rows"), sem("c_e_stored")
        block = ctx.enter_context(nc.Block())
        C, HH, Z, B = range(4)
        tail = SEQ - GROUPS[-1][0]

        @block.sync
        def _(sp):
            with sp.Fori(0, KT) as c:
                sp.wait_ge(evac[B], NG * (c + 2))
                sp.dma_start(y_t[bass.ds(c * P, P), :], sz[:, :]).then_inc(y_stored, 16)
            sp.wait_ge(e_rows, 2)
            sp.dma_start(conv_p, edge_rows[0:2, :]).then_inc(e_stored, 16)
            sp.dma_start(conv_s, edge_rows[2:2 + NB * 2, :]).then_inc(e_stored, 16)
            sp.wait_ge(y_stored, 16 * KT)
            sp.wait_ge(e_stored, 32)

        @block.gpsimd
        def _(pool):
            weight_stream(pool, KT, order, room, raw_loaded, scaled, hi_ready, w_ready, mm_done, passed)

        @block.tensor
        def _(pe):
            for c in range(KT):
                mm = pe.transpose(pm[:, 0, c * 16:(c + 1) * 16], st_rows[:, c * P:(c + 1) * P],
                                  ident[0:NB * 2, 0:NB * 2])
            mm.then_inc(st_turned, 1)
            pe.sem_inc(mm_done[C], NG)

            def projections(c, first_m):
                for m in range(first_m, 4):
                    s = m % 2
                    pe.wait_ge(w_ready[s], 2 * c + m // 2 + 1)
                    for g, (a, n) in enumerate(GROUPS):
                        pe.wait_ge(evac[(m - 1) % 4], NG * c + g + 1)
                        mm = project(pe, pg[g][:, 0:n], wh[s], wl[s], xh, xl, a, n)
                        mm.then_inc(mm_done[m], 1)

            projections(0, HH)
            with pe.Fori(1, KT) as c:
                projections(c, C)
            pe.wait_ge(edge_done, 2 * KT)
            for c in range(KT):
                mm = pe.transpose(pm[0:18, c // 4, (c % 4) * P:(c % 4 + 1) * P], edge[:, c, :], ident[:, :])
            mm.then_inc(e_turned, 1)

        @block.scalar
        def _(act):
            act.wait_ge(st_turned, 1)
            act.activation(st_t[:, :, :].rearrange("p a b -> p (a b)"), pm[:, 0, 0:KT * 16],
                           ACT.Copy).then_inc(st_ready, 1)
            with act.Fori(0, KT) as c:
                for g, (a, n) in enumerate(GROUPS):
                    act.wait_ge(mm_done[C], NG * c + g + 1)
                    act.wait_ge(evac[HH], NG * c)
                    act.activation(cg[:, a:a + n], pg[g][:, 0:n], ACT.Copy).then_inc(evac[C], 1)
                act.wait_ge(y_stored, 16 * c)
                for g, (a, n) in enumerate(GROUPS):
                    act.wait_ge(mm_done[Z], NG * c + g + 1)
                    act.activation(sz[:, a:a + n], pg[g][:, 0:n], ACT.Silu).then_inc(evac[Z], 1)
            act.wait_ge(e_turned, 1)
            for half in range(2):
                act.activation(edge_rows[:, half * 512:(half + 1) * 512], pm[0:18, half, :],
                               ACT.Copy).then_inc(e_rows, 1)

        @block.vector
        def _(dve):
            dve.wait_ge(st_ready, 1)
            dve.memset(u[:, 0:2], 0.0).then_inc(evac[B], NG)
            t_s = t[:, SEQ:T].rearrange("p (b q) -> p b q", q=NQ)
            with dve.Fori(0, KT) as c:
                dve.wait_ge(taps, 5 * c)
                dve.tensor_copy(cw[:, :], cw_all[:, c, :]).then_inc(cw_ready, 1)
                dve.tensor_copy(us[:, :, 0:2], st_t[:, c, :].rearrange("p (b w) -> p b w", w=2))\
                   .then_inc(prefix, 1)
                for g, (a, n) in enumerate(GROUPS):
                    dve.wait_ge(mm_done[HH], NG * c + g + 1)
                    dve.wait_ge(evac[C], NG * c + g + 1)
                    np_ = n if g < NG - 1 else tail
                    op = dve.tensor_tensor(u[:, 2 + a:2 + a + np_], pg[g][:, 0:np_], cg[:, a:a + np_], ALU.mult)
                    if g == NG - 1:
                        op = dve.tensor_tensor(
                            us[:, :, 2:2 + NQ], pg[g][:, np_:n].rearrange("p (b q) -> p b q", q=NQ),
                            cg[:, SEQ:T].rearrange("p (b q) -> p b q", q=NQ), ALU.mult)
                    op.then_inc(evac[HH], 1)
                dve.wait_ge(evac[HH], NG * (c + 1))
                dve.wait_ge(cw_ready, c + 1)
                dve.wait_ge(prefix, c + 1)
                dve.wait_ge(evac[B], NG * (c + 1))
                dve.tensor_copy(edge[:, c, 0:2], u[:, SEQ:SEQ + 2]).then_inc(edge_done, 1)
                dve.tensor_copy(edge[:, c, 2:18].rearrange("p (b w) -> p b w", w=2),
                                us[:, :, NQ:NQ + 2]).then_inc(edge_done, 1)
                dve.tensor_scalar(t[:, 0:SEQ], u[:, 0:SEQ], cw[:, 0:1], None, ALU.mult).then_inc(taps, 1)
                dve.tensor_scalar(t_s, us[:, :, 0:NQ], cw[:, 0:1], None, ALU.mult).then_inc(taps, 1)
                dve.wait_ge(taps, 5 * c + 2)
                dve.scalar_tensor_tensor(t[:, 0:SEQ], u[:, 1:1 + SEQ], cw[:, 1:2], t[:, 0:SEQ],
                                         ALU.mult, ALU.add).then_inc(taps, 1)
                dve.scalar_tensor_tensor(t_s, us[:, :, 1:1 + NQ], cw[:, 1:2], t_s, ALU.mult, ALU.add)\
                   .then_inc(taps, 1)
                dve.wait_ge(taps, 5 * c + 4)
                dve.scalar_tensor_tensor(t[:, 0:SEQ], u[:, 2:2 + SEQ], cw[:, 2:3], t[:, 0:SEQ],
                                         ALU.mult, ALU.add)
                dve.scalar_tensor_tensor(t_s, us[:, :, 2:2 + NQ], cw[:, 2:3], t_s, ALU.mult, ALU.add)\
                   .then_inc(taps, 1)
                dve.wait_ge(taps, 5 * c + 5)
                for g, (a, n) in enumerate(GROUPS):
                    dve.wait_ge(evac[Z], NG * c + g + 1)
                    dve.tensor_tensor(t[:, a:a + n], t[:, a:a + n], sz[:, a:a + n], ALU.mult)\
                       .then_inc(gated, 1)
                for g, (a, n) in enumerate(GROUPS):
                    dve.wait_ge(mm_done[B], NG * c + g + 1)
                    dve.wait_ge(gated, NG * c + g + 1)
                    dve.tensor_tensor(sz[:, a:a + n], pg[g][:, 0:n], t[:, a:a + n], ALU.mult)\
                       .then_inc(evac[B], 1)


def out_weights(nc, ctx, tag):
    wh = ctx.enter_context(nc.sbuf_tensor(tag + "wh", [P, KT, D], F32R))
    at = (nc.sbuf_base + 31) // 32 * 32
    ctx.enter_context(nc.sbuf_tensor(tag + "w_room", [P, KT * D], F32))
    raw, wl = (nc.alloc_sbuf_tensor_at(tag + n, [P, KT, D], dt, offset=at) for n, dt in (("raw", F32), ("wl", F32R)))
    return raw, wh, wl


def load_weights(sp, w_out, raw, w_loaded):
    for kt in range(KT):
        sp.dma_start(raw[:, kt, :], w_out[kt * P:(kt + 1) * P, :]).then_inc(w_loaded[kt], 16)


def phase_out(nc, tag, parts, w_out, post_gain, x_prompt, x_sample, ident, out_prompt, out_sample, x32, ready=None,
              begin_next=None):
    with ExitStack() as ctx:
        sb, pb, sem, sem2 = make_tools(nc, ctx)
        n_in = len(parts)
        raw, wh, wl = ready or out_weights(nc, ctx, tag)
        gain = sb(tag + "gain", [P, D])
        y_in = sb(tag + "y_in", [P, 2, n_in, KT, P])
        yh = [sb(f"{tag}yh{s}", [P, KT, P], F32R) for s in range(2)]
        yl = [sb(f"{tag}yl{s}", [P, KT, P], F32R) for s in range(2)]
        x_in = sb(tag + "x", [P, 2, D])
        xn = sb(tag + "xn", [P, 2, D])
        xs = sb(tag + "xs", [P, D])
        junk = sb(tag + "junk", [P, D])
        ss = sb(tag + "ss", [P, 2, 2])
        std = sb(tag + "std", [P, 2, 2])
        rstd = sb(tag + "rstd", [P, 2, 2])
        epsb = sb(tag + "eps", [P, 1])
        ph = pb(tag + "ph", [P, 2, D])
        pt = pb(tag + "pt", [P, 2, KT, P])
        w_loaded, w_hi, w_lo = sem2(tag + "w_loaded", KT), sem(tag + "w_hi"), sem(tag + "w_lo")
        consts, passed = sem(tag + "consts"), sem(tag + "passed")
        y_loaded, y_sum, y_whole, y_hi, y_lo = (sem2(tag + "y_loaded"), sem2(tag + "y_sum"), sem2(tag + "y_whole"),
                                                sem2(tag + "y_hi"), sem2(tag + "y_lo"))
        x_loaded, mm_done = sem2(tag + "x_loaded"), sem2(tag + "mm_done")
        squared, std_ready, rstd_ready = sem2(tag + "squared"), sem2(tag + "std_ready"), sem2(tag + "rstd_ready")
        normed, summed, stored = sem2(tag + "normed"), sem2(tag + "summed"), sem2(tag + "stored")
        scaled, turned, kept = sem(tag + "scaled"), sem2(tag + "turned"), sem2(tag + "kept")
        block = ctx.enter_context(nc.Block())
        views = [a.rearrange("(kt p) t -> p kt t", p=P) for a in parts]
        norms = 2 if x32 is not None else 1

        @block.sync
        def _(sp):
            def load_y(j, s):
                at = bass.ds((2 * j + s) * P, P)
                for i, v in enumerate(views):
                    sp.dma_start(y_in[:, s, i, :, :], v[:, :, at]).then_inc(y_loaded[s], 16)

            def load(j, s):
                if not (isinstance(j, int) and j == 0):
                    sp.wait_ge(y_lo[s], j)
                    load_y(j, s)
                    sp.wait_ge(summed[s], j)
                src = x_sample if is_sample(j, s) else x_prompt[bass.ds((2 * j + s) * P, P), :]
                sp.dma_start(x_in[:, s, :], src).then_inc(x_loaded[s], 16)

            load_y(0, 0)
            load_y(0, 1)
            if ready is None:
                load_weights(sp, w_out, raw, w_loaded)
            sp.dma_start(gain[:, :], post_gain.partition_broadcast(P)).then_inc(consts, 16)
            token_tiles(sp, load, nothing)

        @block.gpsimd
        def _(pool):
            def store(j, s):
                pool.wait_ge(summed[s], j + 1)
                apart(pool, passed)
                dst = out_sample if is_sample(j, s) else out_prompt[bass.ds((2 * j + s) * P, P), :]
                pool.dma_start(dst, xn[:, s, :]).then_inc(stored[s], 16)

            if begin_next is not None:
                pool.wait_ge(w_lo, KT)
                begin_next(pool, sem)
            token_tiles(pool, nothing, store)
            pool.wait_ge(stored[0], 16 * (NT // 2 + 1))
            pool.wait_ge(stored[1], 16 * (NT // 2))

        @block.scalar
        def _(act):
            def split(j, s):
                if n_in == 1:
                    act.wait_ge(y_loaded[s], 16 * (j + 1))
                else:
                    act.wait_ge(y_whole[s], j + 1)
                act.wait_ge(mm_done[s], j)
                act.activation(yh[s][:, :, :], y_in[:, s, 0, :, :], ACT.Copy).then_inc(y_hi[s], 1)

            def rms(src, j, s, k):
                act.wait_ge(rstd_ready[s], norms * j + k)
                act.activation(junk[:, :], src, ACT.Square, accum_out=ss[:, s, k:k + 1]).then_inc(squared[s], 1)
                act.wait_ge(squared[s], norms * j + k + 1)
                act.activation(std[:, s, k:k + 1], ss[:, s, k:k + 1], ACT.Sqrt, scale=1.0 / D,
                               bias=epsb[:, :]).then_inc(std_ready[s], 1)

            def tail(j, s):
                act.wait_ge(mm_done[s], j + 1)
                rms(ph[:, s, :], j, s, 0)
                if x32 is not None:
                    act.wait_ge(summed[s], j + 1)
                    rms(xn[:, s, :], j, s, 1)

            def keep(j, s):
                if x32 is not None:
                    act.wait_ge(turned[s], j + 1)
                    act.activation(x32[:, :, bass.ds((2 * j + s) * P, P)], pt[:, s, :, :],
                                   ACT.Copy).then_inc(kept[s], 1)

            def split_all(j, s):
                split(j, s)
                if ready is None and isinstance(j, int) and (j, s) == (0, 1):
                    for kt in range(KT):
                        act.wait_ge(w_loaded[kt], 16)
                        act.activation(wh[:, kt, :], raw[:, kt, :], ACT.Copy).then_inc(w_hi, 1)
                    act.wait_ge(consts, 1)

            if ready is not None:
                act.wait_ge(consts, 1)
            token_tiles(act, split_all, tail, keep)

        @block.vector
        def _(dve):
            dve.memset(epsb[:, :], EPS).then_inc(consts, 1)
            def split(j, s):
                y = y_in[:, s, 0, :, :]
                if n_in == 3:
                    dve.wait_ge(y_loaded[s], 16 * n_in * (j + 1))
                    dve.tensor_tensor(y, y, y_in[:, s, 1, :, :], ALU.add).then_inc(y_sum[s], 1)
                    dve.wait_ge(y_sum[s], j + 1)
                    dve.tensor_tensor(y, y, y_in[:, s, 2, :, :], ALU.mult).then_inc(y_whole[s], 1)
                dve.wait_ge(y_hi[s], j + 1)
                dve.tensor_tensor(yl[s][:, :, :], y, yh[s][:, :, :].bitcast(F32),
                                  ALU.subtract).then_inc(y_lo[s], 1)

            def inverse(j, s, k):
                dve.wait_ge(std_ready[s], norms * j + k + 1)
                dve.reciprocal(rstd[:, s, k:k + 1], std[:, s, k:k + 1]).then_inc(rstd_ready[s], 1)
                dve.wait_ge(rstd_ready[s], norms * j + k + 1)

            def tail(j, s):
                inverse(j, s, 0)
                dve.wait_ge(stored[s], 16 * j)
                dve.scalar_tensor_tensor(xn[:, s, :], ph[:, s, :], rstd[:, s, 0:1], gain[:, :],
                                         ALU.mult, ALU.mult).then_inc(normed[s], 1)
                dve.wait_ge(normed[s], j + 1)
                dve.wait_ge(x_loaded[s], 16 * (j + 1))
                dve.tensor_tensor(xn[:, s, :], xn[:, s, :], x_in[:, s, :], ALU.add).then_inc(summed[s], 1)
                if x32 is not None:
                    inverse(j, s, 1)
                    dve.wait_ge(turned[1 - s], j + s)
                    dve.tensor_scalar(xs[:, :], xn[:, s, :], rstd[:, s, 1:2], None, ALU.mult).then_inc(scaled, 1)

            def split_all(j, s):
                split(j, s)
                if isinstance(j, int) and (j, s) == (0, 1):
                    if ready is None:
                        for kt in range(KT):
                            dve.wait_ge(w_hi, kt + 1)
                            dve.tensor_tensor(wl[:, kt, :], raw[:, kt, :],
                                              wh[:, kt, :].bitcast(F32), ALU.subtract).then_inc(w_lo, 1)
                    dve.wait_ge(consts, 17)

            token_tiles(dve, split_all, tail)

        @block.tensor
        def _(pe):
            def products(s, n, kt):
                r = slice(n * 512, (n + 1) * 512)
                o = ph[:, s, r]
                pe.matmul(o, yh[s][:, kt, :], wh[:, kt, r], start=(kt == 0), stop=False)
                pe.matmul(o, yh[s][:, kt, :], wl[:, kt, r], start=False, stop=False)
                return pe.matmul(o, yl[s][:, kt, :], wh[:, kt, r], start=False, stop=(kt == KT - 1))

            def multiply(j, s):
                if ready is None and isinstance(j, int) and j == 0:
                    if s == 1:
                        for kt in range(KT):
                            pe.wait_ge(w_lo, kt + 1)
                            for t in range(2):
                                pe.wait_ge(y_lo[t], 1)
                                for n in range(2):
                                    mm = products(t, n, kt)
                                if kt == KT - 1:
                                    mm.then_inc(mm_done[t], 1)
                    return
                pe.wait_ge(y_lo[s], j + 1)
                pe.wait_ge(normed[s], j)
                for n in range(2):
                    for kt in range(KT):
                        mm = products(s, n, kt)
                mm.then_inc(mm_done[s], 1)

            def turn(j, s):
                if x32 is not None:
                    pe.wait_ge(scaled, 2 * j + s + 1)
                    pe.wait_ge(kept[s], j)
                    for kt in range(KT):
                        mm = pe.transpose(pt[:, s, kt, :], xs[:, kt * P:(kt + 1) * P], ident[:, :])
                    mm.then_inc(turned[s], 1)

            token_tiles(pe, multiply, turn)


def phase_qkvz(nc, order, room, ident, x32, xl, qh_t, ql_t, kh_t, kl_t, sz_t,
               k_prompt, v_prompt, k_sample, v_sample):
    with ExitStack() as ctx:
        sb, pb, sem, sem2 = make_tools(nc, ctx)
        xh = sb("q_xh", [P, KT, T], F32R)
        room = whole_room(sb, "q_", room)
        _, wh, wl, _ = room
        hi = sb("q_hi", [P, 2, 512], F32R)
        lo = sb("q_lo", [P, 2, 512], F32R)
        full = sb("q_full", [P, 2, 512])
        gate = sb("q_gate", [P, 2, 512])
        rows = sb("q_rows", [P, 2, 4, P])
        pg = [pb(f"q_pg{g}", [P, 512]) for g in range(NG)]
        pt = pb("q_pt", [P, 2, 4, P])
        raw_loaded, scaled, hi_ready, w_ready = (
            sem2("q_raw_loaded"), sem2("q_scaled"), sem2("q_hi_ready"), sem2("q_w_ready"))
        passed, passed_sp = sem("q_passed"), sem("q_passed_sp")
        x_hi, x_lo = sem("q_x_hi"), sem("q_x_lo")
        mm_done = [sem(f"q_mm_{n}") for n in "kvqz"]
        high, low, hl_stored = sem2("q_high"), sem2("q_low"), sem2("q_hl_stored")
        whole, turned, rowed, rows_stored = sem2("q_whole"), sem2("q_turned"), sem2("q_rowed"), sem2("q_rows_stored")
        gated, gate_stored = sem("q_gated"), sem2("q_gate_stored")
        block = ctx.enter_context(nc.Block())
        K, V, Q, Z = range(4)
        X_PARTS = [(0, 2 * i, 2 * i + 2) for i in range(KT // 2)] + [(g, 0, KT) for g in range(1, NG)]
        def uses(kinds, m, g):
            n = [(mm, gg) for mm in kinds for gg in range(NG)]
            s = (NG * m + g) % 2
            same = [x for x in n if (NG * x[0] + x[1]) % 2 == s]
            return s, len(same), same.index((m, g))

        @block.sync
        def _(sp):
            def rows_out(c, m, g):
                a, n = GROUPS[g]
                s, per, k = uses((K, V), m, g)
                sp.wait_ge(rowed[s], per * c + k + 1)
                apart(sp, passed_sp)
                out_p, out_s = ((k_prompt, k_sample), (v_prompt, v_sample))[m]
                nt, np_ = n // P, (min(a + n, SEQ) - a) // P
                cols = bass.ds(c * P, P)
                sp.dma_start(out_p[a:a + np_ * P, cols].rearrange("(i p) f -> p i f", p=P),
                             rows[:, s, 0:np_, :]).then_inc(rows_stored[s], 16)
                if np_ < nt:
                    sp.dma_start(out_s[:, cols], rows[:, s, np_, :]).then_inc(rows_stored[s], 16)
                else:
                    sp.sem_inc(rows_stored[s], 16)

            with sp.Fori(0, KT) as c:
                at = bass.ds(c * P, P)
                for m in (K, V, Q, Z):
                    for g, (a, n) in enumerate(GROUPS):
                        if m in (K, Q):
                            s, per, k = uses((K, Q), m, g)
                            for part, done, dst in ((hi, high, (kh_t, qh_t)), (lo, low, (kl_t, ql_t))):
                                sp.wait_ge(done[s], per * c + k + 1)
                                sp.dma_start(dst[m == Q][at, a:a + n], part[:, s, 0:n].bitcast(F32))\
                                  .then_inc(hl_stored[s], 16)
                        if m == Z:
                            s, per, k = uses((Z,), m, g)
                            sp.wait_ge(gated, NG * (c + 1) + g + 1)
                            sp.dma_start(sz_t[at, a:a + n], gate[:, s, 0:n]).then_inc(gate_stored[s], 16)
                        if m in (K, V) and g >= 1:
                            rows_out(c, m, g - 1)
                        if m in (V, Q) and g == 0:
                            rows_out(c, m - 1, NG - 1)
            for s in range(2):
                sp.wait_ge(hl_stored[s], 32 * uses((K, Q), 0, s)[1] * KT)
                sp.wait_ge(gate_stored[s], 16 * uses((Z,), Z, 1 - s)[1] * KT)
                sp.wait_ge(rows_stored[s], 32 * uses((K, V), 0, s)[1] * KT)

        @block.gpsimd
        def _(pool):
            weight_stream(pool, KT, order, room, raw_loaded, scaled, hi_ready, w_ready, mm_done, passed)

        @block.tensor
        def _(pe):
            def turn(c, m, g):
                s, per, k = uses((K, V), m, g)
                pe.wait_ge(whole[s], per * c + k + 1)
                pe.wait_ge(rowed[s], per * c + k)
                for i in range(GROUPS[g][1] // P):
                    mm = pe.transpose(pt[:, s, i, :], full[:, s, i * P:(i + 1) * P], ident[:, :])
                mm.then_inc(turned[s], 1)

            def bank_read(c, m, g):
                if m == K:
                    pe.wait_ge(gated, NG * c + g + 1)
                else:
                    kinds, done = ((K, Q), low) if m - 1 in (K, Q) else ((K, V), whole)
                    s, per, k = uses(kinds, m - 1, g)
                    pe.wait_ge(done[s], per * c + k + 1)

            with pe.Fori(0, KT) as c:
                for m in range(4):
                    s = m % 2
                    pe.wait_ge(w_ready[s], 2 * c + m // 2 + 1)
                    for g, (a, n) in enumerate(GROUPS):
                        bank_read(c, m, g)
                        if m == K:
                            pe.wait_ge(x_lo, KT // 2 + g)
                        mm = project(pe, pg[g][:, 0:n], wh[s], wl[s], xh, xl, a, n)
                        mm.then_inc(mm_done[m], 1)
                        if m in (K, V) and g >= 1:
                            turn(c, m, g - 1)
                        if m in (V, Q) and g == 0:
                            turn(c, m - 1, NG - 1)

        def rows_copy(act, c, m, g):
            s, per, k = uses((K, V), m, g)
            nt = GROUPS[g][1] // P
            act.wait_ge(turned[s], per * c + k + 1)
            act.wait_ge(rows_stored[s], 32 * (per * c + k))
            act.activation(rows[:, s, 0:nt, :], pt[:, s, 0:nt, :], ACT.Copy).then_inc(rowed[s], 1)

        @block.scalar
        def _(act):
            for g, k0, k1 in X_PARTS:
                a, n = GROUPS[g]
                act.activation(xh[:, k0:k1, a:a + n], x32[:, k0:k1, a:a + n], ACT.Copy).then_inc(x_hi, 1)
            with act.Fori(0, KT) as c:
                for m in range(4):
                    for g, (a, n) in enumerate(GROUPS):
                        act.wait_ge(mm_done[m], NG * c + g + 1)
                        if m in (K, V):
                            s, per, k = uses((K, V), m, g)
                            act.wait_ge(turned[s], per * c + k)
                            act.activation(full[:, s, 0:n], pg[g][:, 0:n], ACT.Copy).then_inc(whole[s], 1)
                        if m == Q:
                            s, per, k = uses((K, Q), m, g)
                            act.wait_ge(hl_stored[s], 32 * (per * c + k))
                            act.activation(hi[:, s, 0:n], pg[g][:, 0:n], ACT.Copy).then_inc(high[s], 1)
                        if m == Z:
                            s, per, k = uses((Z,), m, g)
                            act.wait_ge(gate_stored[s], 16 * (per * c + k))
                            act.activation(gate[:, s, 0:n], pg[g][:, 0:n], ACT.Silu).then_inc(gated, 1)
                        if m in (K, V) and g >= 1:
                            rows_copy(act, c, m, g - 1)
                        if m in (V, Q) and g == 0:
                            rows_copy(act, c, m - 1, NG - 1)

        @block.vector
        def _(dve):
            dve.sem_inc(gated, NG)
            for i, (g, k0, k1) in enumerate(X_PARTS):
                a, n = GROUPS[g]
                dve.wait_ge(x_hi, i + 1)
                dve.tensor_tensor(xl[:, k0:k1, a:a + n], x32[:, k0:k1, a:a + n],
                                  xh[:, k0:k1, a:a + n].bitcast(F32), ALU.subtract).then_inc(x_lo, 1)
            with dve.Fori(0, KT) as c:
                for m in (K, Q):
                    for g, (a, n) in enumerate(GROUPS):
                        s, per, k = uses((K, Q), m, g)
                        if m == K:
                            ws, wper, wk = uses((K, V), m, g)
                            dve.wait_ge(whole[ws], wper * c + wk + 1)
                            dve.wait_ge(hl_stored[s], 32 * (per * c + k))
                            dve.tensor_copy(hi[:, s, 0:n], pg[g][:, 0:n]).then_inc(high[s], 1)
                        dve.wait_ge(high[s], per * c + k + 1)
                        dve.wait_ge(hl_stored[s], 32 * (per * c + k))
                        dve.tensor_tensor(lo[:, s, 0:n], pg[g][:, 0:n], hi[:, s, 0:n].bitcast(F32),
                                          ALU.subtract).then_inc(low[s], 1)


Z_W = 1024
ORDER = list(reversed(range(NGQ)))
PIECES = [(i, p, min(p + Z_W, (i + 1) * P)) for g in ORDER for i in range(QG * g, QG * (g + 1))
          for p in reversed(range(0, (i + 1) * P, Z_W))]
BLOCKS = [(g, kb) for g in ORDER for kb in range(QG * (g + 1))]
N_PIECE, N_BLOCK = len(PIECES), len(BLOCKS)


def piece_uses(n):
    return sum(PIECES[m][0] % 2 == PIECES[n][0] % 2 for m in range(n))


def tile_uses(i):
    last = max(n for n, x in enumerate(PIECES) if x[0] == i)
    return piece_uses(last) + 1


LEAD = 9344
TS = 3
ON_PE, ON_ACT, ON_DVE = -1, 0, 1


def cycle(behind):
    starts = [sum(p1 - p0 for _, p0, p1 in PIECES[:n]) for n in range(N_PIECE + 1)]
    total = starts[-1]
    items = [(b * total / N_BLOCK, "value", b, 0) for b in range(N_BLOCK)]
    for n in range(N_PIECE):
        turn, k = divmod(n + behind, N_PIECE)
        at = starts[k] + total * turn - LEAD
        items.append((at + total * (at < 0), "score", n, int(at < 0)))
    return [x[1:] for x in sorted(items)]


def phase_attend(nc, qh_t, ql_t, kh_t, kl_t, v_prompt, ident, identr, maskr, oa_t, ob_t):
    with ExitStack() as ctx:
        sb, pb, sem, sem2 = make_tools(nc, ctx)
        q2 = [sb(f"a_q{s}", [P, SEQ], F32R) for s in range(2)]
        kh2 = [sb(f"a_kh{s}", [P, SEQ], F32R) for s in range(2)]
        kl2 = [sb(f"a_kl{s}", [P, SEQ], F32R) for s in range(2)]
        v_in = sb("a_v_in", [P, 2, QT, HD])
        v2 = [sb(f"a_v{s}", [P, QT, 2, HD], F32R) for s in range(2)]
        a = [sb(f"a_a{g}", [P, QG, QG * P * (g + 1)]) for g in range(NGQ)]
        keep = sb("a_keep", [P, 2, SEQ])
        prod = sb("a_prod", [P, 2, SEQ + 1])
        ath = [sb(f"a_ath{s}", [P, QG * P], F32R) for s in range(4)]
        atl = [sb(f"a_atl{s}", [P, QG * P], F32R) for s in range(4)]
        o_sb = sb("a_o", [P, 2, QG * P])
        pz = pb("a_pz", [P, 2, Z_W])
        pt = pb("a_pt", [P, TS, QG * P])
        po = pb("a_po", [P, QG * P])
        passed, passed_sp, first_loaded = sem("a_passed"), sem("a_passed_sp"), sem("a_first_loaded")
        qk_loaded, v_loaded = sem2("a_qk_loaded"), sem2("a_v_loaded")
        v_hi, v_ready = sem2("a_v_hi"), sem2("a_v_ready")
        z_ready, z_used = sem2("a_z_ready"), sem2("a_z_used")
        scanned, weighted, one_set = sem2("a_scanned"), sem2("a_weighted"), sem("a_one_set")
        t_ready, at_hi, at_ready, av_done = (sem2("a_t_ready", TS), sem2("a_at_hi", 4), sem2("a_at_ready", 4),
                                             sem2("a_av_done", 4))
        o_read, o_stored = sem2("a_o_read"), sem2("a_o_stored")
        block = ctx.enter_context(nc.Block())
        NPAIR = H // 2
        group_end = [BLOCKS.index((g, QG * (g + 1) - 1)) // 4 + 1 for g in range(NGQ)]
        per_z, per_i, per_at = N_PIECE // 2, N_PIECE // 2, N_BLOCK // 4

        ENDS = {BLOCKS.index((g, QG * (g + 1) - 1)): g for g in range(1, NGQ)}

        def group_uses(pr, hh, g):
            return (2 * pr + hh) * (NGQ // 2) + ORDER.index(g) // 2

        def turned_uses(pr, hh, b):
            return (2 * pr + hh) * len(range(b % TS, N_BLOCK, TS)) + b // TS

        def all_heads(eng, behind, score, value=nothing, tail=nothing):
            def pair(pr, last):
                for hh in range(2):
                    for what, n, ahead in cycle(behind):
                        if what == "value":
                            value(pr, hh, n)
                            if n - TS in ENDS:
                                tail(pr, hh, ENDS[n - TS])
                            if n == TS - 1 and hh == 1:
                                tail(pr, 0, 0)
                        elif not ahead:
                            score(pr, hh, n)
                        elif hh == 0:
                            score(pr, 1, n)
                        elif not last:
                            score(pr + 1, 0, n)
                tail(pr, 1, 0)

            for what, n, ahead in cycle(behind):
                if ahead:
                    score(0, 0, n)
            with eng.Fori(0, NPAIR - 1) as pr:
                pair(pr, False)
            pair(NPAIR - 1, True)

        @block.sync
        def _(sp):
            def load(pr, hh, tokens=slice(0, SEQ), done=None):
                rows = bass.ds((2 * pr + hh) * HD, HD)
                for dst, top, bottom in ((q2, qh_t, ql_t), (kh2, kh_t, kh_t), (kl2, kl_t, kl_t)):
                    for part, src in ((slice(0, HD), top), (slice(HD, P), bottom)):
                        sp.dma_start(dst[hh][part, tokens].bitcast(F32), src[rows, tokens])\
                          .then_inc(done or qk_loaded[hh], 16)

            def load_v(pr, hh):
                cols = bass.ds((2 * pr + hh) * HD, HD)
                sp.dma_start(v_in[:, hh, :, :], v_prompt[:, cols].rearrange("(b p) d -> p b d", p=P))\
                  .then_inc(v_loaded[hh], 16)

            def pair(pr, last):
                for hh in range(2):
                    for g in ORDER:
                        sp.wait_ge(o_read[g % 2], group_uses(pr, hh, g) + 1)
                        apart(sp, passed_sp)
                        rows, at = bass.ds((2 * pr + hh) * HD, HD), slice(g * QG * P, (g + 1) * QG * P)
                        sp.dma_start(oa_t[rows, at], o_sb[0:HD, g % 2, :]).then_inc(o_stored[g % 2], 16)
                        sp.dma_start(ob_t[rows, at], o_sb[HD:P, g % 2, :]).then_inc(o_stored[g % 2], 16)
                        if g == NGQ - 1 and not last:
                            sp.wait_ge(z_ready[1], per_z * (2 * pr + hh + 1))
                            load(pr + 1, hh)
                            sp.wait_ge(v_ready[hh], pr + 1)
                            apart(sp, passed_sp)
                            load_v(pr + 1, hh)

            load(0, 0, slice(SEQ - Z_W, SEQ), first_loaded)
            load(0, 0, slice(0, SEQ - Z_W))
            load_v(0, 0)
            load(0, 1)
            load_v(0, 1)
            with sp.Fori(0, NPAIR - 1) as pr:
                pair(pr, False)
            pair(NPAIR - 1, True)
            for s in range(2):
                sp.wait_ge(o_stored[s], 32 * H * NGQ // 2)

        @block.tensor
        def _(pe):
            def score(pr, hh, n):
                i, p0, p1 = PIECES[n]
                first = isinstance(pr, int) and pr == 0 and hh == 0
                if first and n == 0:
                    pe.wait_ge(first_loaded, 96)
                elif n == int(first):
                    pe.wait_ge(qk_loaded[hh], 96 * (pr + 1))
                s = n % 2
                pe.wait_ge(z_used[s], (2 * pr + hh) * per_z + n // 2)
                for r0 in range(p0, p1, 512):
                    r1 = min(r0 + 512, p1)
                    o = pz[:, s, r0 - p0:r1 - p0]
                    lhs = q2[hh][:, i * P:(i + 1) * P]
                    pe.matmul(o, lhs, kh2[hh][:, r0:r1], start=True, stop=False)
                    if r1 == (i + 1) * P:
                        pe.matmul(pz[:, s, r1 - P - p0:r1 - p0], identr[:, :], maskr[:, :],
                                  start=False, stop=False)
                    mm = pe.matmul(o, lhs, kl2[hh][:, r0:r1], start=False, stop=True)
                mm.then_inc(z_ready[s], 1)

            def multiply(pr, hh, b):
                g, kb = BLOCKS[b]
                c0, s = max(0, kb - QG * g) * P, b % 4
                if kb == 0:
                    if g == ORDER[0]:
                        pe.wait_ge(o_read[ORDER[-1] % 2], (2 * pr + hh) * (NGQ // 2))
                    else:
                        pe.wait_ge(o_read[(g + 1) % 2], group_uses(pr, hh, g + 1) + 1)
                pe.wait_ge(at_ready[s], (2 * pr + hh) * per_at + b // 4 + 1)
                o = po[:, c0:QG * P]
                last = kb == QG * (g + 1) - 1
                pe.matmul(o, v2[hh][:, kb, :, :], ath[s][:, c0:], start=(kb == 0), stop=False,
                          skip_group_check=True)
                pe.matmul(o, v2[hh][:, kb, :, :], atl[s][:, c0:], start=False, stop=last,
                          skip_group_check=True).then_inc(av_done[s], 1)

            def value(pr, hh, b):
                g, kb = BLOCKS[b]
                if b == 0:
                    pe.wait_ge(v_ready[hh], pr + 1)
                if kb == 0:
                    for i in (QG * g + 2, QG * g + 3):
                        pe.wait_ge(weighted[i % 2], (2 * pr + hh) * per_i + tile_uses(i))
                before = b - TS if b >= TS else max(range(b, N_BLOCK, TS)) - N_BLOCK
                pe.wait_ge(at_ready[before % 4], (2 * pr + hh) * per_at + before // 4 + 1)
                for i in range(max(kb, QG * g), QG * (g + 1)):
                    q = i - QG * g
                    mm = pe.transpose(pt[:, b % TS, q * P:(q + 1) * P], a[g][:, q, kb * P:(kb + 1) * P],
                                      ident[:, :])
                mm.then_inc(t_ready[b % TS], 1)
                if b >= TS:
                    multiply(pr, hh, b - TS)
                elif hh == 1:
                    multiply(pr, 0, N_BLOCK + b - TS)

            def tail(pr, hh, g):
                if (hh, g) == (1, 0):
                    for b in range(N_BLOCK - TS, N_BLOCK):
                        multiply(pr, hh, b)

            all_heads(pe, ON_PE, score, value, tail)

        @block.scalar
        def _(act):
            def score(pr, hh, n):
                i, p0, p1 = PIECES[n]
                s, g = n % 2, i // QG
                if p1 == (i + 1) * P:
                    if ("score", n, 1) in cycle(ON_ACT) and not (isinstance(pr, int) and pr == 0 and hh == 0):
                        act.wait_ge(av_done[3], (2 * pr + hh - 1) * per_at + group_end[g])
                    act.wait_ge(scanned[i % 2], (2 * pr + hh) * per_i + piece_uses(n))
                act.wait_ge(z_ready[s], (2 * pr + hh) * per_z + n // 2 + 1)
                act.activation(a[g][:, i % QG, p0:p1], pz[:, s, 0:p1 - p0], ACT.Sigmoid, scale=SCALE)
                act.activation(keep[:, i % 2, p0:p1], pz[:, s, 0:p1 - p0], ACT.Sigmoid,
                               scale=-SCALE).then_inc(z_used[s], 1)

            def value(pr, hh, b):
                g, kb = BLOCKS[b]
                c0, s = max(0, kb - QG * g) * P, b % 4
                act.wait_ge(t_ready[b % TS], turned_uses(pr, hh, b) + 1)
                act.wait_ge(av_done[s], (2 * pr + hh) * per_at + b // 4)
                act.activation(ath[s][:, c0:], pt[:, b % TS, c0:], ACT.Copy).then_inc(at_hi[s], 1)

            all_heads(act, ON_ACT, score, value)

        @block.vector
        def _(dve):
            def score(pr, hh, n):
                i, p0, p1 = PIECES[n]
                s, at = i % 2, SEQ - (i + 1) * P
                dve.wait_ge(z_used[n % 2], (2 * pr + hh) * per_z + n // 2 + 1)
                if p1 == (i + 1) * P:
                    dve.wait_ge(weighted[s], (2 * pr + hh) * per_i + piece_uses(n))
                    start = 1.0
                else:
                    dve.wait_ge(scanned[s], (2 * pr + hh) * per_i + piece_uses(n))
                    start = prod[:, s, at + p1:at + p1 + 1]
                back = keep[:, s, p0:p1][:, ::-1]
                dve.tensor_tensor_scan(prod[:, s, at + p0:at + p1][:, ::-1], back, back, start,
                                       ALU.mult, ALU.bypass).then_inc(scanned[s], 1)

            def value(pr, hh, b):
                g, kb = BLOCKS[b]
                c0, s = max(0, kb - QG * g) * P, b % 4
                dve.wait_ge(at_hi[s], (2 * pr + hh) * per_at + b // 4 + 1)
                dve.tensor_tensor(atl[s][:, c0:], pt[:, b % TS, c0:], ath[s][:, c0:].bitcast(F32),
                                  ALU.subtract).then_inc(at_ready[s], 1)

            def tail(pr, hh, g):
                dve.wait_ge(av_done[3], (2 * pr + hh) * per_at + group_end[g])
                dve.wait_ge(o_stored[g % 2], 32 * (group_uses(pr, hh, g)))
                dve.tensor_copy(o_sb[:, g % 2, :], po[:, :]).then_inc(o_read[g % 2], 1)

            dve.memset(prod[:, :, SEQ:SEQ + 1], 1.0).then_inc(one_set, 1)
            dve.wait_ge(one_set, 1)
            all_heads(dve, ON_DVE, score, value, tail)

        @block.gpsimd
        def _(pool):
            def score(pr, hh, n):
                i, p0, p1 = PIECES[n]
                s, at = i % 2, SEQ - (i + 1) * P
                piece = a[i // QG][:, i % QG, p0:p1]
                pool.wait_ge(scanned[s], (2 * pr + hh) * per_i + piece_uses(n) + 1)
                pool.tensor_tensor(piece, piece, prod[:, s, at + p0 + 1:at + p1 + 1], ALU.mult)\
                    .then_inc(weighted[s], 1)

            def split_v(pr, hh):
                pool.wait_ge(v_loaded[hh], 16 * (pr + 1))
                apart(pool, passed)
                pool.tensor_copy(v2[hh][:, :, 0, :], v_in[:, hh, :, :]).then_inc(v_hi[hh], 1)
                pool.wait_ge(v_hi[hh], pr + 1)
                pool.tensor_tensor(v2[hh][:, :, 1, :], v_in[:, hh, :, :], v2[hh][:, :, 0, :].bitcast(F32),
                                   ALU.subtract).then_inc(v_ready[hh], 1)

            def value(pr, hh, b):
                if b == N_BLOCK // 2:
                    if hh == 0:
                        pool.wait_ge(av_done[3], (2 * pr) * per_at)
                        split_v(pr, 1)
                    elif not (isinstance(pr, int) and pr == NPAIR - 1):
                        pool.wait_ge(av_done[3], (2 * pr + 1) * per_at)
                        split_v(pr + 1, 0)

            split_v(0, 0)
            pool.wait_ge(one_set, 1)
            all_heads(pool, ON_DVE, score, value)


def stream_order(eng, keys, values, score, weigh, finish):
    def steps(j, s, last, more):
        score(j, s)
        if last is not None:
            finish(*last)
        if more is not None:
            keys(*more)
        weigh(j, s)
        if more is not None:
            values(*more)

    keys(0, 0)
    values(0, 0)
    steps(0, 0, None, (0, 1))
    with eng.Fori(0, NB // 2 - 1) as j:
        steps(j, 1, (j, 0), (j + 1, 0))
        steps(j + 1, 0, (j, 1), (j + 1, 1))
    steps(NB // 2 - 1, 1, (NB // 2 - 1, 0), None)
    finish(NB // 2 - 1, 1)


def phase_attend_sample(nc, qh_t, ql_t, kh_t, kl_t, cache_k, cache_v, v_sample, ident, identr, mask_r,
                        oa_t, ob_t, w_out, raw, wh, wl):
    with ExitStack() as ctx:
        sb, pb, sem, sem2 = make_tools(nc, ctx)
        NK, KB = PAST + NQ, PAST // P
        HP = KT // 2
        W = HP * P
        PAD = P + 2 * NQ
        qh, ql, knh, knl = (sb(f"s_{n}", [P, KT, P]) for n in ("qh", "ql", "knh", "knl"))
        pad_h = [sb(f"s_pad_h{s}", [P, 2, HP * PAD], F32R) for s in range(2)]
        pad_l = [sb(f"s_pad_l{s}", [P, 2, HP * PAD], F32R) for s in range(2)]
        k_in = [sb(f"s_k_in{s}", [P, KB, D]) for s in range(2)]
        v_in = sb("s_v_in", [P, KB, D])
        vn_in = sb("s_vn_in", [NQ, D])
        kth = [sb(f"s_kth{s}", [P, KT, NK], F32R) for s in range(2)]
        ktl = [sb(f"s_ktl{s}", [P, KT, NK], F32R) for s in range(2)]
        vh = sb("s_vh", [P, KB, D], F32R)
        vl = sb("s_vl", [P, KB, D], F32R)
        vnh = sb("s_vnh", [NQ, D], F32R)
        vnl = sb("s_vnl", [NQ, D], F32R)
        a = sb("s_a", [P, 2, NK])
        keep = sb("s_keep", [P, 2, NK])
        prod = sb("s_prod", [P, 2, NK + 1])
        ath = [sb(f"s_ath{f}", [P, KB + 1, P], F32R) for f in range(2)]
        atl = [sb(f"s_atl{f}", [P, KB + 1, P], F32R) for f in range(2)]
        own = sb("s_own", [P, 2, P])
        o_t = sb("s_o_t", [P, KT, P])
        none = sb("s_none", [P, P])
        pz = pb("s_pz", [P, 2, 512])
        pk = pb("s_pk", [P, 2, 4, P])
        pa = pb("s_pa", [P, 2, 4, P])
        po = pb("s_po", [P, 2, W])
        loaded, cleared = sem("s_loaded"), sem("s_cleared")
        k_loaded, v_loaded = sem2("s_k_loaded"), sem("s_v_loaded")
        w_loaded, w_hi, w_lo = sem2("s_w_loaded"), sem("s_w_hi"), sem("s_w_lo")
        small, ahead = sem("s_small"), sem("s_ahead")
        k_turned, k_hi, k_lo = sem2("s_k_turned"), sem2("s_k_hi"), sem2("s_k_lo")
        v_hi, v_lo = sem("s_v_hi"), sem("s_v_lo")
        vn_hi, vn_lo = sem("s_vn_hi"), sem("s_vn_lo")
        z_ready, z_used = sem2("s_z_ready"), sem2("s_z_used")
        scanned, weighted = sem2("s_scanned"), sem2("s_weighted")
        a_turned, at_hi, at_lo, av_done = sem2("s_a_turned"), sem2("s_at_hi"), sem2("s_at_lo"), sem2("s_av_done")
        picked, o_turned, o_read = sem2("s_picked"), sem2("s_o_turned"), sem2("s_o_read")
        o_stored = sem("s_o_stored")
        block = ctx.enter_context(nc.Block())
        assert NB == KT
        NROUND = KB * KT // 4
        RS = NROUND // 2
        new = slice(SEQ, T)
        feature_major = lambda ap: ap[:, new].rearrange("(kt p) t -> p kt t", p=P)

        @block.sync
        def _(sp):
            def fetch(j, s, between=nothing):
                b = 2 * j + s
                for r in range(2):
                    wait_past(sp, k_turned[r], RS * (b - 1))
                for kb in range(KB):
                    sp.dma_start(k_in[s][:, kb, :], cache_k[b, kb * P:(kb + 1) * P, :]).then_inc(k_loaded[s], 16)
                between()
                wait_past(sp, v_lo, 2 * b)
                wait_past(sp, vn_lo, 2 * b)
                for kb in range(KB):
                    sp.dma_start(v_in[:, kb, :], cache_v[b, kb * P:(kb + 1) * P, :]).then_inc(v_loaded, 16)
                sp.dma_start(vn_in[:, :], v_sample[bass.ds(b * NQ, NQ), :]).then_inc(v_loaded, 16)
                wait_past(sp, w_lo, b - 1)
                sp.dma_start(raw[:, b, :], w_out[bass.ds(b * P, P), :]).then_inc(w_loaded[s], 16)

            def fetch_new():
                for dst, src in ((qh, qh_t), (ql, ql_t), (knh, kh_t), (knl, kl_t)):
                    sp.dma_start(dst[:, :, :], feature_major(src)).then_inc(loaded, 16)

            fetch(0, 0, fetch_new)
            fetch(0, 1)
            with sp.Fori(1, NB // 2) as j:
                fetch(j, 0)
                fetch(j, 1)
            sp.wait_ge(cleared, 6)
            for kt in range(KT):
                sp.dma_start(ob_t[kt * P:(kt + 1) * P, new], none[:, :]).then_inc(o_stored, 16)
            for f in range(2):
                sp.wait_ge(o_read[f], 2 * NB)
            sp.dma_start(feature_major(oa_t), o_t[:, :, :]).then_inc(o_stored, 16)
            sp.wait_ge(o_stored, 16 * (KT + 1))

        @block.gpsimd
        def _(pool):
            def keys(j, s):
                b = 2 * j + s
                at = bass.ds(b * NQ, NQ)
                wait_past(pool, z_ready[1], b - 1)
                wait_past(pool, w_lo, b)
                apart(pool, ahead)
                for top in range(2):
                    rows = slice(top * HD, (top + 1) * HD)
                    for pad, q in ((pad_h[s], qh), (pad_l[s], ql)):
                        pool.tensor_copy(pad[rows, :, :].rearrange("p f (i r) -> p f i r", r=PAD)
                                         [:, :, :, top * NQ:(top + 1) * NQ],
                                         q[rows, :, at].rearrange("p (f i) t -> p f i t", f=2))\
                            .then_inc(small, 1)
                    pool.wait_ge(small, 6 * b + 2 * (top + 1))
                    apart(pool, ahead)
                for dst, src in ((kth[s], knh), (ktl[s], knl)):
                    pool.tensor_copy(dst[:, :, PAST:NK], src[:, :, at]).then_inc(small, 1)

            def values(j, s):
                b = 2 * j + s
                pool.wait_ge(small, 6 * (b + 1))
                for f in range(2):
                    cols = slice(f * W, (f + 1) * W)
                    pool.wait_ge(vn_hi, 2 * b + f + 1)
                    pool.tensor_tensor(vnl[:, cols], vn_in[:, cols], vnh[:, cols].bitcast(F32), ALU.subtract)\
                        .then_inc(vn_lo, 1)
                pool.wait_ge(vn_lo, 2 * (b + 1))
                pool.wait_ge(w_hi, b + 1)
                apart(pool, ahead)
                pool.tensor_tensor(wl[:, b, :], raw[:, b, :], wh[:, b, :].bitcast(F32), ALU.subtract)\
                    .then_inc(w_lo, 1)

            for s in range(2):
                for pad in (pad_h[s], pad_l[s]):
                    pool.memset(pad[:, :, :].bitcast(F32), 0.0).then_inc(cleared, 1)
            pool.memset(none[:, :], 0.0).then_inc(cleared, 1)
            pool.memset(prod[:, :, NK:NK + 1], 1.0).then_inc(cleared, 1)
            pool.wait_ge(cleared, 6)
            pool.wait_ge(loaded, 64)
            stream_order(pool, keys, values, nothing, nothing, nothing)
            pool.wait_ge(w_lo, NB)

        @block.tensor
        def _(pe):
            def keys(j, s):
                b = 2 * j + s
                pe.wait_ge(k_loaded[s], 16 * KB * (j + 1))
                for r in range(NROUND):
                    slot, kb, i0 = r % 2, r // 2, 4 * (r % 2)
                    wait_past(pe, k_lo[slot], RS * b + r // 2)
                    for i in range(4):
                        at = slice((i0 + i) * P, (i0 + i + 1) * P)
                        mm = pe.transpose(pk[:, slot, i, :], k_in[s][:, kb, at], ident[:, :])
                    mm.then_inc(k_turned[slot], 1)

            def score(j, s):
                b = 2 * j + s
                pe.wait_ge(small, 6 * (b + 1))
                for r in range(2):
                    pe.wait_ge(k_lo[r], RS * (b + 1))
                for f in range(2):
                    wait_past(pe, z_used[f], b)
                    for i in range(HP):
                        hi, lo = (pad[s][:, f, i * P:(i + 1) * P] for pad in (pad_h, pad_l))
                        kh, kl = (kt[s][:, HP * f + i, :] for kt in (kth, ktl))
                        o = pz[:, f, 0:NK]
                        pe.matmul(o, hi, kh, start=(i == 0), stop=False)
                        pe.matmul(o, hi, kl, start=False, stop=False)
                        pe.matmul(o, lo, kh, start=False, stop=False)
                    pe.matmul(pz[:, f, PAST:NK], identr[:, :], mask_r[:, :], start=False, stop=True)\
                        .then_inc(z_ready[f], 1)

            def weigh(j, s):
                b = 2 * j + s
                for f in range(2):
                    pe.wait_ge(weighted[f], b + 1)
                    wait_past(pe, o_read[f], 2 * b)
                    for kb in range(KB):
                        pe.transpose(pa[:, f, kb, :], a[:, f, kb * P:(kb + 1) * P], ident[:, :])
                    pe.transpose(pa[0:NQ, f, KB, :], a[:, f, PAST:NK], ident[:, :]).then_inc(a_turned[f], 1)
                for f in range(2):
                    pe.wait_ge(v_lo, 2 * b + f + 1)
                    pe.wait_ge(vn_lo, 2 * b + f + 1)
                    pe.wait_ge(at_lo[f], 2 * (b + 1))
                    wait_past(pe, picked[f], HP * b)
                    cols = slice(f * W, (f + 1) * W)
                    for kb in range(KB + 1):
                        rows = slice(0, P if kb < KB else NQ)
                        hi, lo = (at[f][rows, kb, :] for at in (ath, atl))
                        val_h = vh[:, kb, cols] if kb < KB else vnh[:, cols]
                        val_l = vl[:, kb, cols] if kb < KB else vnl[:, cols]
                        pe.matmul(po[:, f, :], hi, val_h, start=(kb == 0), stop=False)
                        pe.matmul(po[:, f, :], hi, val_l, start=False, stop=False)
                        mm = pe.matmul(po[:, f, :], lo, val_h, start=False, stop=(kb == KB))
                    mm.then_inc(av_done[f], 1)

            def finish(j, s):
                b = 2 * j + s
                for f in range(2):
                    pe.wait_ge(picked[f], HP * (b + 1))
                    pe.transpose(pa[:, f, 0, :], own[:, f, :], ident[:, :]).then_inc(o_turned[f], 1)

            stream_order(pe, keys, nothing, score, weigh, finish)

        @block.scalar
        def _(act):
            def keys(j, s):
                b = 2 * j + s
                wait_past(act, z_ready[1], b - 1)
                for r in range(NROUND):
                    slot, kb, i0 = r % 2, r // 2, 4 * (r % 2)
                    act.wait_ge(k_turned[slot], RS * b + r // 2 + 1)
                    act.activation(kth[s][:, i0:i0 + 4, kb * P:(kb + 1) * P], pk[:, slot, :, :],
                                   ACT.Copy).then_inc(k_hi[slot], 1)

            def values(j, s):
                b = 2 * j + s
                first = isinstance(b, int) and b == 0
                if not first:
                    act.wait_ge(w_loaded[s], 16 * (j + 1))
                    act.activation(wh[:, b, :], raw[:, b, :], ACT.Copy).then_inc(w_hi, 1)
                act.wait_ge(v_loaded, 16 * (KB + 1) * (b + 1))
                for f in range(2):
                    cols = slice(f * W, (f + 1) * W)
                    wait_past(act, av_done[f], b)
                    act.activation(vh[:, :, cols], v_in[:, :, cols], ACT.Copy).then_inc(v_hi, 1)
                    act.activation(vnh[:, cols], vn_in[:, cols], ACT.Copy).then_inc(vn_hi, 1)
                if first:
                    act.wait_ge(w_loaded[s], 16)
                    act.activation(wh[:, b, :], raw[:, b, :], ACT.Copy).then_inc(w_hi, 1)

            def score(j, s):
                b = 2 * j + s
                for f in range(2):
                    act.wait_ge(z_ready[f], b + 1)
                    wait_past(act, a_turned[f], b)
                    act.activation(a[:, f, :], pz[:, f, 0:NK], ACT.Sigmoid, scale=SCALE)
                    wait_past(act, scanned[f], b)
                    act.activation(keep[:, f, :], pz[:, f, 0:NK], ACT.Sigmoid, scale=-SCALE)\
                       .then_inc(z_used[f], 1)

            def weigh(j, s):
                b = 2 * j + s
                for f in range(2):
                    act.wait_ge(a_turned[f], b + 1)
                    wait_past(act, av_done[f], b)
                    act.activation(ath[f][:, 0:KB, :], pa[:, f, 0:KB, :], ACT.Copy).then_inc(at_hi[f], 1)
                    act.activation(ath[f][0:NQ, KB, :], pa[0:NQ, f, KB, :], ACT.Copy).then_inc(at_hi[f], 1)

            def finish(j, s):
                b = 2 * j + s
                for f in range(2):
                    act.wait_ge(o_turned[f], b + 1)
                    for top in range(2):
                        rows = slice(top * HD, (top + 1) * HD)
                        mine = pa[rows, f, 0, :].rearrange("p (i g q) -> p i g q", g=2, q=NQ)[:, :, top, :]
                        act.activation(o_t[rows, HP * f:HP * (f + 1), bass.ds(b * NQ, NQ)], mine,
                                       ACT.Copy).then_inc(o_read[f], 1)

            stream_order(act, keys, values, score, weigh, finish)

        @block.vector
        def _(dve):
            def keys(j, s):
                b = 2 * j + s
                for r in range(NROUND):
                    slot, kb, i0 = r % 2, r // 2, 4 * (r % 2)
                    at = slice(kb * P, (kb + 1) * P)
                    dve.wait_ge(k_hi[slot], RS * b + r // 2 + 1)
                    dve.tensor_tensor(ktl[s][:, i0:i0 + 4, at], pk[:, slot, :, :],
                                      kth[s][:, i0:i0 + 4, at].bitcast(F32), ALU.subtract)\
                       .then_inc(k_lo[slot], 1)

            def values(j, s):
                b = 2 * j + s
                for f in range(2):
                    cols = slice(f * W, (f + 1) * W)
                    dve.wait_ge(v_hi, 2 * b + f + 1)
                    dve.tensor_tensor(vl[:, :, cols], v_in[:, :, cols], vh[:, :, cols].bitcast(F32),
                                      ALU.subtract).then_inc(v_lo, 1)

            def score(j, s):
                b = 2 * j + s
                for f in range(2):
                    dve.wait_ge(z_used[f], b + 1)
                    wait_past(dve, weighted[f], b)
                    dve.tensor_tensor_scan(prod[:, f, 0:NK][:, ::-1], keep[:, f, :][:, ::-1],
                                           keep[:, f, :][:, ::-1], 1.0, ALU.mult, ALU.bypass)\
                       .then_inc(scanned[f], 1)
                    dve.wait_ge(scanned[f], b + 1)
                    dve.tensor_tensor(a[:, f, :], a[:, f, :], prod[:, f, 1:NK + 1], ALU.mult)\
                       .then_inc(weighted[f], 1)

            def weigh(j, s):
                b = 2 * j + s
                for f in range(2):
                    dve.wait_ge(at_hi[f], 2 * (b + 1))
                    dve.tensor_tensor(atl[f][:, 0:KB, :], pa[:, f, 0:KB, :], ath[f][:, 0:KB, :].bitcast(F32),
                                      ALU.subtract).then_inc(at_lo[f], 1)
                    dve.tensor_tensor(atl[f][0:NQ, KB, :], pa[0:NQ, f, KB, :],
                                      ath[f][0:NQ, KB, :].bitcast(F32), ALU.subtract).then_inc(at_lo[f], 1)
                for f in range(2):
                    dve.wait_ge(av_done[f], b + 1)
                    wait_past(dve, o_turned[f], b)
                    for i in range(HP):
                        rows = slice(2 * NQ * i, 2 * NQ * (i + 1))
                        dve.tensor_copy(own[rows, f, :], po[rows, f, i * P:(i + 1) * P]).then_inc(picked[f], 1)

            dve.wait_ge(cleared, 6)
            stream_order(dve, keys, values, score, weigh, nothing)


def build(nc, x_prompt, x_sample, state_conv, cache_k, cache_v, a_norm_pre, a_w_in, a_conv_w, a_w_out,
          a_norm_post, kv_norm, w_k, w_v, b_norm_pre, b_w_in, b_w_out, b_norm_post, ident_in, mask_in,
          mask_s_in, y_prompt, y_sample, conv_p, conv_s, k_prompt, v_prompt, k_sample, v_sample):
    flat = lambda ap: ap.rearrange("b t d -> (b t) d")
    heads = lambda ap: ap.rearrange("b t h d -> (b t) (h d)")
    xp, xsm, yp, ysm = flat(x_prompt), flat(x_sample), flat(y_prompt), flat(y_sample)
    kp, vp, ks, vs = heads(k_prompt), heads(v_prompt), heads(k_sample), heads(v_sample)

    def scratch(name, shape):
        return nc.dram_tensor(name, shape, F32, kind="Internal").ap()

    y_t, qh_t, ql_t, kh_t, kl_t, sz_t, oa_t, ob_t = (
        scratch(n, [D, T]) for n in ("y_t", "qh_t", "ql_t", "kh_t", "kl_t", "sz_t", "oa_t", "ob_t"))
    x1 = scratch("x1", [T, D])

    with ExitStack() as ctx:
        sb, pb, sem, sem2 = make_tools(nc, ctx)
        ident = sb("ident", [P, P])
        mask = sb("mask", [P, P])
        mask_s = sb("mask_s", [P, NQ])
        identr = sb("identr", [P, P], F32R)
        maskr = sb("maskr", [P, P], F32R)
        mask_sr = sb("mask_sr", [P, NQ], F32R)
        loaded, rounded = sem("k_loaded"), sem("k_rounded")
        with nc.Block() as block:
            @block.sync
            def _(sp):
                for dst, src in ((ident, ident_in), (mask, mask_in), (mask_s, mask_s_in)):
                    sp.dma_start(dst[:, :], src).then_inc(loaded, 16)

            @block.vector
            def _(dve):
                dve.wait_ge(loaded, 48)
                for dst, src in ((identr, ident), (maskr, mask), (mask_sr, mask_s)):
                    dve.tensor_copy(dst[:, :], src[:, :]).then_inc(rounded, 1)
                dve.wait_ge(rounded, 3)

        with ExitStack() as act_ctx:
            slab_at = (nc.sbuf_base + 31) // 32 * 32
            act_ctx.enter_context(nc.sbuf_tensor("slab", [P, KT * T], F32))
            at_slab = lambda name, dt: nc.alloc_sbuf_tensor_at(name, [P, KT, T], dt, offset=slab_at)
            with ExitStack() as conv_ctx:
                new = lambda name, shape, dt=F32: conv_ctx.enter_context(nc.sbuf_tensor(name, shape, dt))
                xh = new("a_xh", [P, KT, T], F32R)
                st_rows, cw_all = new("st_rows", [NB * 2, D]), new("cw_all", [P, KT, CW])
                xl = at_slab("a_xl", F32R)
                room = stream_room(nc, conv_ctx, "c_", 1)
                order = conv_order(a_w_in[0], room)
                consts = [(st_rows[:, :], state_conv[0].rearrange("b w d -> (b w) d"))]
                consts += [(cw_all[:, :, w], a_conv_w[0, w].rearrange("(c p) -> p c", p=P)) for w in range(CW)]
                pg = [conv_ctx.enter_context(nc.psum_tensor(f"c_pg{g}", [P, 512], F32)) for g in range(NG)]
                phase_norm_in(nc, xp, xsm, ident, xh, xl, consts,
                              lambda pool, sem, split: begin_stream(pool, room, order, [a_norm_pre[0]], sem,
                                                                    "n_next_", split), room, pg)
                phase_conv(nc, order, room, pg, st_rows, cw_all, ident, xh, xl, y_t, conv_p[0, 0],
                           conv_s[0].rearrange("b w d -> (b w) d"))
            with ExitStack() as qkvz_ctx:
                x32 = at_slab("b_x32", F32)
                q_room = stream_room(nc, qkvz_ctx, "q_", 2)
                q_order = qkvz_order(w_k, w_v, b_w_in[0], q_room)
                phase_out(nc, "f_", [y_t], a_w_out[0], a_norm_post[0], xp, xsm, ident, x1[0:SEQ, :], x1[SEQ:T, :],
                          x32, begin_next=lambda pool, sem: begin_stream(
                              pool, q_room, q_order, [kv_norm, b_norm_pre[0]], sem, "f_next_",
                              sem("f_next_split")))
                phase_qkvz(nc, q_order, q_room, ident, x32, at_slab("b_xl", F32R), qh_t, ql_t, kh_t, kl_t, sz_t,
                           kp, vp, ks, vs)
        phase_attend(nc, qh_t, ql_t, kh_t, kl_t, vp, ident, identr, maskr, oa_t, ob_t)
        with ExitStack() as w_ctx:
            weights = out_weights(nc, w_ctx, "g_")
            phase_attend_sample(nc, qh_t, ql_t, kh_t, kl_t, cache_k.rearrange("b t h d -> b t (h d)"),
                                cache_v.rearrange("b t h d -> b t (h d)"), vs, ident, identr, mask_sr,
                                oa_t, ob_t, b_w_out[0], *weights)
            phase_out(nc, "g_", [oa_t, ob_t, sz_t], b_w_out[0], b_norm_post[0], x1[0:SEQ, :], x1[SEQ:T, :],
                      ident, yp, ysm, None, weights)


_INS = ["x_prompt", "x_sample", "state_conv", "cache_k", "cache_v", "a_norm_pre", "a_w_in", "a_conv_w",
        "a_w_out", "a_norm_post", "kv_norm", "w_k", "w_v", "b_norm_pre", "b_w_in", "b_w_out", "b_norm_post"]
_OUTS = [(1, SEQ, D), (NB, NQ, D), (1, 1, 2, D), (1, NB, 2, D), (1, SEQ, H, HD), (1, SEQ, H, HD),
         (NB, NQ, H, HD), (NB, NQ, H, HD)]


def kernel(**inputs):
    import concourse.bacc as bacc
    from concourse.bass_utils import run_bass_kernel_spmd

    nc = bacc.Bacc("TRN2", target_bir_lowering=False, num_devices=1)
    arrays = {name: np.ascontiguousarray(inputs[name]) for name in _INS}
    arrays["ident"] = np.eye(P, dtype=np.float32)
    arrays["mask"] = np.where(np.arange(P)[None, :] >= np.arange(P)[:, None], MASKED, 0.0).astype(np.float32)
    arrays["mask_s"] = np.where(np.arange(NQ)[None, :] >= np.arange(P)[:, None] % NQ, MASKED, 0.0)\
        .astype(np.float32)
    args = [nc.dram_tensor("in_" + n, a.shape, F32, kind="ExternalInput").ap() for n, a in arrays.items()]
    args += [nc.dram_tensor(f"out_{i}", s, F32, kind="ExternalOutput").ap() for i, s in enumerate(_OUTS)]
    build(nc, *args)
    r = run_bass_kernel_spmd(nc, [{"in_" + n: a for n, a in arrays.items()}], core_ids=[0])
    return tuple(r.results[0][f"out_{i}"] for i in range(len(_OUTS)))
```
